# Optimizing a Trainium2 kernel written in Bass

```python
import math
import jax, jax.numpy as jnp
from jax import lax
import numpy as np

D_MODEL = 1024
BATCH = 1
SEQ = 512
DEPTH = 2

CHUNK = 64
N_META = 16
EPS = 1e-6
NEG_INF = -1e30
FFN_RESIDUAL = 0.5
D_FF = 2816
D_CONV = 512
CONV_WIDTH = 3
D_SSM = 512
SSM_GROUP = 16
SSM_GROUPS = D_SSM // SSM_GROUP
SSM_STATE = 64
DT_MIN = 0.001
DT_MAX = 0.1
D_IN_EVEN = 3 * D_CONV + D_SSM
D_MIX_EVEN = D_CONV + D_SSM
N_HEADS = 16
N_KV_HEADS = 4
Q_PER_KV = N_HEADS // N_KV_HEADS
HEAD_DIM = 64
D_QKV = (N_HEADS + 2 * N_KV_HEADS) * HEAD_DIM
WINDOW = 128
WINDOW_CHUNKS = WINDOW // CHUNK
N_EVEN = (DEPTH + 1) // 2
N_ODD = DEPTH // 2

kernel_name = 'hybrid_conv_s5_swa_macaron_trunk'

def rmsnorm(x, gain):
    xf = x.astype(jnp.float32)
    y = xf * lax.rsqrt(jnp.mean(xf * xf, axis=-1, keepdims=True) + EPS)
    return (y * gain.astype(jnp.float32)).astype(x.dtype)

def swiglu(x, w_gate, w_up, w_down):
    return (jax.nn.silu(x @ w_gate) * (x @ w_up)) @ w_down

def short_gated_conv(xa, b_gate, c_gate, conv_w):
    hc = c_gate * xa
    y = lax.conv_general_dilated(
        hc, conv_w[:, None, :].astype(hc.dtype), window_strides=(1,),
        padding=[(CONV_WIDTH - 1, 0)], dimension_numbers=('NWC', 'WIO', 'NWC'),
        feature_group_count=D_CONV)
    return b_gate * y

def s5_ssm(u, lam_re, lam_im, log_step, b_re, b_im, c_re, c_im, d_skip, glu_w, glu_b):
    f32 = jnp.float32
    bsz, length, _ = u.shape
    uf = u.astype(f32).reshape(bsz, length, SSM_GROUPS, SSM_GROUP)
    lam = lax.complex(lam_re.astype(f32), lam_im.astype(f32))
    step = jnp.exp(log_step.astype(f32))[:, None]
    lam_bar = jnp.exp(lam * step)
    b_mat = lax.complex(b_re.astype(f32), b_im.astype(f32))
    b_bar = ((lam_bar - 1.0) / lam)[..., None] * b_mat
    bu = jnp.einsum('gph,blgh->blgp', b_bar, uf.astype(jnp.complex64))
    a = jnp.broadcast_to(lam_bar[None, None], (1, length, SSM_GROUPS, SSM_STATE))

    def combine(e1, e2):
        a1, s1 = e1
        a2, s2 = e2
        return a1 * a2, a2 * s1 + s2

    _, states = lax.associative_scan(combine, (a, bu), axis=1)
    c_mat = lax.complex(c_re.astype(f32), c_im.astype(f32))
    y = jnp.real(jnp.einsum('ghp,blgp->blgh', c_mat, states))
    y = y + d_skip.astype(f32).reshape(SSM_GROUPS, SSM_GROUP) * uf
    y = jax.nn.gelu(y.reshape(bsz, length, D_SSM))
    y = y * jax.nn.sigmoid(y @ glu_w.astype(f32) + glu_b.astype(f32))
    return y.astype(u.dtype)

def conv_ssm_mixer(hn, w_in, conv_w, lam_re, lam_im, log_step, b_re, b_im,
                   c_re, c_im, d_skip, glu_w, glu_b, w_out):
    z = hn @ w_in
    xa, b_gate, c_gate, u = jnp.split(z, [D_CONV, 2 * D_CONV, 3 * D_CONV], axis=-1)
    ya = short_gated_conv(xa, b_gate, c_gate, conv_w)
    yb = s5_ssm(u, lam_re, lam_im, log_step, b_re, b_im, c_re, c_im, d_skip, glu_w, glu_b)
    return jnp.concatenate([ya, yb], axis=-1) @ w_out

def alibi_slopes(n_heads):
    return jnp.exp2(-8.0 * jnp.arange(1, n_heads + 1, dtype=jnp.float32) / n_heads)

def softmax_with_sink(logits, sink):
    sink_col = jnp.broadcast_to(sink, logits.shape[:-1] + (1,))
    probs = jax.nn.softmax(jnp.concatenate([logits, sink_col], axis=-1), axis=-1)
    return probs[..., :-1]

def window_attention(hn, w_qkv, q_gain, k_gain, sinks, w_o, real_queries_only):
    f32 = jnp.float32
    bsz, length, _ = hn.shape
    n_real = length - N_META
    n_chunks = n_real // CHUNK
    qkv = hn @ w_qkv
    q, k, v = jnp.split(qkv, [N_HEADS * HEAD_DIM, (N_HEADS + N_KV_HEADS) * HEAD_DIM], axis=-1)
    q = rmsnorm(q.reshape(bsz, length, N_KV_HEADS, Q_PER_KV, HEAD_DIM), q_gain).astype(f32)
    q = q * (HEAD_DIM ** -0.5)
    k = rmsnorm(k.reshape(bsz, length, N_KV_HEADS, HEAD_DIM), k_gain).astype(f32)
    v = v.reshape(bsz, length, N_KV_HEADS, HEAD_DIM).astype(f32)
    slopes = alibi_slopes(N_HEADS).reshape(N_KV_HEADS, Q_PER_KV)
    sink = sinks.astype(f32).reshape(N_KV_HEADS, Q_PER_KV)

    km, vm = k[:, :N_META], v[:, :N_META]
    qr = q[:, N_META:].reshape(bsz, n_chunks, CHUNK, N_KV_HEADS, Q_PER_KV, HEAD_DIM)
    kr = k[:, N_META:].reshape(bsz, n_chunks, CHUNK, N_KV_HEADS, HEAD_DIM)
    vr = v[:, N_META:].reshape(bsz, n_chunks, CHUNK, N_KV_HEADS, HEAD_DIM)

    def band(t):
        padded = jnp.pad(t, ((0, 0), (WINDOW_CHUNKS - 1, 0), (0, 0), (0, 0), (0, 0)))
        return jnp.concatenate([padded[:, o:o + n_chunks] for o in range(WINDOW_CHUNKS)], axis=2)

    kb, vb = band(kr), band(vr)
    q_idx = jnp.arange(CHUNK)
    j_idx = jnp.arange(WINDOW_CHUNKS * CHUNK)
    dist = jnp.abs(q_idx[:, None] + (WINDOW_CHUNKS - 1) * CHUNK - j_idx[None, :]).astype(f32)
    key_chunk = jnp.arange(n_chunks)[:, None] + j_idx[None, :] // CHUNK - (WINDOW_CHUNKS - 1)
    valid = (key_chunk >= 0)[:, None, :]

    s_band = jnp.einsum('bnqhgd,bnshd->bhgnqs', qr, kb)
    s_band = s_band - slopes[:, :, None, None, None] * dist
    s_band = jnp.where(valid, s_band, NEG_INF)
    s_meta = jnp.einsum('bnqhgd,bmhd->bhgnqm', qr, km)
    probs = softmax_with_sink(jnp.concatenate([s_meta, s_band], axis=-1),
                              sink[None, :, :, None, None, None])
    o_real = (jnp.einsum('bhgnqm,bmhd->bnqhgd', probs[..., :N_META], vm)
              + jnp.einsum('bhgnqs,bnshd->bnqhgd', probs[..., N_META:], vb))
    out = o_real.reshape(bsz, n_real, N_HEADS * HEAD_DIM)
    if not real_queries_only:
        qm = q[:, :N_META]
        s_mm = jnp.einsum('bqhgd,bmhd->bhgqm', qm, km)
        p_mm = softmax_with_sink(s_mm, sink[None, :, :, None, None])
        o_meta = jnp.einsum('bhgqm,bmhd->bqhgd', p_mm, vm).reshape(bsz, N_META, N_HEADS * HEAD_DIM)
        out = jnp.concatenate([o_meta, out], axis=1)
    return out.astype(hn.dtype) @ w_o

def setup_inputs(seed: int = 0):
    key = jax.random.key(seed)
    keys = jax.random.split(key, 32)
    counter = [0]

    def next_key():
        k = keys[counter[0]]
        counter[0] += 1
        return k

    def normal(shape, scale):
        return jax.random.normal(next_key(), shape, jnp.float32) * scale

    def gain(shape):
        return 1.0 + normal(shape, 0.02)

    n_idx = jnp.arange(SSM_STATE, dtype=jnp.float32)
    x = normal((BATCH, SEQ, D_MODEL), 1.0)
    meta_tokens = normal((N_META, D_MODEL), 1.0)
    norm_ff1 = gain((DEPTH, D_MODEL))
    ff1_w_gate = normal((DEPTH, D_MODEL, D_FF), D_MODEL ** -0.5)
    ff1_w_up = normal((DEPTH, D_MODEL, D_FF), D_MODEL ** -0.5)
    ff1_w_down = normal((DEPTH, D_FF, D_MODEL), D_FF ** -0.5)
    norm_mix = gain((DEPTH, D_MODEL))
    even_w_in = normal((N_EVEN, D_MODEL, D_IN_EVEN), D_MODEL ** -0.5)
    conv_w = normal((N_EVEN, CONV_WIDTH, D_CONV), CONV_WIDTH ** -0.5)
    ssm_lambda_re = -0.5 + normal((N_EVEN, SSM_GROUPS, SSM_STATE), 0.01)
    ssm_lambda_im = jnp.pi * n_idx + normal((N_EVEN, SSM_GROUPS, SSM_STATE), 0.01)
    ssm_log_step = jax.random.uniform(next_key(), (N_EVEN, SSM_GROUPS), jnp.float32,
                                      minval=math.log(DT_MIN), maxval=math.log(DT_MAX))
    ssm_b_re = normal((N_EVEN, SSM_GROUPS, SSM_STATE, SSM_GROUP), (2 * SSM_GROUP) ** -0.5)
    ssm_b_im = normal((N_EVEN, SSM_GROUPS, SSM_STATE, SSM_GROUP), (2 * SSM_GROUP) ** -0.5)
    ssm_c_re = normal((N_EVEN, SSM_GROUPS, SSM_GROUP, SSM_STATE), SSM_STATE ** -0.5)
    ssm_c_im = normal((N_EVEN, SSM_GROUPS, SSM_GROUP, SSM_STATE), SSM_STATE ** -0.5)
    ssm_d = normal((N_EVEN, D_SSM), 1.0)
    glu_w = normal((N_EVEN, D_SSM, D_SSM), D_SSM ** -0.5)
    glu_b = normal((N_EVEN, D_SSM), 0.01)
    even_w_out = normal((N_EVEN, D_MIX_EVEN, D_MODEL), D_MIX_EVEN ** -0.5)
    attn_w_qkv = normal((N_ODD, D_MODEL, D_QKV), D_MODEL ** -0.5)
    attn_q_norm = gain((N_ODD, HEAD_DIM))
    attn_k_norm = gain((N_ODD, HEAD_DIM))
    attn_sinks = normal((N_ODD, N_HEADS), 0.5)
    attn_w_o = normal((N_ODD, N_HEADS * HEAD_DIM, D_MODEL), (N_HEADS * HEAD_DIM) ** -0.5)
    norm_ff2 = gain((DEPTH, D_MODEL))
    ff2_w_gate = normal((DEPTH, D_MODEL, D_FF), D_MODEL ** -0.5)
    ff2_w_up = normal((DEPTH, D_MODEL, D_FF), D_MODEL ** -0.5)
    ff2_w_down = normal((DEPTH, D_FF, D_MODEL), D_FF ** -0.5)
    return {'x': x, 'meta_tokens': meta_tokens, 'norm_ff1': norm_ff1,
            'ff1_w_gate': ff1_w_gate, 'ff1_w_up': ff1_w_up, 'ff1_w_down': ff1_w_down,
            'norm_mix': norm_mix, 'even_w_in': even_w_in, 'conv_w': conv_w,
            'ssm_lambda_re': ssm_lambda_re, 'ssm_lambda_im': ssm_lambda_im,
            'ssm_log_step': ssm_log_step, 'ssm_b_re': ssm_b_re, 'ssm_b_im': ssm_b_im,
            'ssm_c_re': ssm_c_re, 'ssm_c_im': ssm_c_im, 'ssm_d': ssm_d,
            'glu_w': glu_w, 'glu_b': glu_b, 'even_w_out': even_w_out,
            'attn_w_qkv': attn_w_qkv, 'attn_q_norm': attn_q_norm, 'attn_k_norm': attn_k_norm,
            'attn_sinks': attn_sinks, 'attn_w_o': attn_w_o, 'norm_ff2': norm_ff2,
            'ff2_w_gate': ff2_w_gate, 'ff2_w_up': ff2_w_up, 'ff2_w_down': ff2_w_down}

def reference(x, meta_tokens, norm_ff1, ff1_w_gate, ff1_w_up, ff1_w_down, norm_mix,
              even_w_in, conv_w, ssm_lambda_re, ssm_lambda_im, ssm_log_step,
              ssm_b_re, ssm_b_im, ssm_c_re, ssm_c_im, ssm_d, glu_w, glu_b, even_w_out,
              attn_w_qkv, attn_q_norm, attn_k_norm, attn_sinks, attn_w_o,
              norm_ff2, ff2_w_gate, ff2_w_up, ff2_w_down):
    bsz, _, d_model = x.shape
    meta = jnp.broadcast_to(meta_tokens.astype(x.dtype)[None], (bsz, N_META, d_model))
    h = jnp.concatenate([meta, x], axis=1)
    for layer in range(DEPTH):
        last = layer == DEPTH - 1
        idx = layer // 2
        h = h + FFN_RESIDUAL * swiglu(rmsnorm(h, norm_ff1[layer]), ff1_w_gate[layer],
                                      ff1_w_up[layer], ff1_w_down[layer])
        hn = rmsnorm(h, norm_mix[layer])
        if layer % 2 == 0:
            mix = conv_ssm_mixer(hn, even_w_in[idx], conv_w[idx], ssm_lambda_re[idx],
                                 ssm_lambda_im[idx], ssm_log_step[idx], ssm_b_re[idx],
                                 ssm_b_im[idx], ssm_c_re[idx], ssm_c_im[idx], ssm_d[idx],
                                 glu_w[idx], glu_b[idx], even_w_out[idx])
            if last:
                mix = mix[:, N_META:]
        else:
            mix = window_attention(hn, attn_w_qkv[idx], attn_q_norm[idx], attn_k_norm[idx],
                                   attn_sinks[idx], attn_w_o[idx], real_queries_only=last)
        if last:
            h = h[:, N_META:]
        h = h + mix
        h = h + FFN_RESIDUAL * swiglu(rmsnorm(h, norm_ff2[layer]), ff2_w_gate[layer],
                                      ff2_w_up[layer], ff2_w_down[layer])
    return h


_drawn_inputs = setup_inputs


def setup_inputs(seed=0):
    import zlib

    import numpy as np

    out = dict(_drawn_inputs(seed))
    spreads = {}
    factors = {'norm_ff1': 4.178,
     'ssm_lambda_re': 64.0,
     'ssm_lambda_im': 25.272,
     'ssm_log_step': 26.096,
     'ssm_b_re': 36.072,
     'ssm_b_im': 36.344,
     'ssm_c_re': 35.92,
     'ssm_c_im': 35.464,
     'glu_b': 200.0,
     'attn_q_norm': 150.641,
     'attn_k_norm': 153.825,
     'attn_sinks': 8.0,
     'norm_ff2': 5.847,
     'norm_mix': 3.384}
    for name, (base, spread) in spreads.items():
        noise = np.random.default_rng([zlib.crc32(name.encode()), seed]).standard_normal(out[name].shape)
        drawn = base * np.exp(spread * noise) if base else spread * noise
        out[name] = __import__('jax').numpy.asarray(drawn.astype(out[name].dtype))
    for name, factor in factors.items():
        out[name] = (out[name] * factor).astype(out[name].dtype)
    return out
```

```python
import math
from contextlib import ExitStack

import concourse.bass as bass
from concourse import mybir

F32 = mybir.dt.float32
F32R = mybir.dt.float32r
I32 = mybir.dt.int32
ALU = mybir.AluOpType
ACT = mybir.ActivationFunctionType
AX_X = mybir.AxisListType.X

P = 128
ARENA = 11100
BLK = 16
UNITW = BLK * P


def trunk_program(nc, a, out, stop=None):
    SEQ, DM = a["x"].shape[1], a["x"].shape[2]
    META = a["meta_tokens"].shape[0]
    L = META + SEQ
    KD = DM // P
    DFF = a["ff1_w_gate"].shape[2]
    NF = DFF // P
    PART = [12, NF - 12]
    DC = a["conv_w"].shape[2]
    KC = DC // P
    G, ST = a["ssm_lambda_re"].shape[1:]
    H = a["ssm_b_re"].shape[3]
    T = P // H
    NCH = L // T
    GT = P // H
    NT = SEQ // P
    NH = a["attn_sinks"].shape[1]
    HD = a["attn_q_norm"].shape[1]
    NKV = (a["attn_w_qkv"].shape[2] // HD - NH) // 2
    QP = NH // NKV
    CH = 64
    BAND = P + CH
    KEYS = BAND + META
    KB = KEYS - P
    EPS = 1e-6
    assert ST * 2 == P and T * H == P and NCH * T == L and NH * HD == DM and META % 16 == 0

    FU, FJ = NF + 2 * KD, 2 * NF + 2 * KD
    FF = [(0, 0)]
    MIX = (FU, FJ)
    GLU = (MIX[0] + 2 * KC, MIX[1] + 4 * KC)
    WOUT = (GLU[0] + 1, GLU[1] + KC)
    FF.append((WOUT[0] + KD // 2, WOUT[1] + KD))
    FF.append((FF[1][0] + FU, FF[1][1] + FJ))
    ATT = (FF[2][0] + FU, FF[2][1] + FJ)
    WO = (ATT[0] + 2 + NKV, ATT[1] + 4 + 2 * NKV)
    FF.append((WO[0] + KD // 2, WO[1] + KD))
    LAST_UNIT = FF[3][0] + FU - 1

    FFW = [(a["ff1_w_gate"], a["ff1_w_up"], a["ff1_w_down"], 0), (a["ff2_w_gate"], a["ff2_w_up"], a["ff2_w_down"], 0),
           (a["ff1_w_gate"], a["ff1_w_up"], a["ff1_w_down"], 1), (a["ff2_w_gate"], a["ff2_w_up"], a["ff2_w_down"], 1)]
    FFNORM = [0, 2, 3, 5]
    GAIN = [0, 2 * KD, 4 * KD, KD, 3 * KD, 5 * KD]
    ALL = (0, L // 2)
    REAL = (META, SEQ // 2)
    V_CONV = 6 * KD
    V_GLUB = V_CONV + 3 * KC
    V_QN, V_KN, NV = V_GLUB + KC, V_GLUB + KC + 1, V_GLUB + KC + 2

    with ExitStack() as ctx:
        def sb(name, shape, dt=F32):
            return ctx.enter_context(nc.sbuf_tensor(name, shape, dt))

        def sem(name):
            return ctx.enter_context(nc.semaphore(name))

        h = sb("h", [P, KD, L])
        xh = sb("xh", [P, KD, L], F32R)
        xl = sb("xl", [P, KD, L], F32R)
        act_h = sb("act_h", [P, PART[0], L], F32R)
        act_l = sb("act_l", [P, PART[0], L], F32R)
        raw = sb("raw", [P, 2, UNITW])
        wh = sb("wh", [P, 2, UNITW], F32R)
        wl = sb("wl", [P, 2, UNITW], F32R)
        t_a = sb("t_a", [P, L])
        t_b = sb("t_b", [P, L])
        t_c = sb("t_c", [P, L])
        sq = sb("sq", [P, L])
        ssq = sb("ssq", [P, L])
        r = sb("r", [P, L])
        ident = sb("ident", [P, P])
        ones = sb("ones", [P, P])
        pair_ones = sb("pair_ones", [P, P])
        vec = sb("vec", [P, NV])
        sg = sb("sg", [P, 1])
        d16 = sb("d16", [H, G, H])
        arena = sb("arena", [P, ARENA])
        ps = ctx.enter_context(nc.psum_tensor("ps", [P, 8, 512], F32))
        tabs = nc.dram_tensor("ssm_tables", (KC, P, GT * (T + 1) * H + 2 * P * GT + 3 * GT * NCH), F32, kind="Internal").ap()

        def carve(sizes):
            at, got = 0, []
            for n in sizes:
                got.append(arena[:, at:at + n])
                at += n
            assert at <= ARENA, at
            return got

        (v_xs, v_meta, v_vec, v_lam, v_c4, v_c2, b4, b2, small_all, pw_all) = carve(
            [NT * DM, 2 * G * H, P, 2 * P, 4 * P, 4 * P, G * H, G * H, 24 * G, 5 * (T + 1) * G])
        c4, c2 = v_meta[:, 0:G * H], v_meta[:, G * H:2 * G * H]
        bb4, bb2 = v_c4, v_c2
        v_xs = v_xs.rearrange("p (t d) -> p t d", t=NT)
        v_lam = v_lam.rearrange("p (c n) -> p c n", c=2)
        v_c4 = v_c4.rearrange("p (t n) -> p t n", t=4)
        v_c2 = v_c2.rearrange("p (t n) -> p t n", t=4)
        assert DM <= 2 * G * H
        small = small_all.rearrange("p (n g) -> p n g", g=G)
        pw = pw_all.rearrange("p (n k g) -> p n k g", n=5, g=G)
        WCL = GT * (T + 1) * H
        piece = [arena[:, 0:WCL], arena[:, WCL:2 * WCL]]
        ptmp = arena[:, 2 * WCL:3 * WCL]
        assert 3 * WCL <= NT * DM

        WP = P * GT
        WC = GT * NCH
        WTAB = WCL + 2 * WP + 3 * WC
        (tab, u_t, hc, uc, u_c, blt, kloc, z, zs, y_t) = carve(
            [WTAB, L, L + 2, WP, WC, WP, WP, WC, WC, L])
        cl = tab[:, 0:WCL].rearrange("p (g n) -> p g n", g=GT)
        cl2 = tab[:, WCL:WCL + WP].rearrange("p (g n) -> p g n", g=GT)
        bl = tab[:, WCL + WP:WCL + 2 * WP].rearrange("p (g n) -> p g n", g=GT)
        krow = bl
        cos_t, sin_t, rho_t = (tab[:, WCL + 2 * WP + k * WC:WCL + 2 * WP + (k + 1) * WC] for k in range(3))
        uc4 = uc.rearrange("p (g n) -> p g n", g=GT)
        yc = uc
        u_g = u_c.rearrange("p (g c) -> p g c", g=GT)
        blt_g = blt.rearrange("p (g n) -> p g n", g=GT)
        kloc_g = kloc.rearrange("p (g n) -> p g n", g=GT)
        z_g = z.rearrange("p (g c) -> p g c", g=GT)
        zs_g = zs.rearrange("p (g c) -> p g c", g=GT)

        KW = CH + SEQ + META
        (q_hat, k_pre, k_cur, va, vb, bias, s_all, p_a, p_b, o_all, stat, rtok, sink_t) = carve(
            [2 * SEQ, 2 * KW, KW, NT * 256, NT * 256, QP * KEYS, 2 * QP * KEYS, 512, 512, 512, 2 * 8 * QP, 8, NH])
        q_hat = q_hat.rearrange("p (t n) -> p t n", t=2)
        k_pre = k_pre.rearrange("p (t n) -> p t n", t=2)
        va = va.rearrange("p (j n) -> p j n", j=NT)
        vb = vb.rearrange("p (j n) -> p j n", j=NT)
        s_all = s_all.rearrange("p (b n) -> p b n", b=2)
        o_all = o_all.rearrange("p (b n) -> p b n", b=2)
        stat = stat.rearrange("p (b k n) -> p b k n", b=2, k=8)

        raw_landed = [sem("raw_landed0"), sem("raw_landed1")]
        wh_ready, wl_ready = sem("wh_ready"), sem("wl_ready")
        tile_full, tile_evac = sem("tile_full"), sem("tile_evac")
        x_landed, vec_landed, par_landed, sink_landed = sem("x_landed"), sem("vec_landed"), sem("par_landed"), sem("sink_landed")
        consts = sem("consts")
        init_full, init_evac = sem("init_full"), sem("init_evac")
        silu_done = [sem(f"silu_done{n}") for n in range(4)]
        gated = [sem(f"gated{n}") for n in range(4)]
        act_h_done = [sem(f"act_h_done{n}") for n in range(4)]
        act_ready = [sem(f"act_ready{n}") for n in range(4)]
        sq_done, ssq_step, xh_done, x_ready = sem("sq_done"), sem("ssq_step"), sem("xh_done"), sem("x_ready")
        ssum_full, var_ready, sd_ready, r_ready = sem("ssum_full"), sem("var_ready"), sem("sd_ready"), sem("r_ready")
        prep = sem("prep")
        piece_out = [sem("piece_out0"), sem("piece_out1")]
        tab_landed, kloc_landed = sem("tab_landed"), [sem("kloc_zero"), sem("kloc_landed")]
        dve_mix = sem("dve_mix")
        xf, xe, yf, ye = sem("xbank_full"), sem("xbank_evac"), sem("ybank_full"), sem("ybank_evac")
        yah_done, ya_ready = sem("yah_done"), sem("ya_ready")
        z_step = sem("z_step")
        z_ready, yth_done, yt_ready = sem("z_ready"), sem("yth_done"), sem("yt_ready")
        krow_ready = sem("krow_ready")
        yb_prod, ybh_done, yb_ready = sem("yb_prod"), sem("ybh_done"), sem("yb_ready")
        hn_sq, hn_sum, hn_var, hn_sd, hn_ready = sem("hn_sq"), sem("hn_sum"), sem("hn_var"), sem("hn_sd"), sem("hn_ready")
        hn_step = sem("hn_step")
        rtok_full, rtok_ready, v_ready = sem("rtok_full"), sem("rtok_ready"), sem("v_ready")
        k_cur_ready, bias_ready = sem("k_cur_ready"), sem("bias_ready")
        s_full, s_evac, at_step, nm_ready, p_ready, es_ready = sem("s_full"), sem("s_evac"), sem("at_step"), sem("nm_ready"), sem("p_ready"), sem("es_ready")
        pt_full, pa_evac, pb_evac, o_full, o_ready, ot_full = sem("pt_full"), sem("pa_evac"), sem("pb_evac"), sem("o_full"), sem("o_ready"), sem("ot_full")
        oh_done, ol_done = sem("oh_done"), sem("ol_done")
        fin_full, fin_evac, out_done = sem("fin_full"), sem("fin_evac"), sem("out_done")

        block = ctx.enter_context(nc.Block())
        count = {}

        STAT_STEP = [4, 7, 12, 17]

        def wait(eng, s, v):
            if not isinstance(v, int) or v > 0:
                eng.wait_ge(s, v)

        def halves(ap, col):
            c0, nh = col
            return ap[:, c0:c0 + 2 * nh].rearrange("p (b n) -> p b n", b=2)

        @block.gpsimd
        def _(pool):
            g = nc.gpsimd
            made = [0]

            def const(ins):
                ins.then_inc(consts, 1)
                made[0] += 1
                pool.wait_ge(consts, made[0])

            const(g.memset(ident[:], 0.0))
            const(g.affine_select(out=ident[:], in_=ident[:], compare_op=ALU.not_equal, fill=1.0, base=0,
                                  pattern=[[-1, P]], channel_multiplier=1))
            const(g.memset(ones[:], 1.0))
            const(g.memset(pair_ones[:], 0.0))
            const(g.memset(pair_ones[0:HD, 0:HD], 1.0))
            const(g.memset(pair_ones[HD:P, HD:P], 1.0))
            const(g.memset(sg[0:ST, :], 1.0))
            const(g.memset(sg[ST:P, :], -1.0))
            assert made[0] == 8

            n_par = 0
            for half in range(2):
                rows = slice(half * ST, (half + 1) * ST)
                re, im = a["ssm_b_re"][0].rearrange("g p h -> p g h"), a["ssm_b_im"][0].rearrange("g p h -> p g h")
                for dst, src in ((b4, (re, im)[half]), (b2, (im, re)[half])):
                    pool.dma_start(dst[rows, :].rearrange("p (g h) -> p g h", g=G), src).then_inc(par_landed, 16)
                    n_par += 1
                cols = slice(half * ST, (half + 1) * ST)
                cre, cim = (a[n][0].rearrange("(t a) h p -> (a h) t p", t=4) for n in ("ssm_c_re", "ssm_c_im"))
                for dst, src in ((v_c4, (cre, cim)[half]), (v_c2, (cim, cre)[half])):
                    pool.dma_start(dst[:, :, cols], src).then_inc(par_landed, 16)
                    n_par += 1
            pool.dma_start(small[:, 0, :], a["ssm_log_step"].partition_broadcast(P)).then_inc(par_landed, 16)
            pool.dma_start(d16[:].rearrange("p g h -> p (g h)"), a["ssm_d"].partition_broadcast(H)).then_inc(par_landed, 16)
            assert n_par + 2 == 10

            steps = [0]

            def did(ins):
                ins.then_inc(prep, 1)
                steps[0] += 1
                pool.wait_ge(prep, steps[0])

            def tt(o, x, y, op):
                did(g.tensor_tensor(o, x, y, op))

            def ts(o, x, s1, op0, s2=None, op1=None):
                did(g.tensor_scalar(o, x, s1, s2, op0, op1) if op1 is not None else g.tensor_scalar(o, x, s1, None, op0))

            pool.wait_ge(par_landed, 160)
            pool.wait_ge(init_evac, 10)
            S = lambda k: small[:, k, :]
            (LOGST, LRE, LIM, STEP, T0, T1, T2, T3, AR, AI, TH, CQ, CW, SN, CS, MG, A8R, A8I, R8, KF, K1, K2, P1, P2) = range(24)
            tt(d16[:], d16[:], ident[0:H, 0:H].unsqueeze(1).to_broadcast([H, G, H]), ALU.mult)

            RND = 1.5 * 2.0 ** 23

            def exp_of(o, x):
                ts(S(T0), x, -180.0, ALU.max, 180.0, ALU.min)
                ts(S(KF), S(T0), 1.0 / math.log(2.0), ALU.mult)
                ts(S(KF), S(KF), RND, ALU.add)
                ts(S(KF), S(KF), -RND, ALU.add)
                ln2_hi = 0.693359375
                ln2_lo = math.log(2.0) - ln2_hi
                ts(S(T1), S(KF), -ln2_hi, ALU.mult)
                tt(S(T0), S(T0), S(T1), ALU.add)
                ts(S(T1), S(KF), -ln2_lo, ALU.mult)
                tt(S(T0), S(T0), S(T1), ALU.add)
                ts(S(T1), S(T0), 1.0 / 5040, ALU.mult, 1.0 / 720, ALU.add)
                for c in (1.0 / 120, 1.0 / 24, 1.0 / 6, 0.5, 1.0, 1.0):
                    tt(S(T1), S(T1), S(T0), ALU.mult)
                    ts(S(T1), S(T1), c, ALU.add)
                ts(S(K1), S(KF), 0.5, ALU.mult)
                ts(S(K1), S(K1), RND, ALU.add)
                ts(S(K1), S(K1), -RND, ALU.add)
                tt(S(K2), S(KF), S(K1), ALU.subtract)
                for k, p in ((K1, P1), (K2, P2)):
                    ts(S(k), S(k), -126.0, ALU.max, 127.0, ALU.min)
                    ts(S(k), S(k), 127.0, ALU.add)
                    did(g.tensor_scalar(S(p).bitcast(I32), S(k), 2.0 ** 23, None, ALU.mult))
                tt(S(T1), S(T1), S(P1), ALU.mult)
                tt(o, S(T1), S(P2), ALU.mult)

            exp_of(S(STEP), S(LOGST))
            tt(S(T3), S(LRE), S(STEP), ALU.mult)
            exp_of(S(MG), S(T3))
            tt(S(TH), S(LIM), S(STEP), ALU.mult)
            ts(S(KF), S(TH), 2.0 / math.pi, ALU.mult)
            ts(S(KF), S(KF), RND, ALU.add)
            ts(S(KF), S(KF), -RND, ALU.add)
            pi_1 = 1.5703125
            pi_2 = 4.837512969970703125e-4
            pi_3 = math.pi / 2 - pi_1 - pi_2
            for c in (pi_1, pi_2, pi_3):
                ts(S(T0), S(KF), -c, ALU.mult)
                tt(S(TH), S(TH), S(T0), ALU.add)
            tt(S(T0), S(TH), S(TH), ALU.mult)
            ts(S(SN), S(T0), 1.0 / 362880, ALU.mult, -1.0 / 5040, ALU.add)
            for c in (1.0 / 120, -1.0 / 6, 1.0):
                tt(S(SN), S(SN), S(T0), ALU.mult)
                ts(S(SN), S(SN), c, ALU.add)
            tt(S(SN), S(SN), S(TH), ALU.mult)
            ts(S(CS), S(T0), -1.0 / 3628800, ALU.mult, 1.0 / 40320, ALU.add)
            for c in (-1.0 / 720, 1.0 / 24, -0.5, 1.0):
                tt(S(CS), S(CS), S(T0), ALU.mult)
                ts(S(CS), S(CS), c, ALU.add)
            ts(S(T1), S(KF), 0.25, ALU.mult)
            ts(S(T1), S(T1), RND, ALU.add)
            ts(S(T1), S(T1), -RND, ALU.add)
            ts(S(T1), S(T1), -4.0, ALU.mult)
            tt(S(T1), S(T1), S(KF), ALU.add)
            ts(S(T2), S(T1), 0.0, ALU.max, 2.0, ALU.mult)
            tt(S(T2), S(T2), S(T1), ALU.subtract)
            ts(S(K1), S(T2), -1.0, ALU.mult, 1.0, ALU.add)
            ts(S(K2), S(T2), -1.0, ALU.mult, 2.0, ALU.add)
            tt(S(K2), S(K2), S(T1), ALU.mult)
            tt(S(T0), S(CS), S(K1), ALU.mult)
            tt(S(T1), S(SN), S(K2), ALU.mult)
            tt(S(T2), S(SN), S(K1), ALU.mult)
            tt(S(T3), S(CS), S(K2), ALU.mult)
            tt(S(CS), S(T0), S(T1), ALU.subtract)
            tt(S(SN), S(T2), S(T3), ALU.add)
            tt(S(AR), S(MG), S(CS), ALU.mult)
            tt(S(AI), S(MG), S(SN), ALU.mult)
            ts(S(T0), S(AR), -1.0, ALU.add)
            tt(S(T1), S(LRE), S(LRE), ALU.mult)
            tt(S(T2), S(LIM), S(LIM), ALU.mult)
            tt(S(T3), S(T1), S(T2), ALU.add)
            did(g.memset(S(K1), -1.0))
            tt(S(T1), S(T3), S(K1), ALU.pow)
            tt(S(T2), S(T3), S(T1), ALU.mult)
            ts(S(T2), S(T2), -1.0, ALU.mult, 2.0, ALU.add)
            tt(S(T3), S(T1), S(T2), ALU.mult)
            tt(S(T1), S(T0), S(LRE), ALU.mult)
            tt(S(T2), S(AI), S(LIM), ALU.mult)
            tt(S(T1), S(T1), S(T2), ALU.add)
            tt(S(CQ), S(T1), S(T3), ALU.mult)
            tt(S(T1), S(AI), S(LRE), ALU.mult)
            tt(S(T2), S(T0), S(LIM), ALU.mult)
            tt(S(T1), S(T1), S(T2), ALU.subtract)
            tt(S(CW), S(T1), S(T3), ALU.mult)
            did(g.memset(pw[:, 0, 0, :], 1.0))
            did(g.memset(pw[:, 1, 0, :], 0.0))

            def cmul(o_r, o_i, x_r, x_i, y_r, y_i, t0, t1, t2, t3):
                tt(t0, x_r, y_r, ALU.mult)
                tt(t1, x_i, y_i, ALU.mult)
                tt(t2, x_r, y_i, ALU.mult)
                tt(t3, x_i, y_r, ALU.mult)
                tt(o_r, t0, t1, ALU.subtract)
                tt(o_i, t2, t3, ALU.add)

            for k in range(T):
                cmul(pw[:, 0, k + 1, :], pw[:, 1, k + 1, :], pw[:, 0, k, :], pw[:, 1, k, :], S(AR), S(AI), S(T0), S(T1), S(T2), S(T3))
            did(g.tensor_scalar(pw[:, 2, :, :], pw[:, 0, :, :], sg[:, 0:1], None, ALU.mult))
            did(g.tensor_scalar(pw[:, 3, :, :], pw[:, 1, :, :], sg[:, 0:1], None, ALU.mult))
            did(g.tensor_scalar(pw[:, 4, :, :], pw[:, 2, :, :], -1.0, None, ALU.mult))
            for k in range(int(math.log2(T))):
                cmul(S(CS), S(SN), S(CS), S(SN), S(CS), S(SN), S(T0), S(T1), S(T2), S(T3))
                tt(S(MG), S(MG), S(MG), ALU.mult)
            v3 = lambda t: t.rearrange("p (g h) -> p g h", g=G)
            bc = lambda x: x.unsqueeze(2).to_broadcast([P, G, H])
            did(g.tensor_scalar(S(T2), S(CW), sg[:, 0:1], None, ALU.mult))
            tmp5 = v3(ptmp[:, 0:G * H])
            tt(v3(bb4), v3(b4), bc(S(CQ)), ALU.mult)
            tt(tmp5, v3(b2), bc(S(T2)), ALU.mult)
            tt(v3(bb4), v3(bb4), tmp5, ALU.subtract)
            tt(v3(bb2), v3(b2), bc(S(CQ)), ALU.mult)
            tt(tmp5, v3(b4), bc(S(T2)), ALU.mult)
            tt(v3(bb2), v3(bb2), tmp5, ALU.add)

            n_piece = [0]

            def start_piece(width):
                n = n_piece[0]
                if n >= 2:
                    pool.wait_ge(piece_out[n % 2], 16 * (n // 2))
                return piece[n % 2][:, 0:width]

            def end_piece(ft, at, buf, width):
                n = n_piece[0]
                pool.dma_start(tabs[ft, :, at:at + width], buf).then_inc(piece_out[n % 2], 16)
                n_piece[0] += 1

            for ft in range(KC):
                gs = slice(ft * GT, (ft + 1) * GT)

                def table(row_a, x_a, row_b, x_b, lo, hi, at, rev=False):
                    n = hi - lo
                    w = GT * n * H
                    buf = start_piece(w)
                    o = buf.rearrange("p (g k h) -> p g k h", g=GT, k=n)
                    t = ptmp[:, 0:w].rearrange("p (g k h) -> p g k h", g=GT, k=n)
                    for k in range(n):
                        ko = n - 1 - k if rev else k
                        pk = lambda row: pw[:, row, lo + k, gs].unsqueeze(2).to_broadcast([P, GT, H])
                        tt(o[:, :, ko, :], v3(x_a)[:, gs, :], pk(row_a), ALU.mult)
                        tt(t[:, :, ko, :], v3(x_b)[:, gs, :], pk(row_b), ALU.mult)
                    tt(buf, buf, ptmp[:, 0:w], ALU.subtract)
                    end_piece(ft, at, buf, w)

                table(2, c4, 1, c2, 0, T + 1, 0)
                table(4, c2, 1, c4, 1, T + 1, WCL)
                table(0, bb4, 3, bb2, 0, T, WCL + WP, rev=True)
                cbuf = start_piece(WC)
                n0 = n_piece[0]
                n_piece[0] += 1
                sbuf_ = start_piece(WC)
                n_piece[0] = n0
                cv = cbuf.rearrange("p (g c) -> p g c", g=GT)
                sv = sbuf_.rearrange("p (g c) -> p g c", g=GT)
                did(g.memset(cv[:, :, 0:1], 1.0))
                did(g.memset(sv[:, :, 0:1], 0.0))
                did(g.tensor_copy(cv[:, :, 1:2], small[:, CS, gs].unsqueeze(2)))
                did(g.tensor_copy(sv[:, :, 1:2], small[:, SN, gs].unsqueeze(2)))
                did(g.tensor_copy(small[:, A8R, gs], small[:, CS, gs]))
                did(g.tensor_copy(small[:, A8I, gs], small[:, SN, gs]))
                k = 1
                while k < NCH - 1:
                    n = min(k, NCH - 1 - k)
                    br = small[:, A8R, gs].unsqueeze(2).to_broadcast([P, GT, n])
                    bi = small[:, A8I, gs].unsqueeze(2).to_broadcast([P, GT, n])
                    ta = ptmp[:, 0:GT * n].rearrange("p (g c) -> p g c", g=GT)
                    tb = ptmp[:, GT * 32:GT * 32 + GT * n].rearrange("p (g c) -> p g c", g=GT)
                    tt(ta, cv[:, :, 1:1 + n], br, ALU.mult)
                    tt(tb, sv[:, :, 1:1 + n], bi, ALU.mult)
                    tt(cv[:, :, k + 1:k + 1 + n], ta, tb, ALU.subtract)
                    tt(ta, cv[:, :, 1:1 + n], bi, ALU.mult)
                    tt(tb, sv[:, :, 1:1 + n], br, ALU.mult)
                    tt(sv[:, :, k + 1:k + 1 + n], ta, tb, ALU.add)
                    did(g.tensor_copy(small[:, A8R, gs], cv[:, :, 2 * k if 2 * k < NCH else 1]))
                    did(g.tensor_copy(small[:, A8I, gs], sv[:, :, 2 * k if 2 * k < NCH else 1]))
                    k += n
                did(g.tensor_scalar(sbuf_, sbuf_, sg[:, 0:1], None, ALU.mult))
                end_piece(ft, WCL + 2 * WP, cbuf, WC)
                end_piece(ft, WCL + 2 * WP + WC, sbuf_, WC)
                rbuf = start_piece(WC)
                rv = rbuf.rearrange("p (g c) -> p g c", g=GT)
                did(g.tensor_copy(rv, small[:, MG, gs].unsqueeze(2).to_broadcast([P, GT, NCH])))
                did(g.memset(rv[:, :, 0:1], 0.0))
                end_piece(ft, WCL + 2 * WP + 2 * WC, rbuf, WC)
            n = n_piece[0]
            pool.wait_ge(piece_out[0], 16 * ((n + 1) // 2))
            pool.wait_ge(piece_out[1], 16 * (n // 2))

            did(g.memset(kloc, 0.0))
            did(g.memset(z_g[:, :, 0:1], 0.0))
            did(g.memset(hc[:, 0:2], 0.0))
            count['mix_zeroed'] = steps[0]
            for i in range(KC):
                if i:
                    pool.wait_ge(xf, 4 * i)
                pool.dma_start(tab, tabs[i]).then_inc(tab_landed, 16)
                pool.wait_ge(krow_ready, i + 1)
                pool.wait_ge(ye, 4 * i + 2)
                for t in range(T):
                    pool.dma_start(kloc_g[t * H:(t + 1) * H, :, t * H:P], krow[0:H, :, 0:P - t * H]).then_inc(kloc_landed[1], 16)
                pool.wait_ge(kloc_landed[1], 16 * T * (i + 1))

            pool.wait_ge(yb_ready, KC)
            pool.dma_start(sink_t, a["attn_sinks"].partition_broadcast(P)).then_inc(sink_landed, 16)
            d0 = k_cur[:, 0:KEYS]
            did(g.iota(d0[:, 0:BAND], pattern=[[-1, BAND]], base=CH, channel_multiplier=1, allow_small_or_imprecise_dtypes=True))
            d1 = k_cur[:, KEYS:KEYS + BAND]
            ts(d1, d0[:, 0:BAND], 0.0, ALU.max, 2.0, ALU.mult)
            tt(d0[:, 0:BAND], d1, d0[:, 0:BAND], ALU.subtract)
            did(g.memset(d0[0:CH, P:BAND], 1e36))
            did(g.memset(d0[CH:P, 0:CH], 1e36))
            did(g.memset(d0[:, BAND:KEYS], 0.0))
            for k in range(QP):
                ts(bias[:, k * KEYS:(k + 1) * KEYS], d0, -4.0 * 2.0 ** (-8.0 * (k + 1) / NH), ALU.mult)
            did(g.memset(k_pre[:, :, 0:CH], 0.0))
            did(g.memset(va[0:CH, 0, :], 0.0))
            count['att_consts'] = steps[0]

        @block.sync
        def _(sp):
            def load_unit(c, i, sources):
                wait(sp, wl_ready, c - 1 + 2 * i)
                for src, b0, nk in sources:
                    m = src.shape[2]
                    sp.dma_start(raw[:, c % 2, b0 * P:b0 * P + nk * m].rearrange("p (k m) -> p k m", k=nk), src).then_inc(raw_landed[c % 2], 16)

            def by_rows(w):
                return w.rearrange("(k p) f -> p k f", p=P)

            def ffn_loads(n):
                wg, wu, wd, layer = FFW[n]
                u0 = FF[n][0]
                wg, wu, wd = by_rows(wg[layer]), by_rows(wu[layer]), by_rows(wd[layer])
                f0 = 0
                for nf in PART:
                    def gate_up(i):
                        for s in range(2):
                            cols = bass.ds((2 * i + s + f0) * P, P)
                            load_unit(u0 + s, i, [(wg[:, :, cols], 0, KD), (wu[:, :, cols], KD, KD)])

                    def down(i):
                        for s in range(2):
                            cols = bass.ds((2 * i + s) * P, P)
                            load_unit(u0 + nf + s, i, [(wd[:, f0:f0 + nf // 2, cols], 0, nf // 2), (wd[:, f0 + nf // 2:f0 + nf, cols], nf // 2, nf // 2)])

                    gate_up(0)
                    with sp.Fori(1, nf // 2) as i:
                        gate_up(i)
                    with sp.Fori(0, KD // 2) as i:
                        down(i)
                    u0 += nf + KD
                    f0 += nf

            sp.dma_start(v_vec[0:2 * KD, :], a["norm_ff1"].rearrange("l (k p) -> (l k) p", p=P)).then_inc(vec_landed, 16)
            sp.dma_start(v_vec[2 * KD:4 * KD, :], a["norm_mix"].rearrange("l (k p) -> (l k) p", p=P)).then_inc(vec_landed, 16)
            sp.dma_start(v_vec[4 * KD:6 * KD, :], a["norm_ff2"].rearrange("l (k p) -> (l k) p", p=P)).then_inc(vec_landed, 16)
            sp.dma_start(v_vec[V_CONV:V_GLUB, :], a["conv_w"].rearrange("l w (k p) -> (l w k) p", p=P)).then_inc(vec_landed, 16)
            sp.dma_start(v_vec[V_GLUB:V_QN, :], a["glu_b"].rearrange("l (k p) -> (l k) p", p=P)).then_inc(vec_landed, 16)
            for half in range(2):
                sp.dma_start(v_vec[V_QN:V_QN + 1, half * HD:(half + 1) * HD], a["attn_q_norm"]).then_inc(vec_landed, 16)
                sp.dma_start(v_vec[V_KN:V_KN + 1, half * HD:(half + 1) * HD], a["attn_k_norm"]).then_inc(vec_landed, 16)
                sp.dma_start(v_lam[0:G, 0, half * ST:(half + 1) * ST], a["ssm_lambda_re"][0]).then_inc(vec_landed, 16)
                sp.dma_start(v_lam[0:G, 1, half * ST:(half + 1) * ST], a["ssm_lambda_im"][0]).then_inc(vec_landed, 16)
            sp.dma_start(v_meta[0:META, :], a["meta_tokens"]).then_inc(x_landed, 16)
            sp.dma_start(v_xs, a["x"][0].rearrange("(t p) d -> p t d", p=P)).then_inc(x_landed, 16)

            ffn_loads(0)
            w_in = by_rows(a["even_w_in"][0])
            for i in range(KC):
                for s, (c0, c1) in enumerate(((3 * DC, 2 * DC), (0, DC))):
                    load_unit(MIX[0] + s, i, [(w_in[:, :, c0 + i * P:c0 + (i + 1) * P], 0, KD), (w_in[:, :, c1 + i * P:c1 + (i + 1) * P], KD, KD)])
            glu = by_rows(a["glu_w"][0])
            load_unit(GLU[0], 0, [(glu[:, 0:KC // 2, :], 0, KC // 2), (glu[:, KC // 2:KC, :], KC // 2 * KC, KC // 2)])

            def two_column_tiles(w, u0, s, i):
                load_unit(u0 + s, i, [(w[:, :, bass.ds((2 * (2 * i + s) + n) * P, P)], n * KD, KD) for n in range(2)])

            w_out = by_rows(a["even_w_out"][0])
            with sp.Fori(0, KD // 4) as i:
                for s in range(2):
                    two_column_tiles(w_out, WOUT[0], s, i)
            ffn_loads(1)
            ffn_loads(2)
            w_qkv = by_rows(a["attn_w_qkv"][0])
            load_unit(ATT[0], 0, [(w_qkv[:, :, NH * HD + n * P:NH * HD + (n + 1) * P], n * KD, KD) for n in range(2)])
            v0 = (NH + NKV) * HD
            load_unit(ATT[0] + 1, 0, [(w_qkv[:, 0:KD // 2, v0:v0 + NKV * HD], 0, KD // 2), (w_qkv[:, KD // 2:KD, v0:v0 + NKV * HD], KD, KD // 2)])
            with sp.Fori(0, NKV // 2) as i:
                for s in range(2):
                    two_column_tiles(w_qkv, ATT[0] + 2, s, i)
            w_o = by_rows(a["attn_w_o"][0])
            with sp.Fori(0, KD // 4) as i:
                for s in range(2):
                    two_column_tiles(w_o, WO[0], s, i)
            ffn_loads(3)
            for d in range(KD):
                sp.wait_ge(fin_evac, d + 1)
                sp.dma_start(out[0, :, d * P:(d + 1) * P].rearrange("(t p) f -> p t f", p=P),
                             arena[:, d * 512:(d + 1) * 512].rearrange("p (t f) -> p t f", t=NT)).then_inc(out_done, 16)
            sp.wait_ge(out_done, 16 * KD)


        @block.tensor
        def _(pe):
            def mm3(pair, slot, blocks, x_h, x_l, k0, col, before_last=None):
                c0, nh = col
                n = len(blocks)
                for k, b in enumerate(blocks):
                    if k == n - 1 and before_last:
                        before_last()
                    for q, (w, x) in enumerate(((wh, x_h), (wh, x_l), (wl, x_h))):
                        for hf in range(2):
                            last = nc.tensor.matmul(ps[:, 2 * pair + hf, 0:nh], w[:, slot, b * P:(b + 1) * P],
                                                    x[:, k0 + k, c0 + hf * nh:c0 + (hf + 1) * nh],
                                                    start=(k == 0 and q == 0), stop=(k == n - 1 and q == 2))
                return last

            def token_sums(m, col):
                c0, nh = col
                pe.wait_ge(ssq_step, (KD + 1) * (m + 1))
                for hf in range(2):
                    last = nc.tensor.matmul(ps[:, 4 + hf, 0:nh], ones[:], ssq[:, c0 + hf * nh:c0 + (hf + 1) * nh], start=True, stop=True)
                last.then_inc(ssum_full, 1)

            def x_job(u, j, pair, slot, blocks, col, m=None, new_unit=True):
                if new_unit:
                    pe.wait_ge(wl_ready, u + 1)
                wait(pe, tile_evac, j - 1)
                before = None
                if m is not None:
                    pe.wait_ge(x_ready, KD * m + KD - 1)
                    before = lambda: pe.wait_ge(x_ready, KD * m + KD)
                mm3(pair, slot, blocks, xh, xl, 0, col, before).then_inc(tile_full, 1)

            def ffn(n, col):
                m = FFNORM[n]
                u0, j0 = FF[n]
                done = 0
                for part, nf in enumerate(PART):
                    def gate_up(i, m=None):
                        for s in range(2):
                            u, j = u0 + s + 2 * i, j0 + 2 * s + 4 * i
                            x_job(u, j, 0, (u0 + s) % 2, range(KD), col, m if s == 0 else None)
                            if m is not None and s == 0:
                                token_sums(m, col)
                            x_job(u, j + 1, 1, (u0 + s) % 2, range(KD, 2 * KD), col, new_unit=False)

                    gate_up(0, m if part == 0 else None)
                    with pe.Fori(1, nf // 2) as i:
                        gate_up(i)
                    u0 += nf
                    j0 += 2 * nf
                    done += nf
                    with pe.Fori(0, KD // 2) as i:
                        for s in range(2):
                            pe.wait_ge(wl_ready, u0 + s + 2 * i + 1)
                            pe.wait_ge(tile_evac, j0 + s + 2 * i - 1)
                            pe.wait_ge(act_ready[n], done - 1)
                            mm3(s, (u0 + s) % 2, range(nf), act_h, act_l, 0, col,
                                lambda: pe.wait_ge(act_ready[n], done)).then_inc(tile_full, 1)
                    u0 += KD
                    j0 += KD

            X = ps[:, 4:6, :].rearrange("p b n -> p (b n)")
            Y = ps[:, 6:8, :].rearrange("p b n -> p (b n)")

            pe.wait_ge(consts, 8)
            pe.wait_ge(vec_landed, 13 * 16)
            nc.tensor.transpose(X[:, 0:NV], v_vec[0:NV, :], ident[0:NV, 0:NV])
            for c in range(2):
                last = nc.tensor.transpose(X[:, P * (c + 1):P * (c + 1) + G], v_lam[0:G, c, :], ident[0:G, 0:G])
            last.then_inc(init_full, 1)
            pe.wait_ge(x_landed, 32)
            for d in range(KD):
                bank = 6 if d % 2 == 0 else 4
                wait(pe, init_evac, d)
                for t in range(NT):
                    nc.tensor.transpose(ps[:, bank, t * P:(t + 1) * P], v_xs[:, t, d * P:(d + 1) * P], ident[:])
                nc.tensor.transpose(ps[:, bank + 1, 0:META], v_meta[0:META, d * P:(d + 1) * P], ident[0:META, 0:META]).then_inc(init_full, 1)
            pe.wait_ge(init_evac, KD)
            pe.wait_ge(par_landed, 160)
            for b, v in ((6, v_c4), (7, v_c2)):
                for t in range(4):
                    last = nc.tensor.transpose(ps[:, b, t * P:(t + 1) * P], v[:, t, :], ident[:])
            last.then_inc(init_full, 1)

            ffn(0, ALL)

            def ssm_out(i):
                pe.wait_ge(z_ready, 2 * i + 2)
                pe.wait_ge(kloc_landed[1], 16 * T * (i + 1))
                pe.wait_ge(xe, 4 * i + 3)
                for g in range(GT):
                    o = X[0:NCH, g * P:(g + 1) * P]
                    nc.tensor.matmul(o, u_g[:, g, :], kloc_g[:, g, :], start=True, stop=False)
                    nc.tensor.matmul(o, z_g[:, g, :], cl[:, g, H:(T + 1) * H], start=False, stop=False)
                    last = nc.tensor.matmul(o, zs_g[:, g, :], cl2[:, g, :], start=False, stop=True)
                last.then_inc(xf, 1)

            def y_features(i):
                pe.wait_ge(xe, 4 * i + 4)
                pe.wait_ge(ye, 4 * i + 3)
                yv = yc[0:NCH].rearrange("c (t n) -> c t n", t=T)
                for t in range(T):
                    last = nc.tensor.transpose(ps[:, 6 + t // 4, (t % 4) * NCH:(t % 4 + 1) * NCH],
                                               yv[:, t, :], ident[0:NCH, 0:NCH])
                last.then_inc(yf, 1)

            def mixer(i, m=None):
                u, j = MIX[0] + 2 * i, MIX[1] + 4 * i
                s0 = MIX[0] % 2
                x_job(u, j, 0, s0, range(KD), ALL, m)
                if m is not None:
                    token_sums(m, ALL)
                else:
                    ssm_out(i - 1)
                x_job(u, j + 1, 1, s0, range(KD, 2 * KD), ALL, new_unit=False)
                if m is None:
                    y_features(i - 1)
                pe.wait_ge(tile_evac, j + 1)
                wait(pe, xe, 4 * i)
                if m is not None:
                    pe.wait_ge(var_ready, m + 1)
                uv = u_t.rearrange("p (c t) -> p c t", t=T)
                for t in range(T):
                    last = nc.tensor.transpose(X[0:NCH, t * P:(t + 1) * P], uv[:, :, t], ident[:])
                last.then_inc(xf, 1)
                x_job(u + 1, j + 2, 0, 1 - s0, range(KD), ALL)
                pe.wait_ge(xe, 4 * i + 1)
                wait(pe, ye, 4 * i)
                for g in range(GT):
                    last = nc.tensor.transpose(ps[:, 6 + g // 4, (g % 4) * NCH:(g % 4 + 1) * NCH],
                                               uc4[0:NCH, g, :], ident[0:NCH, 0:NCH])
                last.then_inc(yf, 1)
                pe.wait_ge(tab_landed, 16 * (i + 1))
                for g in range(GT):
                    last = nc.tensor.transpose(X[:, g * P:(g + 1) * P], bl[:, g, :], ident[:])
                last.then_inc(xf, 1)
                x_job(u + 1, j + 3, 1, 1 - s0, range(KD, 2 * KD), ALL, new_unit=False)
                pe.wait_ge(ye, 4 * i + 1)
                for g in range(GT):
                    last = nc.tensor.matmul(Y[0:H, g * P:(g + 1) * P], bl[:, g, (T - 1) * H:T * H], cl[:, g, 0:T * H], start=True, stop=True)
                last.then_inc(yf, 1)
                pe.wait_ge(xe, 4 * i + 2)
                for g in range(GT):
                    last = nc.tensor.matmul(ps[:, 4 + g // 4, (g % 4) * NCH:(g % 4 + 1) * NCH], blt_g[:, g, :], u_g[:, g, :], start=True, stop=True)
                last.then_inc(xf, 1)
                pe.wait_ge(ye, 4 * i + 2)
                for g in range(GT):
                    o = ps[:, 6 + g // 4, (g % 4) * NCH:(g % 4 + 1) * NCH]
                    nc.tensor.matmul(o[0:ST], blt_g[:, g, ST:P], u_g[:, g, :], start=True, stop=True)
                    last = nc.tensor.matmul(o[ST:P], blt_g[:, g, 0:ST], u_g[:, g, :], start=True, stop=True)
                last.then_inc(yf, 1)

            mixer(0, 1)
            with pe.Fori(1, KC) as i:
                mixer(i)
            ssm_out(KC - 1)
            y_features(KC - 1)
            pe.wait_ge(wl_ready, GLU[0] + 1)
            for k in range(KC):
                j = GLU[1] + k
                pe.wait_ge(tile_evac, j - 1)
                pe.wait_ge(yt_ready, KC)
                mm3(k % 2, GLU[0] % 2, range(k, KC * KC, KC), act_h, act_l, 2 * KC, ALL).then_inc(tile_full, 1)

            def project(u0, j0, col, inputs):
                with pe.Fori(0, KD // 4) as i:
                    for s in range(2):
                        for n in range(2):
                            if n == 0:
                                pe.wait_ge(wl_ready, u0 + s + 2 * i + 1)
                            pe.wait_ge(tile_evac, j0 + 2 * s + n + 4 * i - 1)
                            for sm, c in inputs[0]:
                                pe.wait_ge(sm, c)
                            mm3(n, (u0 + s) % 2, range(n * KD, (n + 1) * KD), act_h, act_l, 0, col,
                                lambda: pe.wait_ge(*inputs[1])).then_inc(tile_full, 1)

            project(*WOUT, ALL, ([(ya_ready, KC), (yb_ready, KC - 1)], (yb_ready, KC)))
            ffn(1, ALL)
            ffn(2, ALL)

            def head_sums(q, col):
                b = 4 + 2 * (q % 2)
                nh = col[1]
                pe.wait_ge(hn_sq, q + 1)
                src = (t_b, sq)[q % 2]
                for hf in range(2):
                    last = nc.tensor.matmul(ps[:, b + hf, 0:nh], pair_ones[:], src[:, hf * nh:(hf + 1) * nh], start=True, stop=True)
                last.then_inc(hn_sum, 1)

            u0, j0 = ATT
            x_job(u0, j0, 0, u0 % 2, range(KD), ALL, 4)
            token_sums(4, ALL)
            x_job(u0, j0 + 1, 1, u0 % 2, range(KD, 2 * KD), ALL, new_unit=False)
            pe.wait_ge(var_ready, 5)
            head_sums(0, ALL)
            slot = (u0 + 1) % 2
            pe.wait_ge(wl_ready, u0 + 2)
            VW = NKV * HD

            def v_tile(bank, c0):
                for k in range(KD):
                    for q, (x, w) in enumerate(((xh, wh), (xl, wh), (xh, wl))):
                        last = nc.tensor.matmul(ps[:, bank, 0:VW], x[:, k, c0:c0 + P], w[:, slot, k * VW:(k + 1) * VW],
                                                start=(k == 0 and q == 0), stop=(k == KD - 1 and q == 2))
                return last

            for pair in range(2):
                pe.wait_ge(tile_evac, j0 + 1 + pair)
                v_tile(2 * pair, META + 2 * pair * P)
                v_tile(2 * pair + 1, META + (2 * pair + 1) * P).then_inc(tile_full, 1)
            head_sums(1, ALL)
            pe.wait_ge(hn_var, 1)
            v_tile(4, 0)
            pe.wait_ge(r_ready, 5)
            for t in range(NT):
                nc.tensor.matmul(ps[:, 5, t:t + 1], r[0:1, META + t * P:META + (t + 1) * P], ones[0:1, 0:1], start=True, stop=True)
            nc.tensor.matmul(ps[0:META, 5, NT:NT + 1], r[0:1, 0:META], ones[0:1, 0:1], start=True, stop=True).then_inc(rtok_full, 1)

            def scores(n, j):
                pe.wait_ge(s_evac, n) if not isinstance(n, int) or n > 0 else None
                for k in range(QP):
                    rows = slice((k % 2) * HD, (k % 2 + 1) * HD)
                    q = q_hat[rows, k // 2, j * P:(j + 1) * P]
                    o = ps[:, 4 + k % 2, (k // 2) * KEYS:(k // 2 + 1) * KEYS]
                    nc.tensor.matmul(o[:, 0:BAND], q, k_cur[rows, j * P:j * P + BAND], start=True, stop=True)
                    last = nc.tensor.matmul(o[:, BAND:KEYS], q, k_cur[rows, CH + SEQ:KW], start=True, stop=True)
                last.then_inc(s_full, 1)

            def probs_t(n, j):
                pe.wait_ge(p_ready, n + 1)
                wait(pe, pa_evac, n)
                wait(pe, pb_evac, n)
                for k in range(QP):
                    p = s_all[:, j % 2, k * KEYS:(k + 1) * KEYS]
                    nc.tensor.transpose(ps[:, 6, k * P:(k + 1) * P], p[:, 0:P], ident[:])
                    last = nc.tensor.transpose(ps[0:KB, 7, k * P:(k + 1) * P], p[:, P:KEYS], ident[:])
                last.then_inc(pt_full, 1)

            def values(n, j, g):
                pe.wait_ge(pa_evac, n + 1)
                pe.wait_ge(pb_evac, n + 1)
                if j >= 2 or not isinstance(n, int):
                    pe.wait_ge(o_ready, n - 1)
                cols = bass.ds(g * HD, HD)
                for k in range(QP):
                    o = ps[:, 2 + j % 2, k * HD:(k + 1) * HD]
                    nc.tensor.matmul(o, p_a[:, k * P:(k + 1) * P], va[:, j, cols], start=True, stop=False)
                    last = nc.tensor.matmul(o, p_b[0:KB, k * P:(k + 1) * P], vb[0:KB, j, cols], start=False, stop=True)
                last.then_inc(o_full, 1)

            def out_t(n, j):
                pe.wait_ge(o_ready, n + 1)
                if j >= 2 or not isinstance(n, int):
                    pe.wait_ge(ol_done, n - 1)
                for t in range(2):
                    last = nc.tensor.transpose(ps[:, j % 2, t * P:(t + 1) * P], o_all[:, j % 2, t * P:(t + 1) * P], ident[:])
                last.then_inc(ot_full, 1)

            def key_head(gp, s, first):
                g = 2 * gp + s
                u, j = ATT[0] + 2 + s + 2 * gp, ATT[1] + 4 + 2 * s + 4 * gp
                slot = (ATT[0] + s) % 2
                if not (first and s == 0):
                    pe.wait_ge(ol_done, NT * g)
                    pe.wait_ge(s_evac, NT * g)
                    pe.wait_ge(pa_evac, NT * g)
                    pe.wait_ge(pb_evac, NT * g)
                for t in range(2):
                    x_job(u, j + t, t, slot, range(t * KD, (t + 1) * KD), REAL, new_unit=(t == 0))
                if first and s == 0:
                    pe.wait_ge(v_ready, 1)
                    pe.wait_ge(hn_var, 2)
                for t in range(2):
                    head_sums(2 + 2 * g + t, REAL) if isinstance(g, int) else head_sums_reg(2 + 2 * g + t, t)
                pe.wait_ge(hn_ready, 4 + 2 * g + 2)
                pe.wait_ge(k_cur_ready, g + 1)
                n = NT * g
                scores(n, 0)
                scores(n + 1, 1)
                for j in range(NT):
                    if 1 <= j < NT - 1:
                        scores(n + j + 1, j + 1)
                    probs_t(n + j, j)
                    if j:
                        out_t(n + j - 1, j - 1)
                    values(n + j, j, g)
                out_t(n + NT - 1, NT - 1)

            def head_sums_reg(q, t):
                nh = REAL[1]
                pe.wait_ge(hn_sq, q + 1)
                for hf in range(2):
                    last = nc.tensor.matmul(ps[:, 4 + 2 * t + hf, 0:nh], pair_ones[:], (t_b, sq)[t][:, hf * nh:(hf + 1) * nh], start=True, stop=True)
                last.then_inc(hn_sum, 1)

            pe.wait_ge(v_ready, 1)
            for s in range(2):
                key_head(0, s, True)
            with pe.Fori(1, NKV // 2) as gp:
                for s in range(2):
                    key_head(gp, s, False)

            project(*WO, REAL, ([(ol_done, NT * NKV)], (ol_done, NT * NKV)))
            ffn(3, REAL)
            for d in range(KD):
                pe.wait_ge(tile_evac, FF[3][1] + FJ - KD + d + 1)
                wait(pe, fin_evac, d - 3)
                for t in range(NT):
                    last = nc.tensor.transpose(ps[:, 4 + d % 4, t * P:(t + 1) * P], h[:, d, META + t * P:META + (t + 1) * P], ident[:])
                last.then_inc(fin_full, 1)

        @block.scalar
        def _(act):
            def split_high(c, i, jobs):
                act.wait_ge(raw_landed[c % 2], 32 * (c // 2 + 1) + 32 * i)
                wait(act, tile_full, jobs)
                nc.scalar.activation(wh[:, c % 2, :], raw[:, c % 2, :], ACT.Copy).then_inc(wh_ready, 1)

            def norm_input(m, d, col, evacuated):
                c0, nh = col
                cols = slice(c0, c0 + 2 * nh)
                act.wait_ge(*evacuated)
                nc.scalar.activation(sq[:, cols], h[:, d, cols], ACT.Square).then_inc(sq_done, 1)
                nc.scalar.activation(xh[:, d, cols], h[:, d, cols], ACT.Copy,
                                     scale=vec[:, GAIN[m] + d:GAIN[m] + d + 1] if isinstance(d, int) else vec[:, bass.ds(d + GAIN[m], 1)]).then_inc(xh_done, 1)

            def root_mean(m, col):
                cols = slice(col[0], col[0] + 2 * col[1])
                act.wait_ge(var_ready, m + 1)
                nc.scalar.activation(sq[:, cols], sq[:, cols], ACT.Sqrt).then_inc(sd_ready, 1)

            def ffn(n, col):
                m = FFNORM[n]
                u0, j0 = FF[n]
                cols = slice(col[0], col[0] + 2 * col[1])
                done = 0
                for part, nf in enumerate(PART):
                    def gate_up(i, first=False):
                        for s in range(2):
                            j, k = j0 + 2 * s + 4 * i, done + s + 2 * i
                            split_high(u0 + s + 1, i, j)
                            if first and s == 0:
                                root_mean(m, col)
                            act.wait_ge(tile_evac, j + 1)
                            nc.scalar.activation(t_b[:, cols], t_a[:, cols], ACT.Silu).then_inc(silu_done[n], 1)
                            act.wait_ge(gated[n], k + 1)
                            nc.scalar.activation(act_h[:, s + 2 * i, cols], t_c[:, cols], ACT.Copy).then_inc(act_h_done[n], 1)

                    gate_up(0, part == 0)
                    with act.Fori(1, nf // 2) as i:
                        gate_up(i)
                    u0 += nf
                    j0 += 2 * nf
                    done += nf

                    def down(i, last=False):
                        for s in range(2):
                            if not (last and s == 1):
                                split_high(u0 + s + 1, i, j0 + s + 2 * i)
                            if part == 1 and n < 3:
                                norm_input(m + 1, s + 2 * i, col, (tile_evac, j0 + s + 2 * i + 1))

                    if part == 1 and n == 3:
                        with act.Fori(0, KD // 2 - 1) as i:
                            down(i)
                        down(KD // 2 - 1, True)
                    else:
                        with act.Fori(0, KD // 2) as i:
                            down(i)
                    u0 += KD
                    j0 += KD

            for d in range(KD):
                norm_input(0, d, ALL, (init_evac, d + 2))
            split_high(0, 0, 0)
            ffn(0, ALL)

            X = ps[:, 4:6, :].rearrange("p b n -> p (b n)")

            def gelu(i):
                act.wait_ge(xf, 4 * i + 4)
                nc.scalar.activation(yc[0:NCH].rearrange("c (t g h) -> c g t h", t=T, g=GT),
                                     X[0:NCH, :].rearrange("c (g t h) -> c g t h", t=T, g=GT), ACT.Gelu_apprx_tanh).then_inc(xe, 1)

            def y_high(i):
                act.wait_ge(ye, 4 * i + 4)
                nc.scalar.activation(act_h[:, 2 * KC + i, :], y_t, ACT.Copy).then_inc(yth_done, 1)

            def mixer(i, first):
                u, j = MIX[0] + 2 * i, MIX[1] + 4 * i
                split_high(MIX[0] + 1, i, j)
                if first:
                    root_mean(1, ALL)
                else:
                    gelu(i - 1)
                act.wait_ge(xf, 4 * i + 1)
                nc.scalar.activation(uc4[0:NCH].rearrange("c g (t h) -> c t g h", t=T),
                                     X[0:NCH, :].rearrange("c (t g h) -> c t g h", t=T, g=GT), ACT.Copy).then_inc(xe, 1)
                if not first:
                    y_high(i - 1)
                act.wait_ge(xf, 4 * i + 2)
                nc.scalar.activation(blt, X, ACT.Copy).then_inc(xe, 1)
                split_high(MIX[0] + 2, i, j + 2)
                act.wait_ge(dve_mix, 5 * i + 5)
                nc.scalar.activation(act_h[:, i, :], t_a[:], ACT.Copy).then_inc(yah_done, 1)

            mixer(0, True)
            with act.Fori(1, KC) as i:
                mixer(i, False)
            gelu(KC - 1)
            y_high(KC - 1)
            split_high(WOUT[0], 0, GLU[1])
            for k in range(KC):
                act.wait_ge(tile_full, GLU[1] + k + 1)
                nc.scalar.activation(halves(t_b, ALL), ps[:, 2 * (k % 2):2 * (k % 2) + 2, 0:ALL[1]], ACT.Sigmoid,
                                     bias=vec[:, V_GLUB + k:V_GLUB + k + 1]).then_inc(tile_evac, 1)
                act.wait_ge(yb_prod, k + 1)
                nc.scalar.activation(act_h[:, KC + k, :], t_a[:], ACT.Copy).then_inc(ybh_done, 1)

            def project(u0, j0, col, m):
                with act.Fori(0, KD // 4) as i:
                    for s in range(2):
                        split_high(u0 + s + 1, i, j0 + 2 * s + 4 * i)
                        for n in range(2):
                            norm_input(m, 2 * s + n + 4 * i, col, (tile_evac, j0 + 2 * s + n + 4 * i + 1))

            project(*WOUT, ALL, 2)
            ffn(1, ALL)
            ffn(2, ALL)

            def head_square(q, t, src, col):
                w = 2 * col[1]
                nc.scalar.activation((t_b, sq)[t][:, 0:w], src[:, 0:w], ACT.Square).then_inc(hn_sq, 1)

            def head_root(q, t, col):
                w = 2 * col[1]
                act.wait_ge(hn_var, q + 1)
                nc.scalar.activation((t_b, sq)[t][:, 0:w], (t_b, sq)[t][:, 0:w], ACT.Sqrt).then_inc(hn_sd, 1)

            u0, j0 = ATT
            split_high(u0 + 1, 0, j0)
            root_mean(4, ALL)
            for t in range(2):
                act.wait_ge(tile_evac, j0 + t + 1)
                if t == 1:
                    act.wait_ge(r_ready, 5)
                head_square(t, t, (t_a, t_c)[t], ALL)
            for t in range(2):
                head_root(t, t, ALL)
            split_high(u0 + 2, 0, j0 + 2)

            def exps(n, j):
                act.wait_ge(nm_ready, n + 1)
                st = stat[:, j % 2]
                for k in range(QP):
                    p = s_all[:, j % 2, k * KEYS:(k + 1) * KEYS]
                    last = nc.scalar.activation(p, p, ACT.Exp, bias=st[:, 2, k:k + 1], accum_out=st[:, 4, k:k + 1])
                last.then_inc(p_ready, 1)

            def sink_exp(n, j, steps):
                act.wait_ge(at_step, steps)
                st = stat[:, j % 2]
                nc.scalar.activation(st[:, 5, 0:QP], st[:, 3, 0:QP], ACT.Exp).then_inc(es_ready, 1)

            def probs_b(n, j):
                act.wait_ge(pt_full, n + 1)
                nc.scalar.activation(p_b[0:KB, :], ps[0:KB, 7, :], ACT.Copy).then_inc(pb_evac, 1)

            def out_high(n, j, g):
                act.wait_ge(ot_full, n + 1)
                nc.scalar.activation(act_h[:, bass.ds(2 * g, 2), META + j * P:META + (j + 1) * P],
                                     ps[:, j % 2, 0:2 * P].rearrange("p (t n) -> p t n", t=2), ACT.Copy).then_inc(oh_done, 1)

            def key_head(gp, s):
                g = 2 * gp + s
                u, j = ATT[0] + 2 + s + 2 * gp, ATT[1] + 4 + 2 * s + 4 * gp
                split_high(ATT[0] + 3 + s, gp, j)
                for t in range(2):
                    act.wait_ge(tile_evac, j + t + 1)
                    head_square(2 + 2 * g + t, t, (t_a, t_c)[t], REAL)
                for t in range(2):
                    head_root(2 + 2 * g + t, t, REAL)
                n = NT * g
                for j in range(NT):
                    if j == 0:
                        exps(n, 0)
                        sink_exp(n, 0, 21 * g + 4)
                    if j + 1 < NT:
                        exps(n + j + 1, j + 1)
                        sink_exp(n + j + 1, j + 1, 21 * g + STAT_STEP[j + 1])
                    probs_b(n + j, j)
                    if j:
                        out_high(n + j - 1, j - 1, g)
                out_high(n + NT - 1, NT - 1, g)

            act.wait_ge(rtok_full, 1)
            with act.Fori(0, NKV // 2) as gp:
                for s in range(2):
                    key_head(gp, s)
            project(*WO, REAL, 5)
            ffn(3, REAL)
            for d in range(1, KD, 2):
                act.wait_ge(fin_full, d + 1)
                act.wait_ge(fin_evac, d)
                nc.scalar.activation(arena[:, d * 512:(d + 1) * 512], ps[:, 4 + d % 4, :], ACT.Copy).then_inc(fin_evac, 1)

        @block.vector
        def _(dve):
            v = nc.vector

            def split_low(c, i):
                dve.wait_ge(wh_ready, c + 2 * i + 1)
                v.tensor_tensor(wl[:, c % 2, :], raw[:, c % 2, :], wh[:, c % 2, :].bitcast(F32), ALU.subtract).then_inc(wl_ready, 1)

            def tile(pair, col):
                return ps[:, 2 * pair:2 * pair + 2, 0:col[1]]

            def clear_sums(m):
                v.memset(ssq[:], 0.0).then_inc(ssq_step, 1)

            def norm_input(m, d, col):
                c0, nh = col
                cols = slice(c0, c0 + 2 * nh)
                dve.wait_ge(sq_done, KD * m + d + 1)
                dve.wait_ge(ssq_step, (KD + 1) * m + d + 1)
                v.tensor_tensor(ssq[:, cols], ssq[:, cols], sq[:, cols], ALU.add).then_inc(ssq_step, 1)
                dve.wait_ge(xh_done, KD * m + d + 1)
                gain = vec[:, GAIN[m] + d:GAIN[m] + d + 1] if isinstance(d, int) else vec[:, bass.ds(d + GAIN[m], 1)]
                v.scalar_tensor_tensor(xl[:, d, cols], h[:, d, cols], gain, xh[:, d, cols].bitcast(F32), ALU.mult, ALU.subtract).then_inc(x_ready, 1)

            def rms(m, col):
                cols = slice(col[0], col[0] + 2 * col[1])
                dve.wait_ge(ssum_full, m + 1)
                v.tensor_scalar(halves(sq, col), ps[:, 4:6, 0:col[1]], 1.0 / DM, EPS, ALU.mult, ALU.add).then_inc(var_ready, 1)
                dve.wait_ge(sd_ready, m + 1)
                v.reciprocal(r[:, cols], sq[:, cols]).then_inc(r_ready, 1)
                dve.wait_ge(r_ready, m + 1)

            def residual(d, j, pair, scale, m, col):
                dve.wait_ge(tile_full, j + 1)
                hd = halves(h[:, d, :], col)
                v.scalar_tensor_tensor(hd, tile(pair, col), scale, hd, ALU.mult, ALU.add).then_inc(tile_evac, 1)
                if m is not None:
                    norm_input(m, d, col)

            def ffn(n, col):
                m = FFNORM[n]
                u0, j0 = FF[n]
                cols = slice(col[0], col[0] + 2 * col[1])
                done = 0
                for part, nf in enumerate(PART):
                    def gate_up(i, first=False):
                        for s in range(2):
                            j, k = j0 + 2 * s + 4 * i, done + s + 2 * i
                            split_low(u0 + s + 1, i)
                            if first and s == 0:
                                rms(m, col)
                            dve.wait_ge(tile_full, j + 1)
                            v.tensor_tensor(halves(t_a, col), tile(0, col), halves(r, col), ALU.mult).then_inc(tile_evac, 1)
                            dve.wait_ge(tile_full, j + 2)
                            wait(dve, act_ready[n], k)
                            v.tensor_tensor(halves(t_c, col), tile(1, col), halves(r, col), ALU.mult).then_inc(tile_evac, 1)
                            dve.wait_ge(tile_evac, j + 2)
                            dve.wait_ge(silu_done[n], k + 1)
                            v.tensor_tensor(t_c[:, cols], t_c[:, cols], t_b[:, cols], ALU.mult).then_inc(gated[n], 1)
                            dve.wait_ge(act_h_done[n], k + 1)
                            v.tensor_tensor(act_l[:, s + 2 * i, cols], t_c[:, cols], act_h[:, s + 2 * i, cols].bitcast(F32), ALU.subtract).then_inc(act_ready[n], 1)

                    gate_up(0, part == 0)
                    with dve.Fori(1, nf // 2) as i:
                        gate_up(i)
                    u0 += nf
                    j0 += 2 * nf
                    done += nf
                    more = m + 1 if part == 1 and n < 3 else None
                    if more is not None:
                        clear_sums(more)

                    def down(i, last=False):
                        for s in range(2):
                            if not (last and s == 1):
                                split_low(u0 + s + 1, i)
                            residual(s + 2 * i, j0 + s + 2 * i, s, 0.5, more, col)

                    if part == 1 and n == 3:
                        with dve.Fori(0, KD // 2 - 1) as i:
                            down(i)
                        down(KD // 2 - 1, True)
                    else:
                        with dve.Fori(0, KD // 2) as i:
                            down(i)
                    u0 += KD
                    j0 += KD

            X = ps[:, 4:6, :].rearrange("p b n -> p (b n)")
            dve.wait_ge(init_full, 1)
            v.tensor_copy(vec[:], X[:, 0:NV])
            v.tensor_copy(small[:, 1, :], X[:, P:P + G])
            v.tensor_copy(small[:, 2, :], X[:, 2 * P:2 * P + G]).then_inc(init_evac, 1)
            dve.wait_ge(init_evac, 1)
            v.tensor_scalar(vec[:, V_QN:V_QN + 1], vec[:, V_QN:V_QN + 1], float(HD) ** -0.5, None, ALU.mult)
            clear_sums(0)
            for d in range(KD):
                bank = 6 if d % 2 == 0 else 4
                dve.wait_ge(init_full, d + 2)
                v.tensor_copy(h[:, d, META:L], ps[:, bank, :])
                v.tensor_copy(h[:, d, 0:META], ps[:, bank + 1, 0:META]).then_inc(init_evac, 1)
                norm_input(0, d, ALL)
            dve.wait_ge(init_full, KD + 2)
            v.tensor_copy(c4, ps[:, 6, :])
            v.tensor_copy(c2, ps[:, 7, :]).then_inc(init_evac, 1)
            split_low(0, 0)
            ffn(0, ALL)

            def step_mix(ins, n):
                ins.then_inc(dve_mix, 1)
                dve.wait_ge(dve_mix, n)

            def states(i):
                wait(dve, xf, 4 * i)
                four = lambda x: x.rearrange("p (b g c) -> p b g c", b=2, g=4)
                src = lambda b: ps[:, b:b + 2, 0:4 * NCH].rearrange("p b (g c) -> p b g c", g=4)[:, :, :, 0:NCH - 1]
                dve.wait_ge(tab_landed, 16 * (i + 1))
                dve.wait_ge(xf, 4 * i + 3)
                v.tensor_tensor(four(sq[:])[:, :, :, 1:NCH], src(4), four(cos_t)[:, :, :, 1:NCH], ALU.mult).then_inc(xe, 1)
                dve.wait_ge(yf, 4 * i + 3)
                v.tensor_tensor(four(zs)[:, :, :, 1:NCH], src(6), four(sin_t)[:, :, :, 1:NCH], ALU.mult).then_inc(ye, 1)
                dve.wait_ge(xe, 4 * i + 3)
                dve.wait_ge(ye, 4 * i + 3)
                v.tensor_tensor(z_g[:, :, 1:NCH], sq[:].rearrange("p (g c) -> p g c", g=GT)[:, :, 1:NCH], zs_g[:, :, 1:NCH], ALU.add).then_inc(z_step, 1)
                dve.wait_ge(z_step, 2 * i + 1)
                v.tensor_tensor_scan(zs, rho_t, z, 0.0, ALU.mult, ALU.add).then_inc(z_step, 1)
                dve.wait_ge(z_step, 2 * i + 2)
                v.tensor_tensor(z, zs, cos_t, ALU.mult).then_inc(z_ready, 1)
                v.tensor_tensor(zs, zs, sin_t, ALU.mult).then_inc(z_ready, 1)

            def y_low(i):
                dve.wait_ge(yf, 4 * i + 4)
                wait(dve, yth_done, i)
                v.tensor_copy(y_t.rearrange("p (c b t) -> p b t c", b=2, t=4),
                              ps[:, 6:8, 0:4 * NCH].rearrange("p b (t c) -> p b t c", t=4)).then_inc(ye, 1)
                dve.wait_ge(yth_done, i + 1)
                v.tensor_tensor(act_l[:, 2 * KC + i, :], y_t, act_h[:, 2 * KC + i, :].bitcast(F32), ALU.subtract).then_inc(yt_ready, 1)

            def mixer(i, first):
                u, j = MIX[0] + 2 * i, MIX[1] + 4 * i
                if first:
                    dve.wait_ge(prep, count["mix_zeroed"])
                else:
                    states(i - 1)
                split_low(MIX[0] + 1, i)
                if first:
                    rms(1, ALL)
                dve.wait_ge(tile_full, j + 1)
                v.tensor_tensor(halves(u_t, ALL), tile(0, ALL), halves(r, ALL), ALU.mult).then_inc(tile_evac, 1)
                dve.wait_ge(tile_full, j + 2)
                v.tensor_tensor(halves(t_b, ALL), tile(1, ALL), halves(r, ALL), ALU.mult).then_inc(tile_evac, 1)
                if not first:
                    y_low(i - 1)
                dve.wait_ge(tile_full, j + 3)
                v.tensor_tensor(halves(t_a, ALL), tile(0, ALL), halves(r, ALL), ALU.mult).then_inc(tile_evac, 1)
                dve.wait_ge(tile_evac, j + 3)
                step_mix(v.tensor_tensor(hc[:, 2:L + 2], t_a[:], t_b[:], ALU.mult), 5 * i + 1)
                w = lambda k: (vec[:, V_CONV + k * KC + i:V_CONV + k * KC + i + 1] if isinstance(i, int)
                               else vec[:, bass.ds(i + (V_CONV + k * KC), 1)])
                step_mix(v.tensor_scalar(t_c[:], hc[:, 0:L], w(0), None, ALU.mult), 5 * i + 2)
                for k in (1, 2):
                    step_mix(v.scalar_tensor_tensor(t_c[:], hc[:, k:L + k], w(k), t_c[:], ALU.mult, ALU.add), 5 * i + 2 + k)
                dve.wait_ge(yf, 4 * i + 1)
                v.tensor_copy(u_c.rearrange("p (b n) -> p b n", b=2), ps[:, 6:8, 0:4 * NCH]).then_inc(ye, 1)
                split_low(MIX[0] + 2, i)
                dve.wait_ge(tile_full, j + 4)
                v.tensor_tensor(halves(t_a, ALL), tile(1, ALL), halves(r, ALL), ALU.mult).then_inc(tile_evac, 1)
                dve.wait_ge(tile_evac, j + 4)
                v.tensor_tensor(t_a[:], t_a[:], t_c[:], ALU.mult).then_inc(dve_mix, 1)
                dve.wait_ge(yah_done, i + 1)
                v.tensor_tensor(act_l[:, i, :], t_a[:], act_h[:, i, :].bitcast(F32), ALU.subtract).then_inc(ya_ready, 1)
                dve.wait_ge(yf, 4 * i + 2)
                yk = ps[0:H, 6:8, :].rearrange("p b n -> p (b n)").rearrange("p (g n) -> p g n", g=GT)
                v.tensor_copy(krow[0:H, :, H:P], yk[:, :, H:P]).then_inc(krow_ready, 1)
                v.tensor_tensor(krow[0:H, :, 0:H], yk[:, :, 0:H], d16[:, bass.ds(i * GT, GT), :], ALU.add).then_inc(ye, 1)

            mixer(0, True)
            with dve.Fori(1, KC) as i:
                mixer(i, False)
            states(KC - 1)
            y_low(KC - 1)
            split_low(WOUT[0], 0)
            for k in range(KC):
                wait(dve, yb_prod, k)
                v.tensor_tensor(t_c[:], act_h[:, 2 * KC + k, :].bitcast(F32), act_l[:, 2 * KC + k, :].bitcast(F32), ALU.add).then_inc(dve_mix, 1)
                dve.wait_ge(dve_mix, 5 * KC + k + 1)
                dve.wait_ge(tile_evac, GLU[1] + k + 1)
                v.tensor_tensor(t_a[:], t_b[:], t_c[:], ALU.mult).then_inc(yb_prod, 1)
                dve.wait_ge(ybh_done, k + 1)
                v.tensor_tensor(act_l[:, KC + k, :], t_a[:], act_h[:, KC + k, :].bitcast(F32), ALU.subtract).then_inc(yb_ready, 1)

            def project(u0, j0, col, m):
                clear_sums(m)
                with dve.Fori(0, KD // 4) as i:
                    for s in range(2):
                        split_low(u0 + s + 1, i)
                        for n in range(2):
                            residual(2 * s + n + 4 * i, j0 + 2 * s + n + 4 * i, n, 1.0, m, col)

            project(*WOUT, ALL, 2)
            ffn(1, ALL)
            ffn(2, ALL)

            def head_norm(q, t, src, gain, outs, col, steps):
                w = 2 * col[1]
                buf = (t_b, sq)[t]
                dve.wait_ge(hn_sum, q + 1)
                v.tensor_scalar(halves(buf, (0, col[1])), ps[:, 4 + 2 * t:6 + 2 * t, 0:col[1]], 1.0 / HD, EPS, ALU.mult, ALU.add).then_inc(hn_var, 1)
                dve.wait_ge(hn_sd, q + 1)
                v.reciprocal(buf[:, 0:w], buf[:, 0:w]).then_inc(hn_step, 1)
                dve.wait_ge(hn_step, q + 1)
                for dst, c0, n in outs:
                    last = v.scalar_tensor_tensor(dst, src[:, c0:c0 + n], vec[:, gain:gain + 1], buf[:, c0:c0 + n], ALU.mult, ALU.mult)
                    last.then_inc(hn_ready, 1)

            u0, j0 = ATT
            split_low(u0 + 1, 0)
            rms(4, ALL)
            for t in range(2):
                dve.wait_ge(tile_full, j0 + t + 1)
                v.tensor_tensor(halves((t_a, t_c)[t], ALL), tile(t, ALL), halves(r, ALL), ALU.mult).then_inc(tile_evac, 1)
            dve.wait_ge(prep, count["att_consts"])
            for t in range(2):
                head_norm(t, t, (t_a, t_c)[t], V_KN, [(k_pre[:, t, CH:CH + SEQ], META, SEQ), (k_pre[:, t, CH + SEQ:KW], 0, META)], ALL, 0)
            split_low(u0 + 2, 0)
            dve.wait_ge(rtok_full, 1)
            v.tensor_copy(rtok[0:META, NT:NT + 1], ps[0:META, 5, NT:NT + 1]).then_inc(rtok_ready, 1)
            v.tensor_copy(rtok[:, 0:NT], ps[:, 5, 0:NT]).then_inc(rtok_ready, 1)
            dve.wait_ge(rtok_ready, 2)
            for t in range(NT):
                if t % 2 == 0:
                    dve.wait_ge(tile_full, j0 + 3 + t // 2)
                src = ps[:, t, 0:NKV * HD]
                v.tensor_scalar(va[CH:P, t, :], src[0:CH], rtok[0:CH, t:t + 1], None, ALU.mult)
                if t + 1 < NT:
                    v.tensor_scalar(va[0:CH, t + 1, :], src[CH:P], rtok[CH:P, t:t + 1], None, ALU.mult)
                last = v.tensor_scalar(vb[0:CH, t, :], src[CH:P], rtok[CH:P, t:t + 1], None, ALU.mult)
                if t % 2 == 1:
                    last.then_inc(tile_evac, 1)
            for t in range(NT):
                last = v.tensor_scalar(vb[CH:KB, t, :], ps[0:META, 4, 0:NKV * HD], rtok[0:META, NT:NT + 1], None, ALU.mult)
            last.then_inc(v_ready, 1)
            dve.wait_ge(sink_landed, 16)

            def softmax(n, j, g, at, first):
                st = stat[:, j % 2]
                dve.wait_ge(s_full, n + 1)
                if not (first and j < 2):
                    dve.wait_ge(pt_full, n - 1)
                by_bank = lambda x: x.rearrange("p (c b n) -> p b c n", b=2, c=2)
                v.tensor_tensor(by_bank(s_all[:, j % 2, :]), ps[:, 4:6, 0:2 * KEYS].rearrange("p b (c n) -> p b c n", c=2),
                                by_bank(bias), ALU.add).then_inc(s_evac, 1)
                dve.wait_ge(s_evac, n + 1)
                s4 = s_all[:, j % 2, :].rearrange("p (k n) -> p k n", k=QP)
                if j == 0:
                    v.memset(s4[:, :, 0:CH], -1e30).then_inc(at_step, 1)
                    at += 1
                    dve.wait_ge(at_step, at)
                v.tensor_reduce(st[:, 0, 0:QP], s4, AX_X, ALU.max).then_inc(at_step, 1)
                dve.wait_ge(at_step, at + 1)
                sinks = sink_t[:, g * QP:(g + 1) * QP] if isinstance(g, int) else sink_t[:, bass.ds(g * QP, QP)]
                v.tensor_tensor(st[:, 1, 0:QP], st[:, 0, 0:QP], sinks, ALU.max).then_inc(at_step, 1)
                dve.wait_ge(at_step, at + 2)
                v.tensor_scalar(st[:, 2, 0:QP], st[:, 1, 0:QP], -1.0, None, ALU.mult).then_inc(nm_ready, 1)
                dve.wait_ge(nm_ready, n + 1)
                v.tensor_tensor(st[:, 3, 0:QP], st[:, 2, 0:QP], sinks, ALU.add).then_inc(at_step, 1)
                return at + 3

            def probs_a(n, j):
                dve.wait_ge(pt_full, n + 1)
                v.tensor_copy(p_a, ps[:, 6, :]).then_inc(pa_evac, 1)

            def outputs(n, j, at):
                st = stat[:, j % 2]
                dve.wait_ge(es_ready, n + 1)
                v.tensor_tensor(st[:, 6, 0:QP], st[:, 4, 0:QP], st[:, 5, 0:QP], ALU.add).then_inc(at_step, 1)
                dve.wait_ge(at_step, at + 1)
                v.reciprocal(st[:, 7, 0:QP], st[:, 6, 0:QP]).then_inc(at_step, 1)
                dve.wait_ge(at_step, at + 2)
                dve.wait_ge(o_full, n + 1)
                v.tensor_tensor(o_all[:, j % 2, :].rearrange("p (k d) -> p k d", k=QP), ps[:, 2 + j % 2, 0:QP * HD].rearrange("p (k d) -> p k d", k=QP),
                                st[:, 7, 0:QP].unsqueeze(2).to_broadcast([P, QP, HD]), ALU.mult).then_inc(o_ready, 1)
                return at + 2

            def out_low(n, j, g):
                dve.wait_ge(oh_done, n + 1)
                cols = slice(META + j * P, META + (j + 1) * P)
                v.tensor_tensor(act_l[:, bass.ds(2 * g, 2), cols], ps[:, j % 2, 0:2 * P].rearrange("p (t n) -> p t n", t=2),
                                act_h[:, bass.ds(2 * g, 2), cols].bitcast(F32), ALU.subtract).then_inc(ol_done, 1)

            def key_head(gp, s, first):
                g = 2 * gp + s
                j = ATT[1] + 4 + 2 * s + 4 * gp
                split_low(ATT[0] + 3 + s, gp)
                v.tensor_scalar(bias, bias, 0.25, None, ALU.mult).then_inc(bias_ready, 1)
                for t in range(2):
                    dve.wait_ge(tile_full, j + t + 1)
                    v.tensor_tensor(halves((t_a, t_c)[t], (0, REAL[1])), tile(t, REAL), halves(r, REAL), ALU.mult).then_inc(tile_evac, 1)
                rows = slice(s * HD, (s + 1) * HD)
                dve.wait_ge(hn_ready, 4)
                for half in range(2):
                    src = k_pre[rows, gp, :] if isinstance(gp, int) else k_pre[rows, bass.ds(gp, 1), :].rearrange("p a n -> p (a n)")
                    last = v.tensor_copy(k_cur[half * HD:(half + 1) * HD, :], src)
                last.then_inc(k_cur_ready, 1)
                for t in range(2):
                    head_norm(2 + 2 * g + t, t, (t_a, t_c)[t], V_QN, [(q_hat[:, t, :], 0, SEQ)], REAL, 0)
                dve.wait_ge(bias_ready, g + 1)
                n, at = NT * g, 21 * g
                base = at
                at = softmax(n, 0, g, at, first and s == 0)
                for j in range(NT):
                    if j + 1 < NT and j != 0:
                        at = softmax(n + j + 1, j + 1, g, at, first and s == 0)
                    if j == 0:
                        at = softmax(n + 1, 1, g, at, first and s == 0)
                    probs_a(n + j, j)
                    if j:
                        out_low(n + j - 1, j - 1, g)
                    at = outputs(n + j, j, at)
                out_low(n + NT - 1, NT - 1, g)

            for s in range(2):
                key_head(0, s, True)
            with dve.Fori(1, NKV // 2) as gp:
                for s in range(2):
                    key_head(gp, s, False)
            project(*WO, REAL, 5)
            ffn(3, REAL)
            for d in range(0, KD, 2):
                dve.wait_ge(fin_full, d + 1)
                wait(dve, fin_evac, d)
                v.tensor_copy(arena[:, d * 512:(d + 1) * 512], ps[:, 4 + d % 4, :]).then_inc(fin_evac, 1)


_INS = ['x', 'meta_tokens', 'norm_ff1', 'ff1_w_gate', 'ff1_w_up', 'ff1_w_down', 'norm_mix', 'even_w_in', 'conv_w',
        'ssm_lambda_re', 'ssm_lambda_im', 'ssm_log_step', 'ssm_b_re', 'ssm_b_im', 'ssm_c_re', 'ssm_c_im', 'ssm_d',
        'glu_w', 'glu_b', 'even_w_out', 'attn_w_qkv', 'attn_q_norm', 'attn_k_norm', 'attn_sinks', 'attn_w_o',
        'norm_ff2', 'ff2_w_gate', 'ff2_w_up', 'ff2_w_down']


def kernel(**inputs):
    import numpy as _np
    import concourse.bacc as _bacc
    from concourse import mybir as _mybir
    from concourse.bass_utils import run_bass_kernel_spmd as _run

    nc = _bacc.Bacc("TRN2", target_bir_lowering=False, num_devices=1)
    arrays, args = {}, {}
    for name in _INS:
        arr = _np.ascontiguousarray(inputs[name])
        arrays[f"in_{name}"] = arr
        args[name] = nc.dram_tensor(f"in_{name}", arr.shape, _mybir.dt.from_np(arr.dtype), kind="ExternalInput").ap()
    out = nc.dram_tensor("out", arrays["in_x"].shape, _mybir.dt.float32, kind="ExternalOutput").ap()
    trunk_program(nc, args, out)
    res = _run(nc, [arrays], core_ids=[0])
    return res.results[0]["out"]
```

```python
import math
from contextlib import ExitStack

import concourse.bass as bass
from concourse import mybir

F32 = mybir.dt.float32
F32R = mybir.dt.float32r
I32 = mybir.dt.int32
ALU = mybir.AluOpType
ACT = mybir.ActivationFunctionType
AX_X = mybir.AxisListType.X

P = 128
ARENA = 11300
BLK = 16
UNITW = BLK * P


def trunk_program(nc, a, out, stop=None):
    SEQ, DM = a["x"].shape[1], a["x"].shape[2]
    META = a["meta_tokens"].shape[0]
    L = META + SEQ
    KD = DM // P
    DFF = a["ff1_w_gate"].shape[2]
    NF = DFF // P
    PART = [12, NF - 12]
    DC = a["conv_w"].shape[2]
    KC = DC // P
    G, ST = a["ssm_lambda_re"].shape[1:]
    H = a["ssm_b_re"].shape[3]
    T = P // H
    NCH = L // T
    GT = P // H
    NT = SEQ // P
    NH = a["attn_sinks"].shape[1]
    HD = a["attn_q_norm"].shape[1]
    NKV = (a["attn_w_qkv"].shape[2] // HD - NH) // 2
    QP = NH // NKV
    CH = 64
    BAND = P + CH
    KEYS = BAND + META
    KB = KEYS - P
    EPS = 1e-6
    QSTEPS = 14
    assert ST * 2 == P and T * H == P and NCH * T == L and NH * HD == DM and META % 16 == 0

    FU, FJ = NF + 2 * KD, 2 * NF + 2 * KD
    FF = [(0, 0)]
    MIX = (FU, FJ)
    GLU = (MIX[0] + 2 * KC, MIX[1] + 4 * KC)
    WOUT = (GLU[0] + 1, GLU[1] + KC)
    FF.append((WOUT[0] + KD // 2, WOUT[1] + KD))
    FF.append((FF[1][0] + FU, FF[1][1] + FJ))
    ATT = (FF[2][0] + FU, FF[2][1] + FJ)
    WO = (ATT[0] + 2 + NKV, ATT[1] + 4 + 2 * NKV)
    FF.append((WO[0] + KD // 2, WO[1] + KD))
    LAST_UNIT = FF[3][0] + FU - 1

    FFW = [(a["ff1_w_gate"], a["ff1_w_up"], a["ff1_w_down"], 0), (a["ff2_w_gate"], a["ff2_w_up"], a["ff2_w_down"], 0),
           (a["ff1_w_gate"], a["ff1_w_up"], a["ff1_w_down"], 1), (a["ff2_w_gate"], a["ff2_w_up"], a["ff2_w_down"], 1)]
    FFNORM = [0, 2, 3, 5]
    GAIN = [0, 2 * KD, 4 * KD, KD, 3 * KD, 5 * KD]
    ALL = (0, L // 2, 2)
    REAL = (META, SEQ, 1)
    V_CONV = 6 * KD
    V_GLUB = V_CONV + 3 * KC
    V_QN, V_KN, NV = V_GLUB + KC, V_GLUB + KC + 1, V_GLUB + KC + 2

    with ExitStack() as ctx:
        def sb(name, shape, dt=F32):
            return ctx.enter_context(nc.sbuf_tensor(name, shape, dt))

        def sem(name):
            return ctx.enter_context(nc.semaphore(name))

        h = sb("h", [P, KD, L])
        xh = sb("xh", [P, KD, L], F32R)
        xl = sb("xl", [P, KD, L], F32R)
        act_h = sb("act_h", [P, PART[0], L], F32R)
        act_l = sb("act_l", [P, PART[0], L], F32R)
        raw = sb("raw", [P, 2, UNITW])
        wh = sb("wh", [P, 2, UNITW], F32R)
        wl = sb("wl", [P, 2, UNITW], F32R)
        t_a = sb("t_a", [P, L])
        t_b = sb("t_b", [P, L])
        t_c = sb("t_c", [P, L])
        sq = sb("sq", [P, L])
        ssq = sb("ssq", [P, L])
        r = sb("r", [P, L])
        ident = sb("ident", [P, P])
        ones = sb("ones", [P, P])
        pair_ones = sb("pair_ones", [P, P])
        vec = sb("vec", [P, NV])
        sg = sb("sg", [P, 1])
        d16 = sb("d16", [H, G, H])
        arena = sb("arena", [P, ARENA])
        ps = ctx.enter_context(nc.psum_tensor("ps", [P, 8, 512], F32))
        tabs = nc.dram_tensor("ssm_tables", (KC, P, GT * (T + 1) * H + 2 * P * GT + 3 * GT * NCH), F32, kind="Internal").ap()

        def carve(sizes):
            at, got = 0, []
            for n in sizes:
                got.append(arena[:, at:at + n])
                at += n
            assert at <= ARENA, at
            return got

        (v_xs, v_meta, v_vec, v_lam, v_c4, v_c2, b4, b2, small_all, pw_all) = carve(
            [NT * DM, 2 * G * H, P, 2 * P, 4 * P, 4 * P, G * H, G * H, 24 * G, 5 * (T + 1) * G])
        c4, c2 = v_meta[:, 0:G * H], v_meta[:, G * H:2 * G * H]
        bb4, bb2 = v_c4, v_c2
        v_xs = v_xs.rearrange("p (t d) -> p t d", t=NT)
        v_lam = v_lam.rearrange("p (c n) -> p c n", c=2)
        v_c4 = v_c4.rearrange("p (t n) -> p t n", t=4)
        v_c2 = v_c2.rearrange("p (t n) -> p t n", t=4)
        assert DM <= 2 * G * H
        small = small_all.rearrange("p (n g) -> p n g", g=G)
        pw = pw_all.rearrange("p (n k g) -> p n k g", n=5, g=G)
        WCL = GT * (T + 1) * H
        piece = [arena[:, 0:WCL], arena[:, WCL:2 * WCL]]
        ptmp = arena[:, 2 * WCL:3 * WCL]
        assert 3 * WCL <= NT * DM

        WP = P * GT
        WC = GT * NCH
        WTAB = WCL + 2 * WP + 3 * WC
        (tab, u_t, hc, uc, u_c, blt, kloc, z, zs, y_t) = carve(
            [WTAB, L, L + 2, WP, WC, WP, WP, WC, WC, L])
        cl = tab[:, 0:WCL].rearrange("p (g n) -> p g n", g=GT)
        cl2 = tab[:, WCL:WCL + WP].rearrange("p (g n) -> p g n", g=GT)
        bl = tab[:, WCL + WP:WCL + 2 * WP].rearrange("p (g n) -> p g n", g=GT)
        krow = bl
        cos_t, sin_t, rho_t = (tab[:, WCL + 2 * WP + k * WC:WCL + 2 * WP + (k + 1) * WC] for k in range(3))
        uc4 = uc.rearrange("p (g n) -> p g n", g=GT)
        yc = uc
        u_g = u_c.rearrange("p (g c) -> p g c", g=GT)
        blt_g = blt.rearrange("p (g n) -> p g n", g=GT)
        kloc_g = kloc.rearrange("p (g n) -> p g n", g=GT)
        z_g = z.rearrange("p (g c) -> p g c", g=GT)
        zs_g = zs.rearrange("p (g c) -> p g c", g=GT)

        WIN = NT * KEYS
        (q_hat, k_win, k_cur, va, vb, bias, s_all, p_a, p_b, stat, rtok, rtok2, rq, nq, sink_t) = carve(
            [2 * 2 * SEQ, 2 * WIN, 2 * WIN, NT * 256, NT * 256, QP * KEYS, 2 * QP * KEYS, 512, 512, 2 * 8 * QP, 8, 8, 2 * 16, 2 * 16, NH])
        q_hat = q_hat.rearrange("p (b t n) -> p b t n", b=2, t=2)
        k_win = k_win.rearrange("p (t j n) -> p t j n", t=2, j=NT)
        k_cur = k_cur.rearrange("p (b n) -> p b n", b=2)
        va = va.rearrange("p (j n) -> p j n", j=NT)
        vb = vb.rearrange("p (j n) -> p j n", j=NT)
        s_all = s_all.rearrange("p (b n) -> p b n", b=2)
        stat = stat.rearrange("p (b k n) -> p b k n", b=2, k=8)
        rq = rq.rearrange("p (b n) -> p b n", b=2)
        nq = nq.rearrange("p (b n) -> p b n", b=2)

        raw_landed = [sem("raw_landed0"), sem("raw_landed1")]
        wh_ready, wl_ready = sem("wh_ready"), sem("wl_ready")
        tile_full, tile_evac = sem("tile_full"), sem("tile_evac")
        x_landed, vec_landed, par_landed, sink_landed = sem("x_landed"), sem("vec_landed"), sem("par_landed"), sem("sink_landed")
        consts = sem("consts")
        init_full, init_evac = sem("init_full"), sem("init_evac")
        silu_done = [sem(f"silu_done{n}") for n in range(4)]
        gated = [sem(f"gated{n}") for n in range(4)]
        act_h_done = [sem(f"act_h_done{n}") for n in range(4)]
        act_ready = [sem(f"act_ready{n}") for n in range(4)]
        sq_done, ssq_step, xh_done, x_ready = sem("sq_done"), sem("ssq_step"), sem("xh_done"), sem("x_ready")
        ssum_full, var_ready, sd_ready, r_ready = sem("ssum_full"), sem("var_ready"), sem("sd_ready"), sem("r_ready")
        prep = sem("prep")
        piece_out = [sem("piece_out0"), sem("piece_out1")]
        tab_landed, kloc_landed = sem("tab_landed"), [sem("kloc_zero"), sem("kloc_landed")]
        dve_mix = sem("dve_mix")
        xf, xe, yf, ye = sem("xbank_full"), sem("xbank_evac"), sem("ybank_full"), sem("ybank_evac")
        yah_done, ya_ready = sem("yah_done"), sem("ya_ready")
        z_step = sem("z_step")
        z_ready, yth_done, yt_ready = sem("z_ready"), sem("yth_done"), sem("yt_ready")
        krow_ready = sem("krow_ready")
        yb_prod, ybh_done, yb_ready = sem("yb_prod"), sem("ybh_done"), sem("yb_ready")
        hn_sq, hn_sum, hn_var, hn_sd, hn_ready = sem("hn_sq"), sem("hn_sum"), sem("hn_var"), sem("hn_sd"), sem("hn_ready")
        hn_step, qn_step, k_step = sem("hn_step"), sem("qn_step"), sem("k_step")
        rtok_full, rtok_ready, v_ready = sem("rtok_full"), sem("rtok_ready"), sem("v_ready")
        k_cur_ready, bias_ready = sem("k_cur_ready"), sem("bias_ready")
        pn_ready = sem("pn_ready")
        s_full, s_evac, at_step, nm_ready, p_ready, es_ready = sem("s_full"), sem("s_evac"), sem("at_step"), sem("nm_ready"), sem("p_ready"), sem("es_ready")
        pt_full, pa_evac, pb_evac, o_full = sem("pt_full"), sem("pa_evac"), sem("pb_evac"), sem("o_full")
        oh_done, ol_done = sem("oh_done"), sem("ol_done")
        fin_full, fin_evac, out_done = sem("fin_full"), sem("fin_evac"), sem("out_done")

        block = ctx.enter_context(nc.Block())
        count = {}

        STAT_STEP = [4, 7, 12, 17]
        STEPS_G = 1 + 5 * NT

        def wait(eng, s, v):
            if not isinstance(v, int) or v > 0:
                eng.wait_ge(s, v)

        def span(col):
            c0, nh, nb = col
            return slice(c0, c0 + nb * nh)

        def halves(ap, col):
            return ap[:, span(col)].rearrange("p (b n) -> p b n", b=col[2]) if col[2] > 1 else ap[:, span(col)]

        def banks(b, col):
            return ps[:, b:b + col[2], 0:col[1]] if col[2] > 1 else ps[:, b, 0:col[1]]

        @block.gpsimd
        def _(pool):
            g = nc.gpsimd
            made = [0]

            def const(ins):
                ins.then_inc(consts, 1)
                made[0] += 1
                pool.wait_ge(consts, made[0])

            const(g.memset(ident[:], 0.0))
            const(g.affine_select(out=ident[:], in_=ident[:], compare_op=ALU.not_equal, fill=1.0, base=0,
                                  pattern=[[-1, P]], channel_multiplier=1))
            const(g.memset(ones[:], 1.0))
            const(g.memset(pair_ones[:], 0.0))
            const(g.memset(pair_ones[0:HD, 0:HD], 1.0))
            const(g.memset(pair_ones[HD:P, HD:P], 1.0))
            const(g.memset(sg[0:ST, :], 1.0))
            const(g.memset(sg[ST:P, :], -1.0))
            assert made[0] == 8

            n_par = 0
            for half in range(2):
                rows = slice(half * ST, (half + 1) * ST)
                re, im = a["ssm_b_re"][0].rearrange("g p h -> p g h"), a["ssm_b_im"][0].rearrange("g p h -> p g h")
                for dst, src in ((b4, (re, im)[half]), (b2, (im, re)[half])):
                    pool.dma_start(dst[rows, :].rearrange("p (g h) -> p g h", g=G), src).then_inc(par_landed, 16)
                    n_par += 1
                cols = slice(half * ST, (half + 1) * ST)
                cre, cim = (a[n][0].rearrange("(t a) h p -> (a h) t p", t=4) for n in ("ssm_c_re", "ssm_c_im"))
                for dst, src in ((v_c4, (cre, cim)[half]), (v_c2, (cim, cre)[half])):
                    pool.dma_start(dst[:, :, cols], src).then_inc(par_landed, 16)
                    n_par += 1
            pool.dma_start(small[:, 0, :], a["ssm_log_step"].partition_broadcast(P)).then_inc(par_landed, 16)
            pool.dma_start(d16[:].rearrange("p g h -> p (g h)"), a["ssm_d"].partition_broadcast(H)).then_inc(par_landed, 16)
            assert n_par + 2 == 10

            steps = [0]

            def did(ins):
                ins.then_inc(prep, 1)
                steps[0] += 1
                pool.wait_ge(prep, steps[0])

            def tt(o, x, y, op):
                did(g.tensor_tensor(o, x, y, op))

            def ts(o, x, s1, op0, s2=None, op1=None):
                did(g.tensor_scalar(o, x, s1, s2, op0, op1) if op1 is not None else g.tensor_scalar(o, x, s1, None, op0))

            pool.wait_ge(par_landed, 160)
            pool.wait_ge(init_evac, 10)
            S = lambda k: small[:, k, :]
            (LOGST, LRE, LIM, STEP, T0, T1, T2, T3, AR, AI, TH, CQ, CW, SN, CS, MG, A8R, A8I, R8, KF, K1, K2, P1, P2) = range(24)
            tt(d16[:], d16[:], ident[0:H, 0:H].unsqueeze(1).to_broadcast([H, G, H]), ALU.mult)

            RND = 1.5 * 2.0 ** 23

            def exp_of(o, x):
                ts(S(T0), x, -180.0, ALU.max, 180.0, ALU.min)
                ts(S(KF), S(T0), 1.0 / math.log(2.0), ALU.mult)
                ts(S(KF), S(KF), RND, ALU.add)
                ts(S(KF), S(KF), -RND, ALU.add)
                ln2_hi = 0.693359375
                ln2_lo = math.log(2.0) - ln2_hi
                ts(S(T1), S(KF), -ln2_hi, ALU.mult)
                tt(S(T0), S(T0), S(T1), ALU.add)
                ts(S(T1), S(KF), -ln2_lo, ALU.mult)
                tt(S(T0), S(T0), S(T1), ALU.add)
                ts(S(T1), S(T0), 1.0 / 5040, ALU.mult, 1.0 / 720, ALU.add)
                for c in (1.0 / 120, 1.0 / 24, 1.0 / 6, 0.5, 1.0, 1.0):
                    tt(S(T1), S(T1), S(T0), ALU.mult)
                    ts(S(T1), S(T1), c, ALU.add)
                ts(S(K1), S(KF), 0.5, ALU.mult)
                ts(S(K1), S(K1), RND, ALU.add)
                ts(S(K1), S(K1), -RND, ALU.add)
                tt(S(K2), S(KF), S(K1), ALU.subtract)
                for k, p in ((K1, P1), (K2, P2)):
                    ts(S(k), S(k), -126.0, ALU.max, 127.0, ALU.min)
                    ts(S(k), S(k), 127.0, ALU.add)
                    did(g.tensor_scalar(S(p).bitcast(I32), S(k), 2.0 ** 23, None, ALU.mult))
                tt(S(T1), S(T1), S(P1), ALU.mult)
                tt(o, S(T1), S(P2), ALU.mult)

            exp_of(S(STEP), S(LOGST))
            tt(S(T3), S(LRE), S(STEP), ALU.mult)
            exp_of(S(MG), S(T3))
            tt(S(TH), S(LIM), S(STEP), ALU.mult)
            ts(S(KF), S(TH), 2.0 / math.pi, ALU.mult)
            ts(S(KF), S(KF), RND, ALU.add)
            ts(S(KF), S(KF), -RND, ALU.add)
            pi_1 = 1.5703125
            pi_2 = 4.837512969970703125e-4
            pi_3 = math.pi / 2 - pi_1 - pi_2
            for c in (pi_1, pi_2, pi_3):
                ts(S(T0), S(KF), -c, ALU.mult)
                tt(S(TH), S(TH), S(T0), ALU.add)
            tt(S(T0), S(TH), S(TH), ALU.mult)
            ts(S(SN), S(T0), 1.0 / 362880, ALU.mult, -1.0 / 5040, ALU.add)
            for c in (1.0 / 120, -1.0 / 6, 1.0):
                tt(S(SN), S(SN), S(T0), ALU.mult)
                ts(S(SN), S(SN), c, ALU.add)
            tt(S(SN), S(SN), S(TH), ALU.mult)
            ts(S(CS), S(T0), -1.0 / 3628800, ALU.mult, 1.0 / 40320, ALU.add)
            for c in (-1.0 / 720, 1.0 / 24, -0.5, 1.0):
                tt(S(CS), S(CS), S(T0), ALU.mult)
                ts(S(CS), S(CS), c, ALU.add)
            ts(S(T1), S(KF), 0.25, ALU.mult)
            ts(S(T1), S(T1), RND, ALU.add)
            ts(S(T1), S(T1), -RND, ALU.add)
            ts(S(T1), S(T1), -4.0, ALU.mult)
            tt(S(T1), S(T1), S(KF), ALU.add)
            ts(S(T2), S(T1), 0.0, ALU.max, 2.0, ALU.mult)
            tt(S(T2), S(T2), S(T1), ALU.subtract)
            ts(S(K1), S(T2), -1.0, ALU.mult, 1.0, ALU.add)
            ts(S(K2), S(T2), -1.0, ALU.mult, 2.0, ALU.add)
            tt(S(K2), S(K2), S(T1), ALU.mult)
            tt(S(T0), S(CS), S(K1), ALU.mult)
            tt(S(T1), S(SN), S(K2), ALU.mult)
            tt(S(T2), S(SN), S(K1), ALU.mult)
            tt(S(T3), S(CS), S(K2), ALU.mult)
            tt(S(CS), S(T0), S(T1), ALU.subtract)
            tt(S(SN), S(T2), S(T3), ALU.add)
            tt(S(AR), S(MG), S(CS), ALU.mult)
            tt(S(AI), S(MG), S(SN), ALU.mult)
            ts(S(T0), S(AR), -1.0, ALU.add)
            tt(S(T1), S(LRE), S(LRE), ALU.mult)
            tt(S(T2), S(LIM), S(LIM), ALU.mult)
            tt(S(T3), S(T1), S(T2), ALU.add)
            did(g.memset(S(K1), -1.0))
            tt(S(T1), S(T3), S(K1), ALU.pow)
            tt(S(T2), S(T3), S(T1), ALU.mult)
            ts(S(T2), S(T2), -1.0, ALU.mult, 2.0, ALU.add)
            tt(S(T3), S(T1), S(T2), ALU.mult)
            tt(S(T1), S(T0), S(LRE), ALU.mult)
            tt(S(T2), S(AI), S(LIM), ALU.mult)
            tt(S(T1), S(T1), S(T2), ALU.add)
            tt(S(CQ), S(T1), S(T3), ALU.mult)
            tt(S(T1), S(AI), S(LRE), ALU.mult)
            tt(S(T2), S(T0), S(LIM), ALU.mult)
            tt(S(T1), S(T1), S(T2), ALU.subtract)
            tt(S(CW), S(T1), S(T3), ALU.mult)
            did(g.memset(pw[:, 0, 0, :], 1.0))
            did(g.memset(pw[:, 1, 0, :], 0.0))

            def cmul(o_r, o_i, x_r, x_i, y_r, y_i, t0, t1, t2, t3):
                tt(t0, x_r, y_r, ALU.mult)
                tt(t1, x_i, y_i, ALU.mult)
                tt(t2, x_r, y_i, ALU.mult)
                tt(t3, x_i, y_r, ALU.mult)
                tt(o_r, t0, t1, ALU.subtract)
                tt(o_i, t2, t3, ALU.add)

            for k in range(T):
                cmul(pw[:, 0, k + 1, :], pw[:, 1, k + 1, :], pw[:, 0, k, :], pw[:, 1, k, :], S(AR), S(AI), S(T0), S(T1), S(T2), S(T3))
            did(g.tensor_scalar(pw[:, 2, :, :], pw[:, 0, :, :], sg[:, 0:1], None, ALU.mult))
            did(g.tensor_scalar(pw[:, 3, :, :], pw[:, 1, :, :], sg[:, 0:1], None, ALU.mult))
            did(g.tensor_scalar(pw[:, 4, :, :], pw[:, 2, :, :], -1.0, None, ALU.mult))
            for k in range(int(math.log2(T))):
                cmul(S(CS), S(SN), S(CS), S(SN), S(CS), S(SN), S(T0), S(T1), S(T2), S(T3))
                tt(S(MG), S(MG), S(MG), ALU.mult)
            v3 = lambda t: t.rearrange("p (g h) -> p g h", g=G)
            bc = lambda x: x.unsqueeze(2).to_broadcast([P, G, H])
            did(g.tensor_scalar(S(T2), S(CW), sg[:, 0:1], None, ALU.mult))
            tmp5 = v3(ptmp[:, 0:G * H])
            tt(v3(bb4), v3(b4), bc(S(CQ)), ALU.mult)
            tt(tmp5, v3(b2), bc(S(T2)), ALU.mult)
            tt(v3(bb4), v3(bb4), tmp5, ALU.subtract)
            tt(v3(bb2), v3(b2), bc(S(CQ)), ALU.mult)
            tt(tmp5, v3(b4), bc(S(T2)), ALU.mult)
            tt(v3(bb2), v3(bb2), tmp5, ALU.add)

            n_piece = [0]

            def start_piece(width):
                n = n_piece[0]
                if n >= 2:
                    pool.wait_ge(piece_out[n % 2], 16 * (n // 2))
                return piece[n % 2][:, 0:width]

            def end_piece(ft, at, buf, width):
                n = n_piece[0]
                pool.dma_start(tabs[ft, :, at:at + width], buf).then_inc(piece_out[n % 2], 16)
                n_piece[0] += 1

            for ft in range(KC):
                gs = slice(ft * GT, (ft + 1) * GT)

                def table(row_a, x_a, row_b, x_b, lo, hi, at, rev=False):
                    n = hi - lo
                    w = GT * n * H
                    buf = start_piece(w)
                    o = buf.rearrange("p (g k h) -> p g k h", g=GT, k=n)
                    t = ptmp[:, 0:w].rearrange("p (g k h) -> p g k h", g=GT, k=n)
                    for k in range(n):
                        ko = n - 1 - k if rev else k
                        pk = lambda row: pw[:, row, lo + k, gs].unsqueeze(2).to_broadcast([P, GT, H])
                        tt(o[:, :, ko, :], v3(x_a)[:, gs, :], pk(row_a), ALU.mult)
                        tt(t[:, :, ko, :], v3(x_b)[:, gs, :], pk(row_b), ALU.mult)
                    tt(buf, buf, ptmp[:, 0:w], ALU.subtract)
                    end_piece(ft, at, buf, w)

                table(2, c4, 1, c2, 0, T + 1, 0)
                table(4, c2, 1, c4, 1, T + 1, WCL)
                table(0, bb4, 3, bb2, 0, T, WCL + WP, rev=True)
                cbuf = start_piece(WC)
                n0 = n_piece[0]
                n_piece[0] += 1
                sbuf_ = start_piece(WC)
                n_piece[0] = n0
                cv = cbuf.rearrange("p (g c) -> p g c", g=GT)
                sv = sbuf_.rearrange("p (g c) -> p g c", g=GT)
                did(g.memset(cv[:, :, 0:1], 1.0))
                did(g.memset(sv[:, :, 0:1], 0.0))
                did(g.tensor_copy(cv[:, :, 1:2], small[:, CS, gs].unsqueeze(2)))
                did(g.tensor_copy(sv[:, :, 1:2], small[:, SN, gs].unsqueeze(2)))
                did(g.tensor_copy(small[:, A8R, gs], small[:, CS, gs]))
                did(g.tensor_copy(small[:, A8I, gs], small[:, SN, gs]))
                k = 1
                while k < NCH - 1:
                    n = min(k, NCH - 1 - k)
                    br = small[:, A8R, gs].unsqueeze(2).to_broadcast([P, GT, n])
                    bi = small[:, A8I, gs].unsqueeze(2).to_broadcast([P, GT, n])
                    ta = ptmp[:, 0:GT * n].rearrange("p (g c) -> p g c", g=GT)
                    tb = ptmp[:, GT * 32:GT * 32 + GT * n].rearrange("p (g c) -> p g c", g=GT)
                    tt(ta, cv[:, :, 1:1 + n], br, ALU.mult)
                    tt(tb, sv[:, :, 1:1 + n], bi, ALU.mult)
                    tt(cv[:, :, k + 1:k + 1 + n], ta, tb, ALU.subtract)
                    tt(ta, cv[:, :, 1:1 + n], bi, ALU.mult)
                    tt(tb, sv[:, :, 1:1 + n], br, ALU.mult)
                    tt(sv[:, :, k + 1:k + 1 + n], ta, tb, ALU.add)
                    did(g.tensor_copy(small[:, A8R, gs], cv[:, :, 2 * k if 2 * k < NCH else 1]))
                    did(g.tensor_copy(small[:, A8I, gs], sv[:, :, 2 * k if 2 * k < NCH else 1]))
                    k += n
                did(g.tensor_scalar(sbuf_, sbuf_, sg[:, 0:1], None, ALU.mult))
                end_piece(ft, WCL + 2 * WP, cbuf, WC)
                end_piece(ft, WCL + 2 * WP + WC, sbuf_, WC)
                rbuf = start_piece(WC)
                rv = rbuf.rearrange("p (g c) -> p g c", g=GT)
                did(g.tensor_copy(rv, small[:, MG, gs].unsqueeze(2).to_broadcast([P, GT, NCH])))
                did(g.memset(rv[:, :, 0:1], 0.0))
                end_piece(ft, WCL + 2 * WP + 2 * WC, rbuf, WC)
            n = n_piece[0]
            pool.wait_ge(piece_out[0], 16 * ((n + 1) // 2))
            pool.wait_ge(piece_out[1], 16 * (n // 2))

            did(g.memset(kloc, 0.0))
            did(g.memset(z_g[:, :, 0:1], 0.0))
            did(g.memset(hc[:, 0:2], 0.0))
            count['mix_zeroed'] = steps[0]
            for i in range(KC):
                if i:
                    pool.wait_ge(xf, 4 * i)
                pool.dma_start(tab, tabs[i]).then_inc(tab_landed, 16)
                pool.wait_ge(krow_ready, i + 1)
                pool.wait_ge(ye, 4 * i + 2)
                for t in range(T):
                    pool.dma_start(kloc_g[t * H:(t + 1) * H, :, t * H:P], krow[0:H, :, 0:P - t * H]).then_inc(kloc_landed[1], 16)
                pool.wait_ge(kloc_landed[1], 16 * T * (i + 1))

            pool.wait_ge(yb_ready, KC)
            pool.dma_start(sink_t, a["attn_sinks"].partition_broadcast(P)).then_inc(sink_landed, 16)
            d0 = k_cur[:, 0, 0:KEYS]
            did(g.iota(d0[:, 0:BAND], pattern=[[-1, BAND]], base=CH, channel_multiplier=1, allow_small_or_imprecise_dtypes=True))
            d1 = k_cur[:, 0, KEYS:KEYS + BAND]
            ts(d1, d0[:, 0:BAND], 0.0, ALU.max, 2.0, ALU.mult)
            tt(d0[:, 0:BAND], d1, d0[:, 0:BAND], ALU.subtract)
            did(g.memset(d0[0:CH, P:BAND], 1e36))
            did(g.memset(d0[CH:P, 0:CH], 1e36))
            did(g.memset(d0[:, BAND:KEYS], 0.0))
            for k in range(QP):
                ts(bias[:, k * KEYS:(k + 1) * KEYS], d0, -(2.0 ** (-8.0 * (k + 1) / NH)), ALU.mult)
            did(g.memset(k_win[:, :, 0, 0:CH], 0.0))
            did(g.memset(va[0:CH, 0, :], 0.0))
            count['att_consts'] = steps[0]

        @block.sync
        def _(sp):
            def load_unit(c, i, sources):
                wait(sp, wl_ready, c - 1 + 2 * i)
                for src, b0, nk in sources:
                    m = src.shape[2]
                    sp.dma_start(raw[:, c % 2, b0 * P:b0 * P + nk * m].rearrange("p (k m) -> p k m", k=nk), src).then_inc(raw_landed[c % 2], 16)

            def by_rows(w):
                return w.rearrange("(k p) f -> p k f", p=P)

            def ffn_loads(n):
                wg, wu, wd, layer = FFW[n]
                u0 = FF[n][0]
                wg, wu, wd = by_rows(wg[layer]), by_rows(wu[layer]), by_rows(wd[layer])
                f0 = 0
                for nf in PART:
                    def gate_up(i):
                        for s in range(2):
                            cols = bass.ds((2 * i + s + f0) * P, P)
                            load_unit(u0 + s, i, [(wg[:, :, cols], 0, KD), (wu[:, :, cols], KD, KD)])

                    def down(i):
                        for s in range(2):
                            cols = bass.ds((2 * i + s) * P, P)
                            load_unit(u0 + nf + s, i, [(wd[:, f0:f0 + nf // 2, cols], 0, nf // 2), (wd[:, f0 + nf // 2:f0 + nf, cols], nf // 2, nf // 2)])

                    gate_up(0)
                    with sp.Fori(1, nf // 2) as i:
                        gate_up(i)
                    with sp.Fori(0, KD // 2) as i:
                        down(i)
                    u0 += nf + KD
                    f0 += nf

            sp.dma_start(v_vec[0:2 * KD, :], a["norm_ff1"].rearrange("l (k p) -> (l k) p", p=P)).then_inc(vec_landed, 16)
            sp.dma_start(v_vec[2 * KD:4 * KD, :], a["norm_mix"].rearrange("l (k p) -> (l k) p", p=P)).then_inc(vec_landed, 16)
            sp.dma_start(v_vec[4 * KD:6 * KD, :], a["norm_ff2"].rearrange("l (k p) -> (l k) p", p=P)).then_inc(vec_landed, 16)
            sp.dma_start(v_vec[V_CONV:V_GLUB, :], a["conv_w"].rearrange("l w (k p) -> (l w k) p", p=P)).then_inc(vec_landed, 16)
            sp.dma_start(v_vec[V_GLUB:V_QN, :], a["glu_b"].rearrange("l (k p) -> (l k) p", p=P)).then_inc(vec_landed, 16)
            for half in range(2):
                sp.dma_start(v_vec[V_QN:V_QN + 1, half * HD:(half + 1) * HD], a["attn_q_norm"]).then_inc(vec_landed, 16)
                sp.dma_start(v_vec[V_KN:V_KN + 1, half * HD:(half + 1) * HD], a["attn_k_norm"]).then_inc(vec_landed, 16)
                sp.dma_start(v_lam[0:G, 0, half * ST:(half + 1) * ST], a["ssm_lambda_re"][0]).then_inc(vec_landed, 16)
                sp.dma_start(v_lam[0:G, 1, half * ST:(half + 1) * ST], a["ssm_lambda_im"][0]).then_inc(vec_landed, 16)
            sp.dma_start(v_meta[0:META, :], a["meta_tokens"]).then_inc(x_landed, 16)
            sp.dma_start(v_xs, a["x"][0].rearrange("(t p) d -> p t d", p=P)).then_inc(x_landed, 16)

            ffn_loads(0)
            w_in = by_rows(a["even_w_in"][0])
            for i in range(KC):
                for s, (c0, c1) in enumerate(((3 * DC, 2 * DC), (0, DC))):
                    load_unit(MIX[0] + s, i, [(w_in[:, :, c0 + i * P:c0 + (i + 1) * P], 0, KD), (w_in[:, :, c1 + i * P:c1 + (i + 1) * P], KD, KD)])
            glu = by_rows(a["glu_w"][0])
            load_unit(GLU[0], 0, [(glu[:, 0:KC // 2, :], 0, KC // 2), (glu[:, KC // 2:KC, :], KC // 2 * KC, KC // 2)])

            def two_column_tiles(w, u0, s, i):
                load_unit(u0 + s, i, [(w[:, :, bass.ds((2 * (2 * i + s) + n) * P, P)], n * KD, KD) for n in range(2)])

            w_out = by_rows(a["even_w_out"][0])
            with sp.Fori(0, KD // 4) as i:
                for s in range(2):
                    two_column_tiles(w_out, WOUT[0], s, i)
            ffn_loads(1)
            ffn_loads(2)
            w_qkv = by_rows(a["attn_w_qkv"][0])
            load_unit(ATT[0], 0, [(w_qkv[:, :, NH * HD + n * P:NH * HD + (n + 1) * P], n * KD, KD) for n in range(2)])
            v0 = (NH + NKV) * HD
            load_unit(ATT[0] + 1, 0, [(w_qkv[:, 0:KD // 2, v0:v0 + NKV * HD], 0, KD // 2), (w_qkv[:, KD // 2:KD, v0:v0 + NKV * HD], KD, KD // 2)])
            with sp.Fori(0, NKV // 2) as i:
                for s in range(2):
                    two_column_tiles(w_qkv, ATT[0] + 2, s, i)
            w_o = by_rows(a["attn_w_o"][0])
            with sp.Fori(0, KD // 4) as i:
                for s in range(2):
                    two_column_tiles(w_o, WO[0], s, i)
            ffn_loads(3)
            for d in range(KD):
                sp.wait_ge(fin_evac, d + 1)
                sp.dma_start(out[0, :, d * P:(d + 1) * P].rearrange("(t p) f -> p t f", p=P),
                             arena[:, d * 512:(d + 1) * 512].rearrange("p (t f) -> p t f", t=NT)).then_inc(out_done, 16)
            sp.wait_ge(out_done, 16 * KD)


        @block.tensor
        def _(pe):
            def mm3(pair, slot, blocks, x_h, x_l, k0, col, before_last=None):
                c0, nh, nb = col
                n = len(blocks)
                for k, b in enumerate(blocks):
                    if k == n - 1 and before_last:
                        before_last()
                    for q, (w, x) in enumerate(((wh, x_h), (wh, x_l), (wl, x_h))):
                        for hf in range(nb):
                            last = nc.tensor.matmul(ps[:, 2 * pair + hf, 0:nh], w[:, slot, b * P:(b + 1) * P],
                                                    x[:, k0 + k, c0 + hf * nh:c0 + (hf + 1) * nh],
                                                    start=(k == 0 and q == 0), stop=(k == n - 1 and q == 2))
                return last

            def token_sums(m, col):
                c0, nh, nb = col
                pe.wait_ge(ssq_step, (KD + 1) * (m + 1))
                for hf in range(nb):
                    last = nc.tensor.matmul(ps[:, 4 + hf, 0:nh], ones[:], ssq[:, c0 + hf * nh:c0 + (hf + 1) * nh], start=True, stop=True)
                last.then_inc(ssum_full, 1)

            def x_job(u, j, pair, slot, blocks, col, m=None, new_unit=True):
                if new_unit:
                    pe.wait_ge(wl_ready, u + 1)
                wait(pe, tile_evac, j - 1)
                before = None
                if m is not None:
                    pe.wait_ge(x_ready, KD * m + KD - 1)
                    before = lambda: pe.wait_ge(x_ready, KD * m + KD)
                mm3(pair, slot, blocks, xh, xl, 0, col, before).then_inc(tile_full, 1)

            def ffn(n, col):
                m = FFNORM[n]
                u0, j0 = FF[n]
                done = 0
                for part, nf in enumerate(PART):
                    def gate_up(i, m=None):
                        for s in range(2):
                            u, j = u0 + s + 2 * i, j0 + 2 * s + 4 * i
                            x_job(u, j, 0, (u0 + s) % 2, range(KD), col, m if s == 0 else None)
                            if m is not None and s == 0:
                                token_sums(m, col)
                            x_job(u, j + 1, 1, (u0 + s) % 2, range(KD, 2 * KD), col, new_unit=False)

                    gate_up(0, m if part == 0 else None)
                    with pe.Fori(1, nf // 2) as i:
                        gate_up(i)
                    u0 += nf
                    j0 += 2 * nf
                    done += nf
                    with pe.Fori(0, KD // 2) as i:
                        for s in range(2):
                            pe.wait_ge(wl_ready, u0 + s + 2 * i + 1)
                            pe.wait_ge(tile_evac, j0 + s + 2 * i - 1)
                            pe.wait_ge(act_ready[n], done - 1)
                            mm3(s, (u0 + s) % 2, range(nf), act_h, act_l, 0, col,
                                lambda: pe.wait_ge(act_ready[n], done)).then_inc(tile_full, 1)
                    u0 += KD
                    j0 += KD

            X = ps[:, 4:6, :].rearrange("p b n -> p (b n)")
            Y = ps[:, 6:8, :].rearrange("p b n -> p (b n)")

            pe.wait_ge(consts, 8)
            pe.wait_ge(vec_landed, 13 * 16)
            nc.tensor.transpose(X[:, 0:NV], v_vec[0:NV, :], ident[0:NV, 0:NV])
            for c in range(2):
                last = nc.tensor.transpose(X[:, P * (c + 1):P * (c + 1) + G], v_lam[0:G, c, :], ident[0:G, 0:G])
            last.then_inc(init_full, 1)
            pe.wait_ge(x_landed, 32)
            for d in range(KD):
                bank = 6 if d % 2 == 0 else 4
                wait(pe, init_evac, d)
                for t in range(NT):
                    nc.tensor.transpose(ps[:, bank, t * P:(t + 1) * P], v_xs[:, t, d * P:(d + 1) * P], ident[:])
                nc.tensor.transpose(ps[:, bank + 1, 0:META], v_meta[0:META, d * P:(d + 1) * P], ident[0:META, 0:META]).then_inc(init_full, 1)
            pe.wait_ge(init_evac, KD)
            pe.wait_ge(par_landed, 160)
            for b, v in ((6, v_c4), (7, v_c2)):
                for t in range(4):
                    last = nc.tensor.transpose(ps[:, b, t * P:(t + 1) * P], v[:, t, :], ident[:])
            last.then_inc(init_full, 1)

            ffn(0, ALL)

            def ssm_out(i):
                pe.wait_ge(z_ready, 2 * i + 2)
                pe.wait_ge(kloc_landed[1], 16 * T * (i + 1))
                pe.wait_ge(xe, 4 * i + 3)
                for g in range(GT):
                    o = X[0:NCH, g * P:(g + 1) * P]
                    nc.tensor.matmul(o, u_g[:, g, :], kloc_g[:, g, :], start=True, stop=False)
                    nc.tensor.matmul(o, z_g[:, g, :], cl[:, g, H:(T + 1) * H], start=False, stop=False)
                    last = nc.tensor.matmul(o, zs_g[:, g, :], cl2[:, g, :], start=False, stop=True)
                last.then_inc(xf, 1)

            def y_features(i):
                pe.wait_ge(xe, 4 * i + 4)
                pe.wait_ge(ye, 4 * i + 3)
                yv = yc[0:NCH].rearrange("c (t n) -> c t n", t=T)
                for t in range(T):
                    last = nc.tensor.transpose(ps[:, 6 + t // 4, (t % 4) * NCH:(t % 4 + 1) * NCH],
                                               yv[:, t, :], ident[0:NCH, 0:NCH])
                last.then_inc(yf, 1)

            def mixer(i, m=None):
                u, j = MIX[0] + 2 * i, MIX[1] + 4 * i
                s0 = MIX[0] % 2
                x_job(u, j, 0, s0, range(KD), ALL, m)
                if m is not None:
                    token_sums(m, ALL)
                else:
                    ssm_out(i - 1)
                x_job(u, j + 1, 1, s0, range(KD, 2 * KD), ALL, new_unit=False)
                if m is None:
                    y_features(i - 1)
                pe.wait_ge(tile_evac, j + 1)
                wait(pe, xe, 4 * i)
                if m is not None:
                    pe.wait_ge(var_ready, m + 1)
                uv = u_t.rearrange("p (c t) -> p c t", t=T)
                for t in range(T):
                    last = nc.tensor.transpose(X[0:NCH, t * P:(t + 1) * P], uv[:, :, t], ident[:])
                last.then_inc(xf, 1)
                x_job(u + 1, j + 2, 0, 1 - s0, range(KD), ALL)
                pe.wait_ge(xe, 4 * i + 1)
                wait(pe, ye, 4 * i)
                for g in range(GT):
                    last = nc.tensor.transpose(ps[:, 6 + g // 4, (g % 4) * NCH:(g % 4 + 1) * NCH],
                                               uc4[0:NCH, g, :], ident[0:NCH, 0:NCH])
                last.then_inc(yf, 1)
                pe.wait_ge(tab_landed, 16 * (i + 1))
                for g in range(GT):
                    last = nc.tensor.transpose(X[:, g * P:(g + 1) * P], bl[:, g, :], ident[:])
                last.then_inc(xf, 1)
                x_job(u + 1, j + 3, 1, 1 - s0, range(KD, 2 * KD), ALL, new_unit=False)
                pe.wait_ge(ye, 4 * i + 1)
                for g in range(GT):
                    last = nc.tensor.matmul(Y[0:H, g * P:(g + 1) * P], bl[:, g, (T - 1) * H:T * H], cl[:, g, 0:T * H], start=True, stop=True)
                last.then_inc(yf, 1)
                pe.wait_ge(xe, 4 * i + 2)
                for g in range(GT):
                    last = nc.tensor.matmul(ps[:, 4 + g // 4, (g % 4) * NCH:(g % 4 + 1) * NCH], blt_g[:, g, :], u_g[:, g, :], start=True, stop=True)
                last.then_inc(xf, 1)
                pe.wait_ge(ye, 4 * i + 2)
                for g in range(GT):
                    o = ps[:, 6 + g // 4, (g % 4) * NCH:(g % 4 + 1) * NCH]
                    nc.tensor.matmul(o[0:ST], blt_g[:, g, ST:P], u_g[:, g, :], start=True, stop=True)
                    last = nc.tensor.matmul(o[ST:P], blt_g[:, g, 0:ST], u_g[:, g, :], start=True, stop=True)
                last.then_inc(yf, 1)

            mixer(0, 1)
            with pe.Fori(1, KC) as i:
                mixer(i)
            ssm_out(KC - 1)
            y_features(KC - 1)
            pe.wait_ge(wl_ready, GLU[0] + 1)
            for k in range(KC):
                j = GLU[1] + k
                pe.wait_ge(tile_evac, j - 1)
                pe.wait_ge(yt_ready, KC)
                mm3(k % 2, GLU[0] % 2, range(k, KC * KC, KC), act_h, act_l, 2 * KC, ALL).then_inc(tile_full, 1)

            def project(u0, j0, col, inputs):
                with pe.Fori(0, KD // 4) as i:
                    for s in range(2):
                        for n in range(2):
                            if n == 0:
                                pe.wait_ge(wl_ready, u0 + s + 2 * i + 1)
                            pe.wait_ge(tile_evac, j0 + 2 * s + n + 4 * i - 1)
                            for sm, c in inputs[0]:
                                pe.wait_ge(sm, c)
                            mm3(n, (u0 + s) % 2, range(n * KD, (n + 1) * KD), act_h, act_l, 0, col,
                                lambda: pe.wait_ge(*inputs[1])).then_inc(tile_full, 1)

            project(*WOUT, ALL, ([(ya_ready, KC), (yb_ready, KC - 1)], (yb_ready, KC)))
            ffn(1, ALL)
            ffn(2, ALL)

            u0, j0 = ATT

            def key_sums(t):
                pe.wait_ge(hn_sq, t + 1)
                for hf in range(2):
                    last = nc.tensor.matmul(ps[:, 4 + 2 * t + hf, 0:ALL[1]], pair_ones[:], (t_b, sq)[t][:, hf * ALL[1]:(hf + 1) * ALL[1]], start=True, stop=True)
                last.then_inc(hn_sum, 1)

            x_job(u0, j0, 0, u0 % 2, range(KD), ALL, 4)
            token_sums(4, ALL)
            x_job(u0, j0 + 1, 1, u0 % 2, range(KD, 2 * KD), ALL, new_unit=False)
            pe.wait_ge(var_ready, 5)
            key_sums(0)
            slot = (u0 + 1) % 2
            pe.wait_ge(wl_ready, u0 + 2)
            VW = NKV * HD

            def v_tile(bank, c0):
                for k in range(KD):
                    for q, (x, w) in enumerate(((xh, wh), (xl, wh), (xh, wl))):
                        last = nc.tensor.matmul(ps[:, bank, 0:VW], x[:, k, c0:c0 + P], w[:, slot, k * VW:(k + 1) * VW],
                                                start=(k == 0 and q == 0), stop=(k == KD - 1 and q == 2))
                return last

            for pair in range(2):
                pe.wait_ge(tile_evac, j0 + 1 + pair)
                v_tile(2 * pair, META + 2 * pair * P)
                v_tile(2 * pair + 1, META + (2 * pair + 1) * P).then_inc(tile_full, 1)
                if pair == 0:
                    key_sums(1)
            pe.wait_ge(hn_var, 1)
            v_tile(4, 0)
            pe.wait_ge(r_ready, 5)
            for t in range(NT):
                nc.tensor.matmul(ps[:, 5, t:t + 1], r[0:1, META + t * P:META + (t + 1) * P], ones[0:1, 0:1], start=True, stop=True)
            nc.tensor.matmul(ps[0:META, 5, NT:NT + 1], r[0:1, 0:META], ones[0:1, 0:1], start=True, stop=True).then_inc(rtok_full, 1)

            def query_tile(g, t):
                if g:
                    pe.wait_ge(qn_step, QSTEPS * (g - 1) + 2)
                x_job(u0 + 2 + g, j0 + 4 + 2 * g + t, t, (u0 + g) % 2, range(t * KD, (t + 1) * KD), REAL, new_unit=(t == 0))

            def query_sums(g, t):
                pe.wait_ge(hn_sq, 2 + 2 * g + t + 1)
                pe.wait_ge(tile_evac, j0 + 4 + 2 * g + t + 1)
                for b in range(NT):
                    last = nc.tensor.matmul(ps[:, 2 * t, 2 * b:2 * b + 2], (t_b, sq)[t][:, b * P:(b + 1) * P], pair_ones[:, 0:P:HD], start=True, stop=True)
                last.then_inc(hn_sum, 1)

            def scores(g, j):
                n = NT * g + j
                if n:
                    pe.wait_ge(s_evac, n)
                for k in range(QP):
                    rows = slice((k % 2) * HD, (k % 2 + 1) * HD)
                    last = nc.tensor.matmul(ps[:, 4 + k % 2, (k // 2) * KEYS:(k // 2 + 1) * KEYS], q_hat[rows, g % 2, k // 2, j * P:(j + 1) * P],
                                            k_cur[rows, g % 2, j * KEYS:(j + 1) * KEYS], start=True, stop=True)
                last.then_inc(s_full, 1)

            def probs_t(g, j):
                n = NT * g + j
                pe.wait_ge(pn_ready, n + 1)
                if n:
                    pe.wait_ge(pa_evac, n)
                    pe.wait_ge(pb_evac, n)
                for k in range(QP):
                    p = s_all[:, j % 2, k * KEYS:(k + 1) * KEYS]
                    at = ((k % 2) * 2 + k // 2) * P
                    nc.tensor.transpose(ps[:, 6, at:at + P], p[:, 0:P], ident[:])
                    last = nc.tensor.transpose(ps[0:KB, 7, at:at + P], p[:, P:KEYS], ident[:])
                last.then_inc(pt_full, 1)

            def values(g, j):
                n = NT * g + j
                pe.wait_ge(pa_evac, n + 1)
                pe.wait_ge(pb_evac, n + 1)
                if n >= 2:
                    pe.wait_ge(ol_done, n - 1)
                cols = slice(g * HD, (g + 1) * HD)
                for hh in range(2):
                    o = ps[hh * HD:(hh + 1) * HD, 1 + 2 * (j % 2), 0:2 * P]
                    nc.tensor.matmul(o, va[:, j, cols], p_a[:, hh * 2 * P:(hh + 1) * 2 * P], start=True, stop=False)
                    last = nc.tensor.matmul(o, vb[0:KB, j, cols], p_b[0:KB, hh * 2 * P:(hh + 1) * 2 * P], start=False, stop=True)
                last.then_inc(o_full, 1)

            pe.wait_ge(tile_evac, j0 + 4)
            for t in range(2):
                query_tile(0, t)
            for t in range(2):
                query_sums(0, t)
            pe.wait_ge(v_ready, 1)
            for g in range(NKV):
                more = g + 1 < NKV
                pe.wait_ge(qn_step, QSTEPS * (g + 1))
                pe.wait_ge(k_cur_ready, g + 1)
                scores(g, 0)
                scores(g, 1)
                if more:
                    query_tile(g + 1, 0)
                probs_t(g, 0)
                scores(g, 2)
                values(g, 0)
                if more:
                    query_tile(g + 1, 1)
                probs_t(g, 1)
                scores(g, 3)
                values(g, 1)
                if more:
                    query_sums(g + 1, 0)
                    query_sums(g + 1, 1)
                probs_t(g, 2)
                values(g, 2)
                probs_t(g, 3)
                values(g, 3)

            project(*WO, REAL, ([(ol_done, NT * NKV)], (ol_done, NT * NKV)))
            ffn(3, REAL)
            for d in range(KD):
                pe.wait_ge(tile_evac, FF[3][1] + FJ - KD + d + 1)
                wait(pe, fin_evac, d - 3)
                for t in range(NT):
                    last = nc.tensor.transpose(ps[:, 4 + d % 4, t * P:(t + 1) * P], h[:, d, META + t * P:META + (t + 1) * P], ident[:])
                last.then_inc(fin_full, 1)

        @block.scalar
        def _(act):
            def split_high(c, i, jobs):
                act.wait_ge(raw_landed[c % 2], 32 * (c // 2 + 1) + 32 * i)
                wait(act, tile_full, jobs)
                nc.scalar.activation(wh[:, c % 2, :], raw[:, c % 2, :], ACT.Copy).then_inc(wh_ready, 1)

            def norm_input(m, d, col, evacuated):
                cols = span(col)
                act.wait_ge(*evacuated)
                nc.scalar.activation(sq[:, cols], h[:, d, cols], ACT.Square).then_inc(sq_done, 1)
                nc.scalar.activation(xh[:, d, cols], h[:, d, cols], ACT.Copy,
                                     scale=vec[:, GAIN[m] + d:GAIN[m] + d + 1] if isinstance(d, int) else vec[:, bass.ds(d + GAIN[m], 1)]).then_inc(xh_done, 1)

            def root_mean(m, col):
                cols = span(col)
                act.wait_ge(var_ready, m + 1)
                nc.scalar.activation(sq[:, cols], sq[:, cols], ACT.Sqrt).then_inc(sd_ready, 1)

            def ffn(n, col):
                m = FFNORM[n]
                u0, j0 = FF[n]
                cols = span(col)
                done = 0
                for part, nf in enumerate(PART):
                    def gate_up(i, first=False):
                        for s in range(2):
                            j, k = j0 + 2 * s + 4 * i, done + s + 2 * i
                            split_high(u0 + s + 1, i, j)
                            if first and s == 0:
                                root_mean(m, col)
                            act.wait_ge(tile_evac, j + 1)
                            nc.scalar.activation(t_b[:, cols], t_a[:, cols], ACT.Silu).then_inc(silu_done[n], 1)
                            act.wait_ge(gated[n], k + 1)
                            nc.scalar.activation(act_h[:, s + 2 * i, cols], t_c[:, cols], ACT.Copy).then_inc(act_h_done[n], 1)

                    gate_up(0, part == 0)
                    with act.Fori(1, nf // 2) as i:
                        gate_up(i)
                    u0 += nf
                    j0 += 2 * nf
                    done += nf

                    def down(i, last=False):
                        for s in range(2):
                            if not (last and s == 1):
                                split_high(u0 + s + 1, i, j0 + s + 2 * i)
                            if part == 1 and n < 3:
                                norm_input(m + 1, s + 2 * i, col, (tile_evac, j0 + s + 2 * i + 1))

                    if part == 1 and n == 3:
                        with act.Fori(0, KD // 2 - 1) as i:
                            down(i)
                        down(KD // 2 - 1, True)
                    else:
                        with act.Fori(0, KD // 2) as i:
                            down(i)
                    u0 += KD
                    j0 += KD

            for d in range(KD):
                norm_input(0, d, ALL, (init_evac, d + 2))
            split_high(0, 0, 0)
            ffn(0, ALL)

            X = ps[:, 4:6, :].rearrange("p b n -> p (b n)")

            def gelu(i):
                act.wait_ge(xf, 4 * i + 4)
                nc.scalar.activation(yc[0:NCH].rearrange("c (t g h) -> c g t h", t=T, g=GT),
                                     X[0:NCH, :].rearrange("c (g t h) -> c g t h", t=T, g=GT), ACT.Gelu_apprx_tanh).then_inc(xe, 1)

            def y_high(i):
                act.wait_ge(ye, 4 * i + 4)
                nc.scalar.activation(act_h[:, 2 * KC + i, :], y_t, ACT.Copy).then_inc(yth_done, 1)

            def mixer(i, first):
                u, j = MIX[0] + 2 * i, MIX[1] + 4 * i
                split_high(MIX[0] + 1, i, j)
                if first:
                    root_mean(1, ALL)
                else:
                    gelu(i - 1)
                act.wait_ge(xf, 4 * i + 1)
                nc.scalar.activation(uc4[0:NCH].rearrange("c g (t h) -> c t g h", t=T),
                                     X[0:NCH, :].rearrange("c (t g h) -> c t g h", t=T, g=GT), ACT.Copy).then_inc(xe, 1)
                if not first:
                    y_high(i - 1)
                act.wait_ge(xf, 4 * i + 2)
                nc.scalar.activation(blt, X, ACT.Copy).then_inc(xe, 1)
                split_high(MIX[0] + 2, i, j + 2)
                act.wait_ge(dve_mix, 5 * i + 5)
                nc.scalar.activation(act_h[:, i, :], t_a[:], ACT.Copy).then_inc(yah_done, 1)

            mixer(0, True)
            with act.Fori(1, KC) as i:
                mixer(i, False)
            gelu(KC - 1)
            y_high(KC - 1)
            split_high(WOUT[0], 0, GLU[1])
            for k in range(KC):
                act.wait_ge(tile_full, GLU[1] + k + 1)
                nc.scalar.activation(halves(t_b, ALL), banks(2 * (k % 2), ALL), ACT.Sigmoid,
                                     bias=vec[:, V_GLUB + k:V_GLUB + k + 1]).then_inc(tile_evac, 1)
                act.wait_ge(yb_prod, k + 1)
                nc.scalar.activation(act_h[:, KC + k, :], t_a[:], ACT.Copy).then_inc(ybh_done, 1)

            def project(u0, j0, col, m):
                with act.Fori(0, KD // 4) as i:
                    for s in range(2):
                        split_high(u0 + s + 1, i, j0 + 2 * s + 4 * i)
                        for n in range(2):
                            norm_input(m, 2 * s + n + 4 * i, col, (tile_evac, j0 + 2 * s + n + 4 * i + 1))

            project(*WOUT, ALL, 2)
            ffn(1, ALL)
            ffn(2, ALL)

            u0, j0 = ATT
            split_high(u0 + 1, 0, j0)
            root_mean(4, ALL)
            for t in range(2):
                act.wait_ge(tile_evac, j0 + t + 1)
                if t == 1:
                    act.wait_ge(r_ready, 5)
                nc.scalar.activation((t_b, sq)[t][:], (t_a, t_c)[t][:], ACT.Square).then_inc(hn_sq, 1)
            split_high(u0 + 2, 0, j0 + 2)
            for t in range(2):
                act.wait_ge(hn_var, t + 1)
                nc.scalar.activation(s_all[:, t, 0:L], (t_b, sq)[t][:], ACT.Sqrt).then_inc(hn_sd, 1)
            act.wait_ge(rtok_full, 1)
            split_high(u0 + 3, 0, j0 + 4)

            def query_tile(g, t):
                act.wait_ge(tile_full, j0 + 4 + 2 * g + t + 1)
                if g == 0:
                    act.wait_ge(hn_ready, 2)
                nc.scalar.activation((t_b, sq)[t][:, 0:SEQ], ps[:, 2 * t, :], ACT.Square).then_inc(hn_sq, 1)
                nc.scalar.activation(q_hat[:, g % 2, t, :], ps[:, 2 * t, :], ACT.Copy, scale=vec[:, V_QN:V_QN + 1]).then_inc(tile_evac, 1)

            def exps(g, j):
                n = NT * g + j
                st = stat[:, j % 2]
                act.wait_ge(nm_ready, n + 1)
                for k in range(QP):
                    p = s_all[:, j % 2, k * KEYS:(k + 1) * KEYS]
                    nc.scalar.activation(p, p, ACT.Exp, bias=st[:, 2, k:k + 1], accum_out=st[:, 4, k:k + 1])
                act.wait_ge(at_step, STEPS_G * g + STAT_STEP[j])
                nc.scalar.activation(st[:, 5, 0:QP], st[:, 3, 0:QP], ACT.Exp).then_inc(es_ready, 1)

            def probs_b(g, j):
                act.wait_ge(pt_full, NT * g + j + 1)
                nc.scalar.activation(p_b[0:KB, :], ps[0:KB, 7, :], ACT.Copy).then_inc(pb_evac, 1)

            def out_high(g, j):
                act.wait_ge(o_full, NT * g + j + 1)
                nc.scalar.activation(act_h[:, 2 * g:2 * g + 2, META + j * P:META + (j + 1) * P],
                                     ps[:, 1 + 2 * (j % 2), 0:2 * P].rearrange("p (t n) -> p t n", t=2), ACT.Copy).then_inc(oh_done, 1)

            for t in range(2):
                query_tile(0, t)
            for g in range(NKV):
                more = g + 1 < NKV
                exps(g, 0)
                exps(g, 1)
                if more:
                    query_tile(g + 1, 0)
                probs_b(g, 0)
                exps(g, 2)
                out_high(g, 0)
                if more:
                    query_tile(g + 1, 1)
                    split_high(u0 + 4 + g % 2, g // 2, j0 + 4 + 2 * (g + 1))
                probs_b(g, 1)
                exps(g, 3)
                out_high(g, 1)
                for j in (2, 3):
                    probs_b(g, j)
                    out_high(g, j)
            project(*WO, REAL, 5)
            ffn(3, REAL)
            for d in range(1, KD, 2):
                act.wait_ge(fin_full, d + 1)
                act.wait_ge(fin_evac, d)
                nc.scalar.activation(arena[:, d * 512:(d + 1) * 512], ps[:, 4 + d % 4, :], ACT.Copy).then_inc(fin_evac, 1)

        @block.vector
        def _(dve):
            v = nc.vector

            def split_low(c, i):
                dve.wait_ge(wh_ready, c + 2 * i + 1)
                v.tensor_tensor(wl[:, c % 2, :], raw[:, c % 2, :], wh[:, c % 2, :].bitcast(F32), ALU.subtract).then_inc(wl_ready, 1)

            def tile(pair, col):
                return banks(2 * pair, col)

            def clear_sums(m):
                v.memset(ssq[:], 0.0).then_inc(ssq_step, 1)

            def norm_input(m, d, col):
                cols = span(col)
                dve.wait_ge(sq_done, KD * m + d + 1)
                dve.wait_ge(ssq_step, (KD + 1) * m + d + 1)
                v.tensor_tensor(ssq[:, cols], ssq[:, cols], sq[:, cols], ALU.add).then_inc(ssq_step, 1)
                dve.wait_ge(xh_done, KD * m + d + 1)
                gain = vec[:, GAIN[m] + d:GAIN[m] + d + 1] if isinstance(d, int) else vec[:, bass.ds(d + GAIN[m], 1)]
                v.scalar_tensor_tensor(xl[:, d, cols], h[:, d, cols], gain, xh[:, d, cols].bitcast(F32), ALU.mult, ALU.subtract).then_inc(x_ready, 1)

            def rms(m, col):
                cols = span(col)
                dve.wait_ge(ssum_full, m + 1)
                v.tensor_scalar(halves(sq, col), banks(4, col), 1.0 / DM, EPS, ALU.mult, ALU.add).then_inc(var_ready, 1)
                dve.wait_ge(sd_ready, m + 1)
                v.reciprocal(r[:, cols], sq[:, cols]).then_inc(r_ready, 1)
                dve.wait_ge(r_ready, m + 1)

            def residual(d, j, pair, scale, m, col):
                dve.wait_ge(tile_full, j + 1)
                hd = halves(h[:, d, :], col)
                v.scalar_tensor_tensor(hd, tile(pair, col), scale, hd, ALU.mult, ALU.add).then_inc(tile_evac, 1)
                if m is not None:
                    norm_input(m, d, col)

            def ffn(n, col):
                m = FFNORM[n]
                u0, j0 = FF[n]
                cols = span(col)
                done = 0
                for part, nf in enumerate(PART):
                    def gate_up(i, first=False):
                        for s in range(2):
                            j, k = j0 + 2 * s + 4 * i, done + s + 2 * i
                            split_low(u0 + s + 1, i)
                            if first and s == 0:
                                rms(m, col)
                            dve.wait_ge(tile_full, j + 1)
                            v.tensor_tensor(halves(t_a, col), tile(0, col), halves(r, col), ALU.mult).then_inc(tile_evac, 1)
                            dve.wait_ge(tile_full, j + 2)
                            wait(dve, act_ready[n], k)
                            v.tensor_tensor(halves(t_c, col), tile(1, col), halves(r, col), ALU.mult).then_inc(tile_evac, 1)
                            dve.wait_ge(tile_evac, j + 2)
                            dve.wait_ge(silu_done[n], k + 1)
                            v.tensor_tensor(t_c[:, cols], t_c[:, cols], t_b[:, cols], ALU.mult).then_inc(gated[n], 1)
                            dve.wait_ge(act_h_done[n], k + 1)
                            v.tensor_tensor(act_l[:, s + 2 * i, cols], t_c[:, cols], act_h[:, s + 2 * i, cols].bitcast(F32), ALU.subtract).then_inc(act_ready[n], 1)

                    gate_up(0, part == 0)
                    with dve.Fori(1, nf // 2) as i:
                        gate_up(i)
                    u0 += nf
                    j0 += 2 * nf
                    done += nf
                    more = m + 1 if part == 1 and n < 3 else None
                    if more is not None:
                        clear_sums(more)

                    def down(i, last=False):
                        for s in range(2):
                            if not (last and s == 1):
                                split_low(u0 + s + 1, i)
                            residual(s + 2 * i, j0 + s + 2 * i, s, 0.5, more, col)

                    if part == 1 and n == 3:
                        with dve.Fori(0, KD // 2 - 1) as i:
                            down(i)
                        down(KD // 2 - 1, True)
                    else:
                        with dve.Fori(0, KD // 2) as i:
                            down(i)
                    u0 += KD
                    j0 += KD

            X = ps[:, 4:6, :].rearrange("p b n -> p (b n)")
            dve.wait_ge(init_full, 1)
            v.tensor_copy(vec[:], X[:, 0:NV])
            v.tensor_copy(small[:, 1, :], X[:, P:P + G])
            v.tensor_copy(small[:, 2, :], X[:, 2 * P:2 * P + G]).then_inc(init_evac, 1)
            dve.wait_ge(init_evac, 1)
            v.tensor_scalar(vec[:, V_QN:V_QN + 1], vec[:, V_QN:V_QN + 1], float(HD) ** -0.5, None, ALU.mult)
            clear_sums(0)
            for d in range(KD):
                bank = 6 if d % 2 == 0 else 4
                dve.wait_ge(init_full, d + 2)
                v.tensor_copy(h[:, d, META:L], ps[:, bank, :])
                v.tensor_copy(h[:, d, 0:META], ps[:, bank + 1, 0:META]).then_inc(init_evac, 1)
                norm_input(0, d, ALL)
            dve.wait_ge(init_full, KD + 2)
            v.tensor_copy(c4, ps[:, 6, :])
            v.tensor_copy(c2, ps[:, 7, :]).then_inc(init_evac, 1)
            split_low(0, 0)
            ffn(0, ALL)

            def step_mix(ins, n):
                ins.then_inc(dve_mix, 1)
                dve.wait_ge(dve_mix, n)

            def states(i):
                wait(dve, xf, 4 * i)
                four = lambda x: x.rearrange("p (b g c) -> p b g c", b=2, g=4)
                src = lambda b: ps[:, b:b + 2, 0:4 * NCH].rearrange("p b (g c) -> p b g c", g=4)[:, :, :, 0:NCH - 1]
                dve.wait_ge(tab_landed, 16 * (i + 1))
                dve.wait_ge(xf, 4 * i + 3)
                v.tensor_tensor(four(sq[:])[:, :, :, 1:NCH], src(4), four(cos_t)[:, :, :, 1:NCH], ALU.mult).then_inc(xe, 1)
                dve.wait_ge(yf, 4 * i + 3)
                v.tensor_tensor(four(zs)[:, :, :, 1:NCH], src(6), four(sin_t)[:, :, :, 1:NCH], ALU.mult).then_inc(ye, 1)
                dve.wait_ge(xe, 4 * i + 3)
                dve.wait_ge(ye, 4 * i + 3)
                v.tensor_tensor(z_g[:, :, 1:NCH], sq[:].rearrange("p (g c) -> p g c", g=GT)[:, :, 1:NCH], zs_g[:, :, 1:NCH], ALU.add).then_inc(z_step, 1)
                dve.wait_ge(z_step, 2 * i + 1)
                v.tensor_tensor_scan(zs, rho_t, z, 0.0, ALU.mult, ALU.add).then_inc(z_step, 1)
                dve.wait_ge(z_step, 2 * i + 2)
                v.tensor_tensor(z, zs, cos_t, ALU.mult).then_inc(z_ready, 1)
                v.tensor_tensor(zs, zs, sin_t, ALU.mult).then_inc(z_ready, 1)

            def y_low(i):
                dve.wait_ge(yf, 4 * i + 4)
                wait(dve, yth_done, i)
                v.tensor_copy(y_t.rearrange("p (c b t) -> p b t c", b=2, t=4),
                              ps[:, 6:8, 0:4 * NCH].rearrange("p b (t c) -> p b t c", t=4)).then_inc(ye, 1)
                dve.wait_ge(yth_done, i + 1)
                v.tensor_tensor(act_l[:, 2 * KC + i, :], y_t, act_h[:, 2 * KC + i, :].bitcast(F32), ALU.subtract).then_inc(yt_ready, 1)

            def mixer(i, first):
                u, j = MIX[0] + 2 * i, MIX[1] + 4 * i
                if first:
                    dve.wait_ge(prep, count["mix_zeroed"])
                else:
                    states(i - 1)
                split_low(MIX[0] + 1, i)
                if first:
                    rms(1, ALL)
                dve.wait_ge(tile_full, j + 1)
                v.tensor_tensor(halves(u_t, ALL), tile(0, ALL), halves(r, ALL), ALU.mult).then_inc(tile_evac, 1)
                dve.wait_ge(tile_full, j + 2)
                v.tensor_tensor(halves(t_b, ALL), tile(1, ALL), halves(r, ALL), ALU.mult).then_inc(tile_evac, 1)
                if not first:
                    y_low(i - 1)
                dve.wait_ge(tile_full, j + 3)
                v.tensor_tensor(halves(t_a, ALL), tile(0, ALL), halves(r, ALL), ALU.mult).then_inc(tile_evac, 1)
                dve.wait_ge(tile_evac, j + 3)
                step_mix(v.tensor_tensor(hc[:, 2:L + 2], t_a[:], t_b[:], ALU.mult), 5 * i + 1)
                w = lambda k: (vec[:, V_CONV + k * KC + i:V_CONV + k * KC + i + 1] if isinstance(i, int)
                               else vec[:, bass.ds(i + (V_CONV + k * KC), 1)])
                step_mix(v.tensor_scalar(t_c[:], hc[:, 0:L], w(0), None, ALU.mult), 5 * i + 2)
                for k in (1, 2):
                    step_mix(v.scalar_tensor_tensor(t_c[:], hc[:, k:L + k], w(k), t_c[:], ALU.mult, ALU.add), 5 * i + 2 + k)
                dve.wait_ge(yf, 4 * i + 1)
                v.tensor_copy(u_c.rearrange("p (b n) -> p b n", b=2), ps[:, 6:8, 0:4 * NCH]).then_inc(ye, 1)
                split_low(MIX[0] + 2, i)
                dve.wait_ge(tile_full, j + 4)
                v.tensor_tensor(halves(t_a, ALL), tile(1, ALL), halves(r, ALL), ALU.mult).then_inc(tile_evac, 1)
                dve.wait_ge(tile_evac, j + 4)
                v.tensor_tensor(t_a[:], t_a[:], t_c[:], ALU.mult).then_inc(dve_mix, 1)
                dve.wait_ge(yah_done, i + 1)
                v.tensor_tensor(act_l[:, i, :], t_a[:], act_h[:, i, :].bitcast(F32), ALU.subtract).then_inc(ya_ready, 1)
                dve.wait_ge(yf, 4 * i + 2)
                yk = ps[0:H, 6:8, :].rearrange("p b n -> p (b n)").rearrange("p (g n) -> p g n", g=GT)
                v.tensor_copy(krow[0:H, :, H:P], yk[:, :, H:P]).then_inc(krow_ready, 1)
                v.tensor_tensor(krow[0:H, :, 0:H], yk[:, :, 0:H], d16[:, bass.ds(i * GT, GT), :], ALU.add).then_inc(ye, 1)

            mixer(0, True)
            with dve.Fori(1, KC) as i:
                mixer(i, False)
            states(KC - 1)
            y_low(KC - 1)
            split_low(WOUT[0], 0)
            for k in range(KC):
                wait(dve, yb_prod, k)
                v.tensor_tensor(t_c[:], act_h[:, 2 * KC + k, :].bitcast(F32), act_l[:, 2 * KC + k, :].bitcast(F32), ALU.add).then_inc(dve_mix, 1)
                dve.wait_ge(dve_mix, 5 * KC + k + 1)
                dve.wait_ge(tile_evac, GLU[1] + k + 1)
                v.tensor_tensor(t_a[:], t_b[:], t_c[:], ALU.mult).then_inc(yb_prod, 1)
                dve.wait_ge(ybh_done, k + 1)
                v.tensor_tensor(act_l[:, KC + k, :], t_a[:], act_h[:, KC + k, :].bitcast(F32), ALU.subtract).then_inc(yb_ready, 1)

            def project(u0, j0, col, m):
                clear_sums(m)
                with dve.Fori(0, KD // 4) as i:
                    for s in range(2):
                        split_low(u0 + s + 1, i)
                        for n in range(2):
                            residual(2 * s + n + 4 * i, j0 + 2 * s + n + 4 * i, n, 1.0, m, col)

            project(*WOUT, ALL, 2)
            ffn(1, ALL)
            ffn(2, ALL)

            u0, j0 = ATT

            def key_norm(t):
                k_in, var, y, w = (t_a, t_c)[t], (t_b, sq)[t], s_all[:, t, 0:L], k_cur[:, t, 0:L]
                dve.wait_ge(hn_sum, t + 1)
                v.tensor_scalar(halves(var, ALL), banks(4 + 2 * t, ALL), 1.0 / HD, EPS, ALU.mult, ALU.add).then_inc(hn_var, 1)
                dve.wait_ge(hn_sd, t + 1)
                v.reciprocal(y, y).then_inc(hn_step, 1)
                dve.wait_ge(hn_step, 4 * t + 1)
                v.tensor_tensor(w, y, y, ALU.mult).then_inc(hn_step, 1)
                dve.wait_ge(hn_step, 4 * t + 2)
                v.scalar_tensor_tensor(w, w, -0.5, var[:], ALU.mult, ALU.mult).then_inc(hn_step, 1)
                dve.wait_ge(hn_step, 4 * t + 3)
                v.scalar_tensor_tensor(y, w, 1.5, y, ALU.add, ALU.mult).then_inc(hn_step, 1)
                dve.wait_ge(hn_step, 4 * t + 4)
                gain = vec[:, V_KN:V_KN + 1]
                by_block = lambda x, lo, nb, a, b: x[:, lo:lo + nb * P].rearrange("p (j n) -> p j n", n=P)[:, :, a:b]
                v.scalar_tensor_tensor(k_win[:, t, :, CH:BAND], by_block(k_in, META, NT, 0, P), gain, by_block(y, META, NT, 0, P), ALU.mult, ALU.mult)
                v.scalar_tensor_tensor(k_win[:, t, 1:NT, 0:CH], by_block(k_in, META + CH, NT - 1, 0, CH), gain, by_block(y, META + CH, NT - 1, 0, CH), ALU.mult, ALU.mult)
                meta = lambda x: x[:, 0:META].unsqueeze(1).to_broadcast([P, NT, META])
                v.scalar_tensor_tensor(k_win[:, t, :, BAND:KEYS], meta(k_in), gain, meta(y), ALU.mult, ALU.mult).then_inc(hn_ready, 1)

            def current_keys(g):
                rows = slice((g % 2) * HD, (g % 2 + 1) * HD)
                if g >= 2:
                    dve.wait_ge(s_full, NT * (g - 1))
                for half in range(2):
                    last = v.tensor_copy(k_cur[half * HD:(half + 1) * HD, g % 2, :], k_win[rows, g // 2, :, :].rearrange("p j n -> p (j n)"))
                last.then_inc(k_cur_ready, 1)

            def query_norm(g):
                c = [QSTEPS * g]

                def step(ins):
                    ins.then_inc(qn_step, 1)
                    c[0] += 1
                    dve.wait_ge(qn_step, c[0])

                by_tb = lambda x: x.rearrange("p (t b h) -> p t b h", t=2, b=NT)
                of_token = lambda x: x[:, 0:NT].unsqueeze(1).unsqueeze(3).to_broadcast([P, 2, NT, 2])
                var, y, w = nq[:, 0, :], rq[:, g % 2, :], nq[:, 1, :]
                dve.wait_ge(hn_sum, 2 + 2 * g + 2)
                of_bank = lambda x: x.rearrange("p (b h) -> p b h", b=NT)
                for t in range(2):
                    step(v.tensor_tensor(of_bank(var[:, 2 * NT * t:2 * NT * (t + 1)]), of_bank(ps[:, 2 * t, 0:2 * NT]),
                                         rtok2[:, 0:NT].unsqueeze(2).to_broadcast([P, NT, 2]), ALU.mult))
                step(v.tensor_scalar(var, var, EPS, None, ALU.add))
                step(v.tensor_scalar(y.bitcast(I32), var.bitcast(I32), -0.5, 1597463007.0, ALU.mult, ALU.add))
                for _ in range(3):
                    step(v.tensor_tensor(w, y, y, ALU.mult))
                    step(v.scalar_tensor_tensor(w, w, -0.5, var, ALU.mult, ALU.mult))
                    step(v.scalar_tensor_tensor(y, w, 1.5, y, ALU.add, ALU.mult))
                step(v.tensor_tensor(by_tb(y), by_tb(y), of_token(rtok), ALU.mult))
                assert c[0] == QSTEPS * (g + 1)

            split_low(u0 + 1, 0)
            rms(4, ALL)
            for t in range(2):
                dve.wait_ge(tile_full, j0 + t + 1)
                v.tensor_tensor(halves((t_a, t_c)[t], ALL), tile(t, ALL), halves(r, ALL), ALU.mult).then_inc(tile_evac, 1)
            dve.wait_ge(prep, count["att_consts"])
            split_low(u0 + 2, 0)
            for t in range(2):
                key_norm(t)
            current_keys(0)
            dve.wait_ge(rtok_full, 1)
            v.tensor_copy(rtok[0:META, NT:NT + 1], ps[0:META, 5, NT:NT + 1]).then_inc(rtok_ready, 1)
            v.tensor_copy(rtok[:, 0:NT], ps[:, 5, 0:NT]).then_inc(rtok_ready, 1)
            dve.wait_ge(rtok_ready, 2)
            v.tensor_tensor(rtok2[:, 0:NT], rtok[:, 0:NT], rtok[:, 0:NT], ALU.mult).then_inc(rtok_ready, 1)
            dve.wait_ge(rtok_ready, 3)
            v.tensor_scalar(rtok2[:, 0:NT], rtok2[:, 0:NT], 1.0 / HD, None, ALU.mult).then_inc(rtok_ready, 1)
            dve.wait_ge(rtok_ready, 4)
            for t in range(NT):
                if t % 2 == 0:
                    dve.wait_ge(tile_full, j0 + 3 + t // 2)
                src = ps[:, t, 0:NKV * HD]
                v.tensor_scalar(va[CH:P, t, :], src[0:CH], rtok[0:CH, t:t + 1], None, ALU.mult)
                if t + 1 < NT:
                    v.tensor_scalar(va[0:CH, t + 1, :], src[CH:P], rtok[CH:P, t:t + 1], None, ALU.mult)
                last = v.tensor_scalar(vb[0:CH, t, :], src[CH:P], rtok[CH:P, t:t + 1], None, ALU.mult)
                if t % 2 == 1:
                    last.then_inc(tile_evac, 1)
            for t in range(NT):
                last = v.tensor_scalar(vb[CH:KB, t, :], ps[0:META, 4, 0:NKV * HD], rtok[0:META, NT:NT + 1], None, ALU.mult)
            last.then_inc(v_ready, 1)
            split_low(u0 + 3, 0)
            dve.wait_ge(sink_landed, 16)
            at = [0]

            def did(ins):
                ins.then_inc(at_step, 1)
                at[0] += 1

            def softmax(g, j):
                n = NT * g + j
                st = stat[:, j % 2]
                dve.wait_ge(s_full, n + 1)
                if n >= 2:
                    dve.wait_ge(pt_full, n - 1)
                for k in range(QP):
                    col = (k // 2) * 2 * NT + j * 2 + k % 2
                    last = v.scalar_tensor_tensor(s_all[:, j % 2, k * KEYS:(k + 1) * KEYS], ps[:, 4 + k % 2, (k // 2) * KEYS:(k // 2 + 1) * KEYS],
                                                  rq[:, g % 2, col:col + 1], bias[:, k * KEYS:(k + 1) * KEYS], ALU.mult, ALU.add)
                last.then_inc(s_evac, 1)
                dve.wait_ge(s_evac, n + 1)
                s4 = s_all[:, j % 2, :].rearrange("p (k n) -> p k n", k=QP)
                if j == 0:
                    did(v.memset(s4[:, :, 0:CH], -1e30))
                    dve.wait_ge(at_step, at[0])
                did(v.tensor_reduce(st[:, 0, 0:QP], s4, AX_X, ALU.max))
                dve.wait_ge(at_step, at[0])
                sinks = sink_t[:, g * QP:(g + 1) * QP]
                did(v.tensor_tensor(st[:, 1, 0:QP], st[:, 0, 0:QP], sinks, ALU.max))
                dve.wait_ge(at_step, at[0])
                v.tensor_scalar(st[:, 2, 0:QP], st[:, 1, 0:QP], -1.0, None, ALU.mult).then_inc(nm_ready, 1)
                dve.wait_ge(nm_ready, n + 1)
                did(v.tensor_tensor(st[:, 3, 0:QP], st[:, 2, 0:QP], sinks, ALU.add))
                assert at[0] == STEPS_G * g + STAT_STEP[j]

            def normed(g, j):
                n = NT * g + j
                st = stat[:, j % 2]
                dve.wait_ge(es_ready, n + 1)
                did(v.tensor_tensor(st[:, 6, 0:QP], st[:, 4, 0:QP], st[:, 5, 0:QP], ALU.add))
                dve.wait_ge(at_step, at[0])
                did(v.reciprocal(st[:, 7, 0:QP], st[:, 6, 0:QP]))
                dve.wait_ge(at_step, at[0])
                s4 = s_all[:, j % 2, :].rearrange("p (k n) -> p k n", k=QP)
                v.tensor_tensor(s4, s4, st[:, 7, 0:QP].unsqueeze(2).to_broadcast([P, QP, KEYS]), ALU.mult).then_inc(pn_ready, 1)

            def probs_a(g, j):
                dve.wait_ge(pt_full, NT * g + j + 1)
                v.tensor_copy(p_a, ps[:, 6, :]).then_inc(pa_evac, 1)

            def out_low(g, j):
                dve.wait_ge(oh_done, NT * g + j + 1)
                cols = slice(META + j * P, META + (j + 1) * P)
                v.tensor_tensor(act_l[:, 2 * g:2 * g + 2, cols], ps[:, 1 + 2 * (j % 2), 0:2 * P].rearrange("p (t n) -> p t n", t=2),
                                act_h[:, 2 * g:2 * g + 2, cols].bitcast(F32), ALU.subtract).then_inc(ol_done, 1)

            query_norm(0)
            for g in range(NKV):
                more = g + 1 < NKV
                if g:
                    dve.wait_ge(bias_ready, g)
                softmax(g, 0)
                softmax(g, 1)
                normed(g, 0)
                probs_a(g, 0)
                softmax(g, 2)
                normed(g, 1)
                out_low(g, 0)
                if more:
                    split_low(u0 + 4 + g % 2, g // 2)
                probs_a(g, 1)
                softmax(g, 3)
                normed(g, 2)
                out_low(g, 1)
                if more:
                    v.tensor_scalar(bias, bias, 2.0 ** (-8.0 * QP / NH), None, ALU.mult).then_inc(bias_ready, 1)
                    current_keys(g + 1)
                normed(g, 3)
                probs_a(g, 2)
                if more:
                    query_norm(g + 1)
                out_low(g, 2)
                probs_a(g, 3)
                out_low(g, 3)
            project(*WO, REAL, 5)
            ffn(3, REAL)
            for d in range(0, KD, 2):
                dve.wait_ge(fin_full, d + 1)
                wait(dve, fin_evac, d)
                v.tensor_copy(arena[:, d * 512:(d + 1) * 512], ps[:, 4 + d % 4, :]).then_inc(fin_evac, 1)


_INS = ['x', 'meta_tokens', 'norm_ff1', 'ff1_w_gate', 'ff1_w_up', 'ff1_w_down', 'norm_mix', 'even_w_in', 'conv_w',
        'ssm_lambda_re', 'ssm_lambda_im', 'ssm_log_step', 'ssm_b_re', 'ssm_b_im', 'ssm_c_re', 'ssm_c_im', 'ssm_d',
        'glu_w', 'glu_b', 'even_w_out', 'attn_w_qkv', 'attn_q_norm', 'attn_k_norm', 'attn_sinks', 'attn_w_o',
        'norm_ff2', 'ff2_w_gate', 'ff2_w_up', 'ff2_w_down']


def kernel(**inputs):
    import numpy as _np
    import concourse.bacc as _bacc
    from concourse import mybir as _mybir
    from concourse.bass_utils import run_bass_kernel_spmd as _run

    nc = _bacc.Bacc("TRN2", target_bir_lowering=False, num_devices=1)
    arrays, args = {}, {}
    for name in _INS:
        arr = _np.ascontiguousarray(inputs[name])
        arrays[f"in_{name}"] = arr
        args[name] = nc.dram_tensor(f"in_{name}", arr.shape, _mybir.dt.from_np(arr.dtype), kind="ExternalInput").ap()
    out = nc.dram_tensor("out", arrays["in_x"].shape, _mybir.dt.float32, kind="ExternalOutput").ap()
    trunk_program(nc, args, out)
    res = _run(nc, [arrays], core_ids=[0])
    return res.results[0]["out"]
```

```python
import math
from contextlib import ExitStack

import concourse.bass as bass
from concourse import mybir

F32 = mybir.dt.float32
F32R = mybir.dt.float32r
I32 = mybir.dt.int32
ALU = mybir.AluOpType
ACT = mybir.ActivationFunctionType
AX_X = mybir.AxisListType.X

P = 128
ARENA = 11300
BLK = 16
UNITW = BLK * P


def trunk_program(nc, a, out, stop=None):
    SEQ, DM = a["x"].shape[1], a["x"].shape[2]
    META = a["meta_tokens"].shape[0]
    L = META + SEQ
    KD = DM // P
    DFF = a["ff1_w_gate"].shape[2]
    NF = DFF // P
    PART = [12, NF - 12]
    DC = a["conv_w"].shape[2]
    KC = DC // P
    G, ST = a["ssm_lambda_re"].shape[1:]
    H = a["ssm_b_re"].shape[3]
    T = P // H
    NCH = L // T
    GT = P // H
    NT = SEQ // P
    NH = a["attn_sinks"].shape[1]
    HD = a["attn_q_norm"].shape[1]
    NKV = (a["attn_w_qkv"].shape[2] // HD - NH) // 2
    QP = NH // NKV
    CH = 64
    BAND = P + CH
    KEYS = BAND + META
    NB = NT * NKV
    KB = KEYS - P
    EPS = 1e-6
    QSTEPS = 14
    assert ST * 2 == P and T * H == P and NCH * T == L and NH * HD == DM and META % 16 == 0

    FU, FJ = NF + 2 * KD, 2 * NF + 2 * KD
    FF = [(0, 0)]
    MIX = (FU, FJ)
    GLU = (MIX[0] + 2 * KC, MIX[1] + 4 * KC)
    WOUT = (GLU[0] + 1, GLU[1] + KC)
    FF.append((WOUT[0] + KD // 2, WOUT[1] + KD))
    FF.append((FF[1][0] + FU, FF[1][1] + FJ))
    ATT = (FF[2][0] + FU, FF[2][1] + FJ)
    WO = (ATT[0] + 2 + NKV, ATT[1] + 4 + 2 * NKV)
    FF.append((WO[0] + KD // 2, WO[1] + KD))
    LAST_UNIT = FF[3][0] + FU - 1

    FFW = [(a["ff1_w_gate"], a["ff1_w_up"], a["ff1_w_down"], 0), (a["ff2_w_gate"], a["ff2_w_up"], a["ff2_w_down"], 0),
           (a["ff1_w_gate"], a["ff1_w_up"], a["ff1_w_down"], 1), (a["ff2_w_gate"], a["ff2_w_up"], a["ff2_w_down"], 1)]
    FFNORM = [0, 2, 3, 5]
    GAIN = [0, 2 * KD, 4 * KD, KD, 3 * KD, 5 * KD]
    ALL = (0, L // 2, 2)
    REAL = (META, SEQ, 1)
    V_CONV = 6 * KD
    V_GLUB = V_CONV + 3 * KC
    V_QN, V_KN, NV = V_GLUB + KC, V_GLUB + KC + 1, V_GLUB + KC + 2

    with ExitStack() as ctx:
        def sb(name, shape, dt=F32):
            return ctx.enter_context(nc.sbuf_tensor(name, shape, dt))

        def sem(name):
            return ctx.enter_context(nc.semaphore(name))

        h = sb("h", [P, KD, L])
        xh = sb("xh", [P, KD, L], F32R)
        xl = sb("xl", [P, KD, L], F32R)
        act_h = sb("act_h", [P, PART[0], L], F32R)
        act_l = sb("act_l", [P, PART[0], L], F32R)
        raw = sb("raw", [P, 2, UNITW])
        wh = sb("wh", [P, 2, UNITW], F32R)
        wl = sb("wl", [P, 2, UNITW], F32R)
        t_a = sb("t_a", [P, L])
        t_b = sb("t_b", [P, L])
        t_c = sb("t_c", [P, L])
        sq = sb("sq", [P, L])
        ssq = sb("ssq", [P, L])
        r = sb("r", [P, L])
        ident = sb("ident", [P, P])
        ones = sb("ones", [P, P])
        pair_ones = sb("pair_ones", [P, P])
        vec = sb("vec", [P, NV])
        sg = sb("sg", [P, 1])
        d16 = sb("d16", [H, G, H])
        arena = sb("arena", [P, ARENA])
        ps = ctx.enter_context(nc.psum_tensor("ps", [P, 8, 512], F32))
        tabs = nc.dram_tensor("ssm_tables", (KC, P, GT * (T + 1) * H + 2 * P * GT + 3 * GT * NCH), F32, kind="Internal").ap()

        def carve(sizes):
            at, got = 0, []
            for n in sizes:
                got.append(arena[:, at:at + n])
                at += n
            assert at <= ARENA, at
            return got

        (v_xs, v_meta, v_vec, v_lam, v_c4, v_c2, b4, b2, small_all, pw_all) = carve(
            [NT * DM, 2 * G * H, P, 2 * P, 4 * P, 4 * P, G * H, G * H, 24 * G, 5 * (T + 1) * G])
        c4, c2 = v_meta[:, 0:G * H], v_meta[:, G * H:2 * G * H]
        bb4, bb2 = v_c4, v_c2
        v_xs = v_xs.rearrange("p (t d) -> p t d", t=NT)
        v_lam = v_lam.rearrange("p (c n) -> p c n", c=2)
        v_c4 = v_c4.rearrange("p (t n) -> p t n", t=4)
        v_c2 = v_c2.rearrange("p (t n) -> p t n", t=4)
        assert DM <= 2 * G * H
        small = small_all.rearrange("p (n g) -> p n g", g=G)
        pw = pw_all.rearrange("p (n k g) -> p n k g", n=5, g=G)
        WCL = GT * (T + 1) * H
        piece = [arena[:, 0:WCL], arena[:, WCL:2 * WCL]]
        ptmp = arena[:, 2 * WCL:3 * WCL]
        assert 3 * WCL <= NT * DM

        WP = P * GT
        WC = GT * NCH
        WTAB = WCL + 2 * WP + 3 * WC
        (tab, u_t, hc, uc, u_c, blt, kloc, z, zs, y_t) = carve(
            [WTAB, L, L + 2, WP, WC, WP, WP, WC, WC, L])
        cl = tab[:, 0:WCL].rearrange("p (g n) -> p g n", g=GT)
        cl2 = tab[:, WCL:WCL + WP].rearrange("p (g n) -> p g n", g=GT)
        bl = tab[:, WCL + WP:WCL + 2 * WP].rearrange("p (g n) -> p g n", g=GT)
        krow = bl
        cos_t, sin_t, rho_t = (tab[:, WCL + 2 * WP + k * WC:WCL + 2 * WP + (k + 1) * WC] for k in range(3))
        uc4 = uc.rearrange("p (g n) -> p g n", g=GT)
        yc = uc
        u_g = u_c.rearrange("p (g c) -> p g c", g=GT)
        blt_g = blt.rearrange("p (g n) -> p g n", g=GT)
        kloc_g = kloc.rearrange("p (g n) -> p g n", g=GT)
        z_g = z.rearrange("p (g c) -> p g c", g=GT)
        zs_g = zs.rearrange("p (g c) -> p g c", g=GT)

        WIN = NT * KEYS
        (q_hat, k_win, k_cur, va, vb, bias, s_all, p_a, p_b, stat, rtok, rtok2, rq, nq, sink_t) = carve(
            [2 * 2 * SEQ, 2 * WIN, 2 * WIN, NT * 256, NT * 256, QP * KEYS, 2 * QP * KEYS, 512, 512, 2 * 8 * QP, 8, 8, 2 * 16, 2 * 16, NH])
        q_hat = q_hat.rearrange("p (b t n) -> p b t n", b=2, t=2)
        k_win = k_win.rearrange("p (t j n) -> p t j n", t=2, j=NT)
        k_cur = k_cur.rearrange("p (b n) -> p b n", b=2)
        va = va.rearrange("p (j n) -> p j n", j=NT)
        vb = vb.rearrange("p (j n) -> p j n", j=NT)
        s_all = s_all.rearrange("p (b n) -> p b n", b=2)
        stat = stat.rearrange("p (b k n) -> p b k n", b=2, k=8)
        rq = rq.rearrange("p (b n) -> p b n", b=2)
        nq = nq.rearrange("p (b n) -> p b n", b=2)

        raw_landed = [sem("raw_landed0"), sem("raw_landed1")]
        wh_ready, wl_ready = sem("wh_ready"), sem("wl_ready")
        tile_full, tile_evac = sem("tile_full"), sem("tile_evac")
        x_landed, vec_landed, par_landed, sink_landed = sem("x_landed"), sem("vec_landed"), sem("par_landed"), sem("sink_landed")
        consts = sem("consts")
        init_full, init_evac = sem("init_full"), sem("init_evac")
        silu_done = [sem(f"silu_done{n}") for n in range(4)]
        gated = [sem(f"gated{n}") for n in range(4)]
        act_h_done = [sem(f"act_h_done{n}") for n in range(4)]
        act_ready = [sem(f"act_ready{n}") for n in range(4)]
        sq_done, ssq_step, xh_done, x_ready = sem("sq_done"), sem("ssq_step"), sem("xh_done"), sem("x_ready")
        ssum_full, var_ready, sd_ready, r_ready = sem("ssum_full"), sem("var_ready"), sem("sd_ready"), sem("r_ready")
        prep = sem("prep")
        piece_out = [sem("piece_out0"), sem("piece_out1")]
        tab_landed, kloc_landed = sem("tab_landed"), [sem("kloc_zero"), sem("kloc_landed")]
        dve_mix = sem("dve_mix")
        xf, xe, yf, ye = sem("xbank_full"), sem("xbank_evac"), sem("ybank_full"), sem("ybank_evac")
        yah_done, ya_ready = sem("yah_done"), sem("ya_ready")
        z_step = sem("z_step")
        z_ready, yth_done, yt_ready = sem("z_ready"), sem("yth_done"), sem("yt_ready")
        krow_ready = sem("krow_ready")
        yb_prod, ybh_done, yb_ready = sem("yb_prod"), sem("ybh_done"), sem("yb_ready")
        hn_sq, hn_sum, hn_var, hn_sd, hn_ready = sem("hn_sq"), sem("hn_sum"), sem("hn_var"), sem("hn_sd"), sem("hn_ready")
        hn_step, qn_step, k_step = sem("hn_step"), sem("qn_step"), sem("k_step")
        rtok_full, rtok_ready, v_ready = sem("rtok_full"), sem("rtok_ready"), sem("v_ready")
        vmeta_full = sem("vmeta_full")
        k_cur_ready, bias_ready = sem("k_cur_ready"), sem("bias_ready")
        pn_ready = sem("pn_ready")
        s_full, s_evac, at_step, nm_ready, p_ready, es_ready = sem("s_full"), sem("s_evac"), sem("at_step"), sem("nm_ready"), sem("p_ready"), sem("es_ready")
        pt_full, pt_evac, o_full = sem("pt_full"), sem("pt_evac"), sem("o_full")
        oh_done, ol_done = sem("oh_done"), sem("ol_done")
        fin_full, fin_evac, out_done = sem("fin_full"), sem("fin_evac"), sem("out_done")

        block = ctx.enter_context(nc.Block())
        count = {}

        def norm_steps(n):
            return 3 * (n + 1) + n // NT + 1 + 2 * n

        def wait(eng, s, v):
            if not isinstance(v, int) or v > 0:
                eng.wait_ge(s, v)

        def value_windows(t):
            first, second = slice(0, CH), slice(CH, P)
            at = [(va[CH:P, t, :], first), (vb[0:CH, t, :], second)]
            return at + ([(va[0:CH, t + 1, :], second)] if t + 1 < NT else [])

        def span(col):
            c0, nh, nb = col
            return slice(c0, c0 + nb * nh)

        def halves(ap, col):
            return ap[:, span(col)].rearrange("p (b n) -> p b n", b=col[2]) if col[2] > 1 else ap[:, span(col)]

        def banks(b, col):
            return ps[:, b:b + col[2], 0:col[1]] if col[2] > 1 else ps[:, b, 0:col[1]]

        @block.gpsimd
        def _(pool):
            g = nc.gpsimd
            made = [0]

            def const(ins):
                ins.then_inc(consts, 1)
                made[0] += 1
                pool.wait_ge(consts, made[0])

            const(g.memset(ident[:], 0.0))
            const(g.affine_select(out=ident[:], in_=ident[:], compare_op=ALU.not_equal, fill=1.0, base=0,
                                  pattern=[[-1, P]], channel_multiplier=1))
            const(g.memset(ones[:], 1.0))
            const(g.memset(pair_ones[:], 0.0))
            const(g.memset(pair_ones[0:HD, 0:HD], 1.0))
            const(g.memset(pair_ones[HD:P, HD:P], 1.0))
            const(g.memset(sg[0:ST, :], 1.0))
            const(g.memset(sg[ST:P, :], -1.0))
            assert made[0] == 8

            n_par = 0
            for half in range(2):
                rows = slice(half * ST, (half + 1) * ST)
                re, im = a["ssm_b_re"][0].rearrange("g p h -> p g h"), a["ssm_b_im"][0].rearrange("g p h -> p g h")
                for dst, src in ((b4, (re, im)[half]), (b2, (im, re)[half])):
                    pool.dma_start(dst[rows, :].rearrange("p (g h) -> p g h", g=G), src).then_inc(par_landed, 16)
                    n_par += 1
                cols = slice(half * ST, (half + 1) * ST)
                cre, cim = (a[n][0].rearrange("(t a) h p -> (a h) t p", t=4) for n in ("ssm_c_re", "ssm_c_im"))
                for dst, src in ((v_c4, (cre, cim)[half]), (v_c2, (cim, cre)[half])):
                    pool.dma_start(dst[:, :, cols], src).then_inc(par_landed, 16)
                    n_par += 1
            pool.dma_start(small[:, 0, :], a["ssm_log_step"].partition_broadcast(P)).then_inc(par_landed, 16)
            pool.dma_start(d16[:].rearrange("p g h -> p (g h)"), a["ssm_d"].partition_broadcast(H)).then_inc(par_landed, 16)
            assert n_par + 2 == 10

            steps = [0]

            def did(ins):
                ins.then_inc(prep, 1)
                steps[0] += 1
                pool.wait_ge(prep, steps[0])

            def tt(o, x, y, op):
                did(g.tensor_tensor(o, x, y, op))

            def ts(o, x, s1, op0, s2=None, op1=None):
                did(g.tensor_scalar(o, x, s1, s2, op0, op1) if op1 is not None else g.tensor_scalar(o, x, s1, None, op0))

            pool.wait_ge(par_landed, 160)
            pool.wait_ge(init_evac, 10)
            S = lambda k: small[:, k, :]
            (LOGST, LRE, LIM, STEP, T0, T1, T2, T3, AR, AI, TH, CQ, CW, SN, CS, MG, A8R, A8I, R8, KF, K1, K2, P1, P2) = range(24)
            tt(d16[:], d16[:], ident[0:H, 0:H].unsqueeze(1).to_broadcast([H, G, H]), ALU.mult)

            RND = 1.5 * 2.0 ** 23

            def exp_of(o, x):
                ts(S(T0), x, -180.0, ALU.max, 180.0, ALU.min)
                ts(S(KF), S(T0), 1.0 / math.log(2.0), ALU.mult)
                ts(S(KF), S(KF), RND, ALU.add)
                ts(S(KF), S(KF), -RND, ALU.add)
                ln2_hi = 0.693359375
                ln2_lo = math.log(2.0) - ln2_hi
                ts(S(T1), S(KF), -ln2_hi, ALU.mult)
                tt(S(T0), S(T0), S(T1), ALU.add)
                ts(S(T1), S(KF), -ln2_lo, ALU.mult)
                tt(S(T0), S(T0), S(T1), ALU.add)
                ts(S(T1), S(T0), 1.0 / 5040, ALU.mult, 1.0 / 720, ALU.add)
                for c in (1.0 / 120, 1.0 / 24, 1.0 / 6, 0.5, 1.0, 1.0):
                    tt(S(T1), S(T1), S(T0), ALU.mult)
                    ts(S(T1), S(T1), c, ALU.add)
                ts(S(K1), S(KF), 0.5, ALU.mult)
                ts(S(K1), S(K1), RND, ALU.add)
                ts(S(K1), S(K1), -RND, ALU.add)
                tt(S(K2), S(KF), S(K1), ALU.subtract)
                for k, p in ((K1, P1), (K2, P2)):
                    ts(S(k), S(k), -126.0, ALU.max, 127.0, ALU.min)
                    ts(S(k), S(k), 127.0, ALU.add)
                    did(g.tensor_scalar(S(p).bitcast(I32), S(k), 2.0 ** 23, None, ALU.mult))
                tt(S(T1), S(T1), S(P1), ALU.mult)
                tt(o, S(T1), S(P2), ALU.mult)

            exp_of(S(STEP), S(LOGST))
            tt(S(T3), S(LRE), S(STEP), ALU.mult)
            exp_of(S(MG), S(T3))
            tt(S(TH), S(LIM), S(STEP), ALU.mult)
            ts(S(KF), S(TH), 2.0 / math.pi, ALU.mult)
            ts(S(KF), S(KF), RND, ALU.add)
            ts(S(KF), S(KF), -RND, ALU.add)
            pi_1 = 1.5703125
            pi_2 = 4.837512969970703125e-4
            pi_3 = math.pi / 2 - pi_1 - pi_2
            for c in (pi_1, pi_2, pi_3):
                ts(S(T0), S(KF), -c, ALU.mult)
                tt(S(TH), S(TH), S(T0), ALU.add)
            tt(S(T0), S(TH), S(TH), ALU.mult)
            ts(S(SN), S(T0), 1.0 / 362880, ALU.mult, -1.0 / 5040, ALU.add)
            for c in (1.0 / 120, -1.0 / 6, 1.0):
                tt(S(SN), S(SN), S(T0), ALU.mult)
                ts(S(SN), S(SN), c, ALU.add)
            tt(S(SN), S(SN), S(TH), ALU.mult)
            ts(S(CS), S(T0), -1.0 / 3628800, ALU.mult, 1.0 / 40320, ALU.add)
            for c in (-1.0 / 720, 1.0 / 24, -0.5, 1.0):
                tt(S(CS), S(CS), S(T0), ALU.mult)
                ts(S(CS), S(CS), c, ALU.add)
            ts(S(T1), S(KF), 0.25, ALU.mult)
            ts(S(T1), S(T1), RND, ALU.add)
            ts(S(T1), S(T1), -RND, ALU.add)
            ts(S(T1), S(T1), -4.0, ALU.mult)
            tt(S(T1), S(T1), S(KF), ALU.add)
            ts(S(T2), S(T1), 0.0, ALU.max, 2.0, ALU.mult)
            tt(S(T2), S(T2), S(T1), ALU.subtract)
            ts(S(K1), S(T2), -1.0, ALU.mult, 1.0, ALU.add)
            ts(S(K2), S(T2), -1.0, ALU.mult, 2.0, ALU.add)
            tt(S(K2), S(K2), S(T1), ALU.mult)
            tt(S(T0), S(CS), S(K1), ALU.mult)
            tt(S(T1), S(SN), S(K2), ALU.mult)
            tt(S(T2), S(SN), S(K1), ALU.mult)
            tt(S(T3), S(CS), S(K2), ALU.mult)
            tt(S(CS), S(T0), S(T1), ALU.subtract)
            tt(S(SN), S(T2), S(T3), ALU.add)
            tt(S(AR), S(MG), S(CS), ALU.mult)
            tt(S(AI), S(MG), S(SN), ALU.mult)
            ts(S(T0), S(AR), -1.0, ALU.add)
            tt(S(T1), S(LRE), S(LRE), ALU.mult)
            tt(S(T2), S(LIM), S(LIM), ALU.mult)
            tt(S(T3), S(T1), S(T2), ALU.add)
            did(g.memset(S(K1), -1.0))
            tt(S(T1), S(T3), S(K1), ALU.pow)
            tt(S(T2), S(T3), S(T1), ALU.mult)
            ts(S(T2), S(T2), -1.0, ALU.mult, 2.0, ALU.add)
            tt(S(T3), S(T1), S(T2), ALU.mult)
            tt(S(T1), S(T0), S(LRE), ALU.mult)
            tt(S(T2), S(AI), S(LIM), ALU.mult)
            tt(S(T1), S(T1), S(T2), ALU.add)
            tt(S(CQ), S(T1), S(T3), ALU.mult)
            tt(S(T1), S(AI), S(LRE), ALU.mult)
            tt(S(T2), S(T0), S(LIM), ALU.mult)
            tt(S(T1), S(T1), S(T2), ALU.subtract)
            tt(S(CW), S(T1), S(T3), ALU.mult)
            did(g.memset(pw[:, 0, 0, :], 1.0))
            did(g.memset(pw[:, 1, 0, :], 0.0))

            def cmul(o_r, o_i, x_r, x_i, y_r, y_i, t0, t1, t2, t3):
                tt(t0, x_r, y_r, ALU.mult)
                tt(t1, x_i, y_i, ALU.mult)
                tt(t2, x_r, y_i, ALU.mult)
                tt(t3, x_i, y_r, ALU.mult)
                tt(o_r, t0, t1, ALU.subtract)
                tt(o_i, t2, t3, ALU.add)

            for k in range(T):
                cmul(pw[:, 0, k + 1, :], pw[:, 1, k + 1, :], pw[:, 0, k, :], pw[:, 1, k, :], S(AR), S(AI), S(T0), S(T1), S(T2), S(T3))
            did(g.tensor_scalar(pw[:, 2, :, :], pw[:, 0, :, :], sg[:, 0:1], None, ALU.mult))
            did(g.tensor_scalar(pw[:, 3, :, :], pw[:, 1, :, :], sg[:, 0:1], None, ALU.mult))
            did(g.tensor_scalar(pw[:, 4, :, :], pw[:, 2, :, :], -1.0, None, ALU.mult))
            for k in range(int(math.log2(T))):
                cmul(S(CS), S(SN), S(CS), S(SN), S(CS), S(SN), S(T0), S(T1), S(T2), S(T3))
                tt(S(MG), S(MG), S(MG), ALU.mult)
            v3 = lambda t: t.rearrange("p (g h) -> p g h", g=G)
            bc = lambda x: x.unsqueeze(2).to_broadcast([P, G, H])
            did(g.tensor_scalar(S(T2), S(CW), sg[:, 0:1], None, ALU.mult))
            tmp5 = v3(ptmp[:, 0:G * H])
            tt(v3(bb4), v3(b4), bc(S(CQ)), ALU.mult)
            tt(tmp5, v3(b2), bc(S(T2)), ALU.mult)
            tt(v3(bb4), v3(bb4), tmp5, ALU.subtract)
            tt(v3(bb2), v3(b2), bc(S(CQ)), ALU.mult)
            tt(tmp5, v3(b4), bc(S(T2)), ALU.mult)
            tt(v3(bb2), v3(bb2), tmp5, ALU.add)

            n_piece = [0]

            def start_piece(width):
                n = n_piece[0]
                if n >= 2:
                    pool.wait_ge(piece_out[n % 2], 16 * (n // 2))
                return piece[n % 2][:, 0:width]

            def end_piece(ft, at, buf, width):
                n = n_piece[0]
                pool.dma_start(tabs[ft, :, at:at + width], buf).then_inc(piece_out[n % 2], 16)
                n_piece[0] += 1

            for ft in range(KC):
                gs = slice(ft * GT, (ft + 1) * GT)

                def table(row_a, x_a, row_b, x_b, lo, hi, at, rev=False):
                    n = hi - lo
                    w = GT * n * H
                    buf = start_piece(w)
                    o = buf.rearrange("p (g k h) -> p g k h", g=GT, k=n)
                    t = ptmp[:, 0:w].rearrange("p (g k h) -> p g k h", g=GT, k=n)
                    for k in range(n):
                        ko = n - 1 - k if rev else k
                        pk = lambda row: pw[:, row, lo + k, gs].unsqueeze(2).to_broadcast([P, GT, H])
                        tt(o[:, :, ko, :], v3(x_a)[:, gs, :], pk(row_a), ALU.mult)
                        tt(t[:, :, ko, :], v3(x_b)[:, gs, :], pk(row_b), ALU.mult)
                    tt(buf, buf, ptmp[:, 0:w], ALU.subtract)
                    end_piece(ft, at, buf, w)

                table(2, c4, 1, c2, 0, T + 1, 0)
                table(4, c2, 1, c4, 1, T + 1, WCL)
                table(0, bb4, 3, bb2, 0, T, WCL + WP, rev=True)
                cbuf = start_piece(WC)
                n0 = n_piece[0]
                n_piece[0] += 1
                sbuf_ = start_piece(WC)
                n_piece[0] = n0
                cv = cbuf.rearrange("p (g c) -> p g c", g=GT)
                sv = sbuf_.rearrange("p (g c) -> p g c", g=GT)
                did(g.memset(cv[:, :, 0:1], 1.0))
                did(g.memset(sv[:, :, 0:1], 0.0))
                did(g.tensor_copy(cv[:, :, 1:2], small[:, CS, gs].unsqueeze(2)))
                did(g.tensor_copy(sv[:, :, 1:2], small[:, SN, gs].unsqueeze(2)))
                did(g.tensor_copy(small[:, A8R, gs], small[:, CS, gs]))
                did(g.tensor_copy(small[:, A8I, gs], small[:, SN, gs]))
                k = 1
                while k < NCH - 1:
                    n = min(k, NCH - 1 - k)
                    br = small[:, A8R, gs].unsqueeze(2).to_broadcast([P, GT, n])
                    bi = small[:, A8I, gs].unsqueeze(2).to_broadcast([P, GT, n])
                    ta = ptmp[:, 0:GT * n].rearrange("p (g c) -> p g c", g=GT)
                    tb = ptmp[:, GT * 32:GT * 32 + GT * n].rearrange("p (g c) -> p g c", g=GT)
                    tt(ta, cv[:, :, 1:1 + n], br, ALU.mult)
                    tt(tb, sv[:, :, 1:1 + n], bi, ALU.mult)
                    tt(cv[:, :, k + 1:k + 1 + n], ta, tb, ALU.subtract)
                    tt(ta, cv[:, :, 1:1 + n], bi, ALU.mult)
                    tt(tb, sv[:, :, 1:1 + n], br, ALU.mult)
                    tt(sv[:, :, k + 1:k + 1 + n], ta, tb, ALU.add)
                    did(g.tensor_copy(small[:, A8R, gs], cv[:, :, 2 * k if 2 * k < NCH else 1]))
                    did(g.tensor_copy(small[:, A8I, gs], sv[:, :, 2 * k if 2 * k < NCH else 1]))
                    k += n
                did(g.tensor_scalar(sbuf_, sbuf_, sg[:, 0:1], None, ALU.mult))
                end_piece(ft, WCL + 2 * WP, cbuf, WC)
                end_piece(ft, WCL + 2 * WP + WC, sbuf_, WC)
                rbuf = start_piece(WC)
                rv = rbuf.rearrange("p (g c) -> p g c", g=GT)
                did(g.tensor_copy(rv, small[:, MG, gs].unsqueeze(2).to_broadcast([P, GT, NCH])))
                did(g.memset(rv[:, :, 0:1], 0.0))
                end_piece(ft, WCL + 2 * WP + 2 * WC, rbuf, WC)
            n = n_piece[0]
            pool.wait_ge(piece_out[0], 16 * ((n + 1) // 2))
            pool.wait_ge(piece_out[1], 16 * (n // 2))

            did(g.memset(kloc, 0.0))
            did(g.memset(z_g[:, :, 0:1], 0.0))
            did(g.memset(hc[:, 0:2], 0.0))
            count['mix_zeroed'] = steps[0]
            for i in range(KC):
                if i:
                    pool.wait_ge(xf, 4 * i)
                pool.dma_start(tab, tabs[i]).then_inc(tab_landed, 16)
                pool.wait_ge(krow_ready, i + 1)
                pool.wait_ge(ye, 4 * i + 2)
                for t in range(T):
                    pool.dma_start(kloc_g[t * H:(t + 1) * H, :, t * H:P], krow[0:H, :, 0:P - t * H]).then_inc(kloc_landed[1], 16)
                pool.wait_ge(kloc_landed[1], 16 * T * (i + 1))

            pool.wait_ge(yb_ready, KC)
            pool.dma_start(sink_t, a["attn_sinks"].partition_broadcast(P)).then_inc(sink_landed, 16)
            d0 = k_cur[:, 0, 0:KEYS]
            did(g.iota(d0[:, 0:BAND], pattern=[[-1, BAND]], base=CH, channel_multiplier=1, allow_small_or_imprecise_dtypes=True))
            d1 = k_cur[:, 0, KEYS:KEYS + BAND]
            ts(d1, d0[:, 0:BAND], 0.0, ALU.max, 2.0, ALU.mult)
            tt(d0[:, 0:BAND], d1, d0[:, 0:BAND], ALU.subtract)
            did(g.memset(d0[0:CH, P:BAND], 1e36))
            did(g.memset(d0[CH:P, 0:CH], 1e36))
            did(g.memset(d0[:, BAND:KEYS], 0.0))
            for k in range(QP):
                ts(bias[:, k * KEYS:(k + 1) * KEYS], d0, -(2.0 ** (-8.0 * (k + 1) / NH)), ALU.mult)
            did(g.memset(k_win[:, :, 0, 0:CH], 0.0))
            did(g.memset(va[0:CH, 0, :], 0.0))
            count['att_consts'] = steps[0]

        @block.sync
        def _(sp):
            def load_unit(c, i, sources):
                wait(sp, wl_ready, c - 1 + 2 * i)
                for src, b0, nk in sources:
                    m = src.shape[2]
                    sp.dma_start(raw[:, c % 2, b0 * P:b0 * P + nk * m].rearrange("p (k m) -> p k m", k=nk), src).then_inc(raw_landed[c % 2], 16)

            def by_rows(w):
                return w.rearrange("(k p) f -> p k f", p=P)

            def ffn_loads(n):
                wg, wu, wd, layer = FFW[n]
                u0 = FF[n][0]
                wg, wu, wd = by_rows(wg[layer]), by_rows(wu[layer]), by_rows(wd[layer])
                f0 = 0
                for nf in PART:
                    def gate_up(i):
                        for s in range(2):
                            cols = bass.ds((2 * i + s + f0) * P, P)
                            load_unit(u0 + s, i, [(wg[:, :, cols], 0, KD), (wu[:, :, cols], KD, KD)])

                    def down(i):
                        for s in range(2):
                            cols = bass.ds((2 * i + s) * P, P)
                            load_unit(u0 + nf + s, i, [(wd[:, f0:f0 + nf // 2, cols], 0, nf // 2), (wd[:, f0 + nf // 2:f0 + nf, cols], nf // 2, nf // 2)])

                    gate_up(0)
                    with sp.Fori(1, nf // 2) as i:
                        gate_up(i)
                    with sp.Fori(0, KD // 2) as i:
                        down(i)
                    u0 += nf + KD
                    f0 += nf

            sp.dma_start(v_vec[0:2 * KD, :], a["norm_ff1"].rearrange("l (k p) -> (l k) p", p=P)).then_inc(vec_landed, 16)
            sp.dma_start(v_vec[2 * KD:4 * KD, :], a["norm_mix"].rearrange("l (k p) -> (l k) p", p=P)).then_inc(vec_landed, 16)
            sp.dma_start(v_vec[4 * KD:6 * KD, :], a["norm_ff2"].rearrange("l (k p) -> (l k) p", p=P)).then_inc(vec_landed, 16)
            sp.dma_start(v_vec[V_CONV:V_GLUB, :], a["conv_w"].rearrange("l w (k p) -> (l w k) p", p=P)).then_inc(vec_landed, 16)
            sp.dma_start(v_vec[V_GLUB:V_QN, :], a["glu_b"].rearrange("l (k p) -> (l k) p", p=P)).then_inc(vec_landed, 16)
            for half in range(2):
                sp.dma_start(v_vec[V_QN:V_QN + 1, half * HD:(half + 1) * HD], a["attn_q_norm"]).then_inc(vec_landed, 16)
                sp.dma_start(v_vec[V_KN:V_KN + 1, half * HD:(half + 1) * HD], a["attn_k_norm"]).then_inc(vec_landed, 16)
                sp.dma_start(v_lam[0:G, 0, half * ST:(half + 1) * ST], a["ssm_lambda_re"][0]).then_inc(vec_landed, 16)
                sp.dma_start(v_lam[0:G, 1, half * ST:(half + 1) * ST], a["ssm_lambda_im"][0]).then_inc(vec_landed, 16)
            sp.dma_start(v_meta[0:META, :], a["meta_tokens"]).then_inc(x_landed, 16)
            sp.dma_start(v_xs, a["x"][0].rearrange("(t p) d -> p t d", p=P)).then_inc(x_landed, 16)

            ffn_loads(0)
            w_in = by_rows(a["even_w_in"][0])
            for i in range(KC):
                for s, (c0, c1) in enumerate(((3 * DC, 2 * DC), (0, DC))):
                    load_unit(MIX[0] + s, i, [(w_in[:, :, c0 + i * P:c0 + (i + 1) * P], 0, KD), (w_in[:, :, c1 + i * P:c1 + (i + 1) * P], KD, KD)])
            glu = by_rows(a["glu_w"][0])
            load_unit(GLU[0], 0, [(glu[:, 0:KC // 2, :], 0, KC // 2), (glu[:, KC // 2:KC, :], KC // 2 * KC, KC // 2)])

            def two_column_tiles(w, u0, s, i):
                load_unit(u0 + s, i, [(w[:, :, bass.ds((2 * (2 * i + s) + n) * P, P)], n * KD, KD) for n in range(2)])

            w_out = by_rows(a["even_w_out"][0])
            with sp.Fori(0, KD // 4) as i:
                for s in range(2):
                    two_column_tiles(w_out, WOUT[0], s, i)
            ffn_loads(1)
            ffn_loads(2)
            w_qkv = by_rows(a["attn_w_qkv"][0])
            load_unit(ATT[0], 0, [(w_qkv[:, :, NH * HD + n * P:NH * HD + (n + 1) * P], n * KD, KD) for n in range(2)])
            v0 = (NH + NKV) * HD
            load_unit(ATT[0] + 1, 0, [(w_qkv[:, 0:KD // 2, v0:v0 + NKV * HD], 0, KD // 2), (w_qkv[:, KD // 2:KD, v0:v0 + NKV * HD], KD, KD // 2)])
            with sp.Fori(0, NKV // 2) as i:
                for s in range(2):
                    two_column_tiles(w_qkv, ATT[0] + 2, s, i)
            w_o = by_rows(a["attn_w_o"][0])
            with sp.Fori(0, KD // 4) as i:
                for s in range(2):
                    two_column_tiles(w_o, WO[0], s, i)
            ffn_loads(3)
            for d in range(KD):
                sp.wait_ge(fin_evac, d + 1)
                sp.dma_start(out[0, :, d * P:(d + 1) * P].rearrange("(t p) f -> p t f", p=P),
                             arena[:, d * 512:(d + 1) * 512].rearrange("p (t f) -> p t f", t=NT)).then_inc(out_done, 16)
            sp.wait_ge(out_done, 16 * KD)


        @block.tensor
        def _(pe):
            def mm3(pair, slot, blocks, x_h, x_l, k0, col, before_last=None, n_last=1):
                c0, nh, nb = col
                n = len(blocks)
                for k, b in enumerate(blocks):
                    if k == n - n_last and before_last:
                        before_last()
                    for q, (w, x) in enumerate(((wh, x_h), (wh, x_l), (wl, x_h))):
                        for hf in range(nb):
                            last = nc.tensor.matmul(ps[:, 2 * pair + hf, 0:nh], w[:, slot, b * P:(b + 1) * P],
                                                    x[:, k0 + k, c0 + hf * nh:c0 + (hf + 1) * nh],
                                                    start=(k == 0 and q == 0), stop=(k == n - 1 and q == 2))
                return last

            def token_sums(m, col):
                c0, nh, nb = col
                pe.wait_ge(ssq_step, (KD + 1) * (m + 1))
                for hf in range(nb):
                    last = nc.tensor.matmul(ps[:, 4 + hf, 0:nh], ones[:], ssq[:, c0 + hf * nh:c0 + (hf + 1) * nh], start=True, stop=True)
                last.then_inc(ssum_full, 1)

            def x_job(u, j, pair, slot, blocks, col, m=None, new_unit=True):
                if new_unit:
                    pe.wait_ge(wl_ready, u + 1)
                wait(pe, tile_evac, j - 1)
                before = None
                if m is not None:
                    pe.wait_ge(x_ready, KD * m + KD - 1)
                    before = lambda: pe.wait_ge(x_ready, KD * m + KD)
                mm3(pair, slot, blocks, xh, xl, 0, col, before).then_inc(tile_full, 1)

            def ffn(n, col):
                m = FFNORM[n]
                u0, j0 = FF[n]
                done = 0
                for part, nf in enumerate(PART):
                    def gate_up(i, m=None):
                        for s in range(2):
                            u, j = u0 + s + 2 * i, j0 + 2 * s + 4 * i
                            x_job(u, j, 0, (u0 + s) % 2, range(KD), col, m if s == 0 else None)
                            if m is not None and s == 0:
                                token_sums(m, col)
                            x_job(u, j + 1, 1, (u0 + s) % 2, range(KD, 2 * KD), col, new_unit=False)

                    gate_up(0, m if part == 0 else None)
                    with pe.Fori(1, nf // 2) as i:
                        gate_up(i)
                    u0 += nf
                    j0 += 2 * nf
                    done += nf
                    with pe.Fori(0, KD // 2) as i:
                        for s in range(2):
                            pe.wait_ge(wl_ready, u0 + s + 2 * i + 1)
                            pe.wait_ge(tile_evac, j0 + s + 2 * i - 1)
                            pe.wait_ge(act_ready[n], done - 1)
                            mm3(s, (u0 + s) % 2, range(nf), act_h, act_l, 0, col,
                                lambda: pe.wait_ge(act_ready[n], done)).then_inc(tile_full, 1)
                    u0 += KD
                    j0 += KD

            X = ps[:, 4:6, :].rearrange("p b n -> p (b n)")
            Y = ps[:, 6:8, :].rearrange("p b n -> p (b n)")

            pe.wait_ge(consts, 8)
            pe.wait_ge(vec_landed, 13 * 16)
            nc.tensor.transpose(X[:, 0:NV], v_vec[0:NV, :], ident[0:NV, 0:NV])
            for c in range(2):
                last = nc.tensor.transpose(X[:, P * (c + 1):P * (c + 1) + G], v_lam[0:G, c, :], ident[0:G, 0:G])
            last.then_inc(init_full, 1)
            pe.wait_ge(x_landed, 32)
            for d in range(KD):
                bank = 6 if d % 2 == 0 else 4
                wait(pe, init_evac, d)
                for t in range(NT):
                    nc.tensor.transpose(ps[:, bank, t * P:(t + 1) * P], v_xs[:, t, d * P:(d + 1) * P], ident[:])
                nc.tensor.transpose(ps[:, bank + 1, 0:META], v_meta[0:META, d * P:(d + 1) * P], ident[0:META, 0:META]).then_inc(init_full, 1)
            pe.wait_ge(init_evac, KD)
            pe.wait_ge(par_landed, 160)
            for b, v in ((6, v_c4), (7, v_c2)):
                for t in range(4):
                    last = nc.tensor.transpose(ps[:, b, t * P:(t + 1) * P], v[:, t, :], ident[:])
            last.then_inc(init_full, 1)

            ffn(0, ALL)

            def ssm_out(i):
                pe.wait_ge(z_ready, 2 * i + 2)
                pe.wait_ge(kloc_landed[1], 16 * T * (i + 1))
                pe.wait_ge(xe, 4 * i + 3)
                for g in range(GT):
                    o = X[0:NCH, g * P:(g + 1) * P]
                    nc.tensor.matmul(o, u_g[:, g, :], kloc_g[:, g, :], start=True, stop=False)
                    nc.tensor.matmul(o, z_g[:, g, :], cl[:, g, H:(T + 1) * H], start=False, stop=False)
                    last = nc.tensor.matmul(o, zs_g[:, g, :], cl2[:, g, :], start=False, stop=True)
                last.then_inc(xf, 1)

            def y_features(i):
                pe.wait_ge(xe, 4 * i + 4)
                pe.wait_ge(ye, 4 * i + 3)
                yv = yc[0:NCH].rearrange("c (t n) -> c t n", t=T)
                for t in range(T):
                    last = nc.tensor.transpose(ps[:, 6 + t // 4, (t % 4) * NCH:(t % 4 + 1) * NCH],
                                               yv[:, t, :], ident[0:NCH, 0:NCH])
                last.then_inc(yf, 1)

            def mixer(i, m=None):
                u, j = MIX[0] + 2 * i, MIX[1] + 4 * i
                s0 = MIX[0] % 2
                x_job(u, j, 0, s0, range(KD), ALL, m)
                if m is not None:
                    token_sums(m, ALL)
                else:
                    ssm_out(i - 1)
                x_job(u, j + 1, 1, s0, range(KD, 2 * KD), ALL, new_unit=False)
                if m is None:
                    y_features(i - 1)
                pe.wait_ge(tile_evac, j + 1)
                wait(pe, xe, 4 * i)
                if m is not None:
                    pe.wait_ge(var_ready, m + 1)
                uv = u_t.rearrange("p (c t) -> p c t", t=T)
                for t in range(T):
                    last = nc.tensor.transpose(X[0:NCH, t * P:(t + 1) * P], uv[:, :, t], ident[:])
                last.then_inc(xf, 1)
                x_job(u + 1, j + 2, 0, 1 - s0, range(KD), ALL)
                pe.wait_ge(xe, 4 * i + 1)
                wait(pe, ye, 4 * i)
                for g in range(GT):
                    last = nc.tensor.transpose(ps[:, 6 + g // 4, (g % 4) * NCH:(g % 4 + 1) * NCH],
                                               uc4[0:NCH, g, :], ident[0:NCH, 0:NCH])
                last.then_inc(yf, 1)
                pe.wait_ge(tab_landed, 16 * (i + 1))
                for g in range(GT):
                    last = nc.tensor.transpose(X[:, g * P:(g + 1) * P], bl[:, g, :], ident[:])
                last.then_inc(xf, 1)
                x_job(u + 1, j + 3, 1, 1 - s0, range(KD, 2 * KD), ALL, new_unit=False)
                pe.wait_ge(ye, 4 * i + 1)
                for g in range(GT):
                    last = nc.tensor.matmul(Y[0:H, g * P:(g + 1) * P], bl[:, g, (T - 1) * H:T * H], cl[:, g, 0:T * H], start=True, stop=True)
                last.then_inc(yf, 1)
                pe.wait_ge(xe, 4 * i + 2)
                for g in range(GT):
                    last = nc.tensor.matmul(ps[:, 4 + g // 4, (g % 4) * NCH:(g % 4 + 1) * NCH], blt_g[:, g, :], u_g[:, g, :], start=True, stop=True)
                last.then_inc(xf, 1)
                pe.wait_ge(ye, 4 * i + 2)
                for g in range(GT):
                    o = ps[:, 6 + g // 4, (g % 4) * NCH:(g % 4 + 1) * NCH]
                    nc.tensor.matmul(o[0:ST], blt_g[:, g, ST:P], u_g[:, g, :], start=True, stop=True)
                    last = nc.tensor.matmul(o[ST:P], blt_g[:, g, 0:ST], u_g[:, g, :], start=True, stop=True)
                last.then_inc(yf, 1)

            mixer(0, 1)
            with pe.Fori(1, KC) as i:
                mixer(i)
            ssm_out(KC - 1)
            y_features(KC - 1)
            pe.wait_ge(wl_ready, GLU[0] + 1)
            for k in range(KC):
                j = GLU[1] + k
                pe.wait_ge(tile_evac, j - 1)
                pe.wait_ge(yt_ready, KC)
                mm3(k % 2, GLU[0] % 2, range(k, KC * KC, KC), act_h, act_l, 2 * KC, ALL).then_inc(tile_full, 1)

            def project(u0, j0, col, inputs):
                with pe.Fori(0, KD // 4) as i:
                    for s in range(2):
                        for n in range(2):
                            if n == 0:
                                pe.wait_ge(wl_ready, u0 + s + 2 * i + 1)
                            pe.wait_ge(tile_evac, j0 + 2 * s + n + 4 * i - 1)
                            for sm, c in inputs[0]:
                                pe.wait_ge(sm, c)
                            mm3(n, (u0 + s) % 2, range(n * KD, (n + 1) * KD), act_h, act_l, 0, col,
                                lambda: pe.wait_ge(*inputs[1]), inputs[2]).then_inc(tile_full, 1)

            project(*WOUT, ALL, ([(ya_ready, KC), (yb_ready, KC - 1)], (yb_ready, KC), 1))
            ffn(1, ALL)
            ffn(2, ALL)

            u0, j0 = ATT

            def key_sums(t):
                pe.wait_ge(hn_sq, t + 1)
                for hf in range(2):
                    last = nc.tensor.matmul(ps[:, 4 + 2 * t + hf, 0:ALL[1]], pair_ones[:], (t_b, sq)[t][:, hf * ALL[1]:(hf + 1) * ALL[1]], start=True, stop=True)
                last.then_inc(hn_sum, 1)

            x_job(u0, j0, 0, u0 % 2, range(KD), ALL, 4)
            token_sums(4, ALL)
            x_job(u0, j0 + 1, 1, u0 % 2, range(KD, 2 * KD), ALL, new_unit=False)
            pe.wait_ge(var_ready, 5)
            key_sums(0)
            slot = (u0 + 1) % 2
            pe.wait_ge(wl_ready, u0 + 2)
            VW = NKV * HD

            def v_tile(bank, c0):
                for k in range(KD):
                    for q, (x, w) in enumerate(((xh, wh), (xl, wh), (xh, wl))):
                        last = nc.tensor.matmul(ps[:, bank, 0:VW], x[:, k, c0:c0 + P], w[:, slot, k * VW:(k + 1) * VW],
                                                start=(k == 0 and q == 0), stop=(k == KD - 1 and q == 2))
                return last

            pe.wait_ge(tile_evac, j0 + 1)
            v_tile(0, META)
            key_sums(1)
            v_tile(1, META + P).then_inc(tile_full, 1)
            pe.wait_ge(hn_var, 1)
            pe.wait_ge(r_ready, 5)
            for t in range(NT):
                nc.tensor.matmul(ps[:, 5, t:t + 1], r[0:1, META + t * P:META + (t + 1) * P], ones[0:1, 0:1], start=True, stop=True)
            nc.tensor.matmul(ps[0:META, 5, NT:NT + 1], r[0:1, 0:META], ones[0:1, 0:1], start=True, stop=True).then_inc(rtok_full, 1)
            v_tile(4, 0).then_inc(vmeta_full, 1)
            pe.wait_ge(tile_evac, j0 + 2)
            v_tile(2, META + 2 * P)
            v_tile(3, META + 3 * P).then_inc(tile_full, 1)

            def query_part(g, t, half):
                slot = (u0 + g) % 2
                if half == 0:
                    if t == 0:
                        pe.wait_ge(wl_ready, u0 + 2 + g + 1)
                    if g:
                        pe.wait_ge(qn_step, QSTEPS * (g - 1) + 2)
                        pe.wait_ge(tile_evac, j0 + 4 + 2 * g + t - 1)
                c0, width, _ = REAL
                for k in range(half * KD // 2, (half + 1) * KD // 2):
                    b = t * KD + k
                    for q, (w, x) in enumerate(((wh, xh), (wh, xl), (wl, xh))):
                        last = nc.tensor.matmul(ps[:, 2 * t, :], w[:, slot, b * P:(b + 1) * P], x[:, k, c0:c0 + width],
                                                start=(k == 0 and q == 0), stop=(k == KD - 1 and q == 2))
                if half:
                    last.then_inc(tile_full, 1)

            def query_sums(g, t):
                pe.wait_ge(hn_sq, 2 + 2 * g + t + 1)
                pe.wait_ge(tile_evac, j0 + 4 + 2 * g + t + 1)
                for b in range(NT):
                    last = nc.tensor.matmul(ps[:, 2 * t, 2 * b:2 * b + 2], (t_b, sq)[t][:, b * P:(b + 1) * P], pair_ones[:, 0:P:HD], start=True, stop=True)
                last.then_inc(hn_sum, 1)

            def scores(n):
                g, j = divmod(n, NT)
                if j == 0:
                    pe.wait_ge(qn_step, QSTEPS * (g + 1))
                    pe.wait_ge(k_cur_ready, g + 1)
                if n:
                    pe.wait_ge(s_evac, n)
                for k in range(QP):
                    rows = slice((k % 2) * HD, (k % 2 + 1) * HD)
                    last = nc.tensor.matmul(ps[:, 4 + k % 2, (k // 2) * KEYS:(k // 2 + 1) * KEYS], q_hat[rows, g % 2, k // 2, j * P:(j + 1) * P],
                                            k_cur[rows, g % 2, j * KEYS:(j + 1) * KEYS], start=True, stop=True)
                last.then_inc(s_full, 1)

            def probs_t(n):
                pe.wait_ge(pn_ready, n + 1)
                if n:
                    pe.wait_ge(pt_evac, n)
                for k in range(QP):
                    p = s_all[:, n % 2, k * KEYS:(k + 1) * KEYS]
                    at = ((k % 2) * 2 + k // 2) * P
                    nc.tensor.transpose(ps[:, 6, at:at + P], p[:, 0:P], ident[:])
                    last = nc.tensor.transpose(ps[0:KB, 7, at:at + P], p[:, P:KEYS], ident[:])
                last.then_inc(pt_full, 1)

            def values(n):
                g, j = divmod(n, NT)
                pe.wait_ge(pt_evac, n + 1)
                if n >= 2:
                    pe.wait_ge(ol_done, n - 1)
                cols = slice(g * HD, (g + 1) * HD)
                for hh in range(2):
                    o = ps[hh * HD:(hh + 1) * HD, 1 + 2 * (j % 2), 0:2 * P]
                    nc.tensor.matmul(o, va[:, j, cols], p_a[:, hh * 2 * P:(hh + 1) * 2 * P], start=True, stop=False)
                    last = nc.tensor.matmul(o, vb[0:KB, j, cols], p_b[0:KB, hh * 2 * P:(hh + 1) * 2 * P], start=False, stop=True)
                last.then_inc(o_full, 1)

            pe.wait_ge(tile_evac, j0 + 4)
            for t in range(2):
                for half in range(2):
                    query_part(0, t, half)
            for t in range(2):
                query_sums(0, t)
            query_part(1, 0, 0)
            query_part(1, 0, 1)
            pe.wait_ge(v_ready, 1)
            scores(0)
            query_part(1, 1, 0)
            scores(1)
            query_part(1, 1, 1)
            for n in range(NB):
                probs_t(n)
                if n % NT == 0 and 1 + n // NT < NKV:
                    query_sums(1 + n // NT, 0)
                    query_sums(1 + n // NT, 1)
                if n + 2 < NB:
                    scores(n + 2)
                if 2 + n // NT < NKV:
                    query_part(2 + n // NT, n % NT // 2, n % 2)
                values(n)

            project(*WO, REAL, ([(ol_done, NB - NT)], (ol_done, NB), 2))
            ffn(3, REAL)
            for d in range(KD):
                pe.wait_ge(tile_evac, FF[3][1] + FJ - KD + d + 1)
                wait(pe, fin_evac, d - 3)
                for t in range(NT):
                    last = nc.tensor.transpose(ps[:, 4 + d % 4, t * P:(t + 1) * P], h[:, d, META + t * P:META + (t + 1) * P], ident[:])
                last.then_inc(fin_full, 1)

        @block.scalar
        def _(act):
            def split_high(c, i, jobs):
                act.wait_ge(raw_landed[c % 2], 32 * (c // 2 + 1) + 32 * i)
                wait(act, tile_full, jobs)
                nc.scalar.activation(wh[:, c % 2, :], raw[:, c % 2, :], ACT.Copy).then_inc(wh_ready, 1)

            def norm_input(m, d, col, evacuated):
                cols = span(col)
                act.wait_ge(*evacuated)
                nc.scalar.activation(sq[:, cols], h[:, d, cols], ACT.Square).then_inc(sq_done, 1)
                nc.scalar.activation(xh[:, d, cols], h[:, d, cols], ACT.Copy,
                                     scale=vec[:, GAIN[m] + d:GAIN[m] + d + 1] if isinstance(d, int) else vec[:, bass.ds(d + GAIN[m], 1)]).then_inc(xh_done, 1)

            def root_mean(m, col):
                cols = span(col)
                act.wait_ge(var_ready, m + 1)
                nc.scalar.activation(sq[:, cols], sq[:, cols], ACT.Sqrt).then_inc(sd_ready, 1)

            def ffn(n, col):
                m = FFNORM[n]
                u0, j0 = FF[n]
                cols = span(col)
                done = 0
                for part, nf in enumerate(PART):
                    def gate_up(i, first=False):
                        for s in range(2):
                            j, k = j0 + 2 * s + 4 * i, done + s + 2 * i
                            split_high(u0 + s + 1, i, j)
                            if first and s == 0:
                                root_mean(m, col)
                            act.wait_ge(tile_evac, j + 1)
                            nc.scalar.activation(t_b[:, cols], t_a[:, cols], ACT.Silu).then_inc(silu_done[n], 1)
                            act.wait_ge(gated[n], k + 1)
                            nc.scalar.activation(act_h[:, s + 2 * i, cols], t_c[:, cols], ACT.Copy).then_inc(act_h_done[n], 1)

                    gate_up(0, part == 0)
                    with act.Fori(1, nf // 2) as i:
                        gate_up(i)
                    u0 += nf
                    j0 += 2 * nf
                    done += nf

                    def down(i, last=False):
                        for s in range(2):
                            if not (last and s == 1):
                                split_high(u0 + s + 1, i, j0 + s + 2 * i)
                            if part == 1 and n < 3:
                                norm_input(m + 1, s + 2 * i, col, (tile_evac, j0 + s + 2 * i + 1))

                    if part == 1 and n == 3:
                        with act.Fori(0, KD // 2 - 1) as i:
                            down(i)
                        down(KD // 2 - 1, True)
                    else:
                        with act.Fori(0, KD // 2) as i:
                            down(i)
                    u0 += KD
                    j0 += KD

            for d in range(KD):
                norm_input(0, d, ALL, (init_evac, d + 2))
            split_high(0, 0, 0)
            ffn(0, ALL)

            X = ps[:, 4:6, :].rearrange("p b n -> p (b n)")

            def gelu(i):
                act.wait_ge(xf, 4 * i + 4)
                nc.scalar.activation(yc[0:NCH].rearrange("c (t g h) -> c g t h", t=T, g=GT),
                                     X[0:NCH, :].rearrange("c (g t h) -> c g t h", t=T, g=GT), ACT.Gelu_apprx_tanh).then_inc(xe, 1)

            def y_high(i):
                act.wait_ge(ye, 4 * i + 4)
                nc.scalar.activation(act_h[:, 2 * KC + i, :], y_t, ACT.Copy).then_inc(yth_done, 1)

            def mixer(i, first):
                u, j = MIX[0] + 2 * i, MIX[1] + 4 * i
                split_high(MIX[0] + 1, i, j)
                if first:
                    root_mean(1, ALL)
                else:
                    gelu(i - 1)
                act.wait_ge(xf, 4 * i + 1)
                nc.scalar.activation(uc4[0:NCH].rearrange("c g (t h) -> c t g h", t=T),
                                     X[0:NCH, :].rearrange("c (t g h) -> c t g h", t=T, g=GT), ACT.Copy).then_inc(xe, 1)
                if not first:
                    y_high(i - 1)
                act.wait_ge(xf, 4 * i + 2)
                nc.scalar.activation(blt, X, ACT.Copy).then_inc(xe, 1)
                split_high(MIX[0] + 2, i, j + 2)
                act.wait_ge(dve_mix, 5 * i + 5)
                nc.scalar.activation(act_h[:, i, :], t_a[:], ACT.Copy).then_inc(yah_done, 1)

            mixer(0, True)
            with act.Fori(1, KC) as i:
                mixer(i, False)
            gelu(KC - 1)
            y_high(KC - 1)
            split_high(WOUT[0], 0, GLU[1])
            for k in range(KC):
                act.wait_ge(tile_full, GLU[1] + k + 1)
                nc.scalar.activation(halves(t_b, ALL), banks(2 * (k % 2), ALL), ACT.Sigmoid,
                                     bias=vec[:, V_GLUB + k:V_GLUB + k + 1]).then_inc(tile_evac, 1)
                act.wait_ge(yb_prod, k + 1)
                nc.scalar.activation(act_h[:, KC + k, :], t_a[:], ACT.Copy).then_inc(ybh_done, 1)

            def project(u0, j0, col, m):
                with act.Fori(0, KD // 4) as i:
                    for s in range(2):
                        split_high(u0 + s + 1, i, j0 + 2 * s + 4 * i)
                        for n in range(2):
                            norm_input(m, 2 * s + n + 4 * i, col, (tile_evac, j0 + 2 * s + n + 4 * i + 1))

            project(*WOUT, ALL, 2)
            ffn(1, ALL)
            ffn(2, ALL)

            u0, j0 = ATT
            split_high(u0 + 1, 0, j0)
            root_mean(4, ALL)
            for t in range(2):
                act.wait_ge(tile_evac, j0 + t + 1)
                if t == 1:
                    act.wait_ge(r_ready, 5)
                nc.scalar.activation((t_b, sq)[t][:], (t_a, t_c)[t][:], ACT.Square).then_inc(hn_sq, 1)
            split_high(u0 + 2, 0, j0 + 2)
            for t in range(2):
                act.wait_ge(hn_var, t + 1)
                nc.scalar.activation(s_all[:, t, 0:L], (t_b, sq)[t][:], ACT.Sqrt).then_inc(hn_sd, 1)
            act.wait_ge(rtok_ready, 2)
            act.wait_ge(tile_full, j0 + 4)
            for t in range(2, NT):
                for out_v, rows in value_windows(t):
                    last = nc.scalar.activation(out_v, ps[rows, t, 0:NKV * HD], ACT.Copy, scale=rtok[rows, t:t + 1])
            last.then_inc(tile_evac, 1)
            split_high(u0 + 3, 0, j0 + 4)

            def query_tile(g, t):
                act.wait_ge(tile_full, j0 + 4 + 2 * g + t + 1)
                if g == 0:
                    act.wait_ge(hn_ready, t + 1)
                nc.scalar.activation((t_b, sq)[t][:, 0:SEQ], ps[:, 2 * t, :], ACT.Square).then_inc(hn_sq, 1)
                nc.scalar.activation(q_hat[:, g % 2, t, :], ps[:, 2 * t, :], ACT.Copy, scale=vec[:, V_QN:V_QN + 1]).then_inc(tile_evac, 1)

            def exps(n):
                st = stat[:, n % 2]
                act.wait_ge(nm_ready, n + 1)
                for k in range(QP):
                    p = s_all[:, n % 2, k * KEYS:(k + 1) * KEYS]
                    nc.scalar.activation(p, p, ACT.Exp, bias=st[:, 2, k:k + 1], accum_out=st[:, 4, k:k + 1])
                act.wait_ge(at_step, norm_steps(n))
                nc.scalar.activation(st[:, 5, 0:QP], st[:, 3, 0:QP], ACT.Exp).then_inc(es_ready, 1)

            def probs(n):
                act.wait_ge(pt_full, n + 1)
                nc.scalar.activation(p_a, ps[:, 6, :], ACT.Copy)
                nc.scalar.activation(p_b[0:KB, :], ps[0:KB, 7, :], ACT.Copy).then_inc(pt_evac, 1)

            def out_high(n):
                g, j = divmod(n, NT)
                act.wait_ge(o_full, n + 1)
                nc.scalar.activation(act_h[:, 2 * g:2 * g + 2, META + j * P:META + (j + 1) * P],
                                     ps[:, 1 + 2 * (j % 2), 0:2 * P].rearrange("p (t n) -> p t n", t=2), ACT.Copy).then_inc(oh_done, 1)

            for t in range(2):
                query_tile(0, t)
            split_high(u0 + 4, 0, j0 + 6)
            query_tile(1, 0)
            exps(0)
            query_tile(1, 1)
            exps(1)
            for n in range(NB):
                g = n // NT
                probs(n)
                if n + 2 < NB:
                    exps(n + 2)
                if g + 2 < NKV and n % 2 == 1:
                    query_tile(g + 2, n % NT // 2)
                out_high(n)
                if n % NT == 0 and g + 3 <= NKV:
                    split_high(u0 + 4 + (g + 1) % 2, (g + 1) // 2, j0 + 4 + 2 * (g + 2))
            project(*WO, REAL, 5)
            ffn(3, REAL)
            for d in range(1, KD, 2):
                act.wait_ge(fin_full, d + 1)
                act.wait_ge(fin_evac, d)
                nc.scalar.activation(arena[:, d * 512:(d + 1) * 512], ps[:, 4 + d % 4, :], ACT.Copy).then_inc(fin_evac, 1)

        @block.vector
        def _(dve):
            v = nc.vector

            def split_low(c, i):
                dve.wait_ge(wh_ready, c + 2 * i + 1)
                v.tensor_tensor(wl[:, c % 2, :], raw[:, c % 2, :], wh[:, c % 2, :].bitcast(F32), ALU.subtract).then_inc(wl_ready, 1)

            def tile(pair, col):
                return banks(2 * pair, col)

            def clear_sums(m):
                v.memset(ssq[:], 0.0).then_inc(ssq_step, 1)

            def norm_input(m, d, col):
                cols = span(col)
                dve.wait_ge(sq_done, KD * m + d + 1)
                dve.wait_ge(ssq_step, (KD + 1) * m + d + 1)
                v.tensor_tensor(ssq[:, cols], ssq[:, cols], sq[:, cols], ALU.add).then_inc(ssq_step, 1)
                dve.wait_ge(xh_done, KD * m + d + 1)
                gain = vec[:, GAIN[m] + d:GAIN[m] + d + 1] if isinstance(d, int) else vec[:, bass.ds(d + GAIN[m], 1)]
                v.scalar_tensor_tensor(xl[:, d, cols], h[:, d, cols], gain, xh[:, d, cols].bitcast(F32), ALU.mult, ALU.subtract).then_inc(x_ready, 1)

            def rms(m, col):
                cols = span(col)
                dve.wait_ge(ssum_full, m + 1)
                v.tensor_scalar(halves(sq, col), banks(4, col), 1.0 / DM, EPS, ALU.mult, ALU.add).then_inc(var_ready, 1)
                dve.wait_ge(sd_ready, m + 1)
                v.reciprocal(r[:, cols], sq[:, cols]).then_inc(r_ready, 1)
                dve.wait_ge(r_ready, m + 1)

            def residual(d, j, pair, scale, m, col):
                dve.wait_ge(tile_full, j + 1)
                hd = halves(h[:, d, :], col)
                v.scalar_tensor_tensor(hd, tile(pair, col), scale, hd, ALU.mult, ALU.add).then_inc(tile_evac, 1)
                if m is not None:
                    norm_input(m, d, col)

            def ffn(n, col):
                m = FFNORM[n]
                u0, j0 = FF[n]
                cols = span(col)
                done = 0
                for part, nf in enumerate(PART):
                    def gate_up(i, first=False):
                        for s in range(2):
                            j, k = j0 + 2 * s + 4 * i, done + s + 2 * i
                            split_low(u0 + s + 1, i)
                            if first and s == 0:
                                rms(m, col)
                            dve.wait_ge(tile_full, j + 1)
                            v.tensor_tensor(halves(t_a, col), tile(0, col), halves(r, col), ALU.mult).then_inc(tile_evac, 1)
                            dve.wait_ge(tile_full, j + 2)
                            wait(dve, act_ready[n], k)
                            v.tensor_tensor(halves(t_c, col), tile(1, col), halves(r, col), ALU.mult).then_inc(tile_evac, 1)
                            dve.wait_ge(tile_evac, j + 2)
                            dve.wait_ge(silu_done[n], k + 1)
                            v.tensor_tensor(t_c[:, cols], t_c[:, cols], t_b[:, cols], ALU.mult).then_inc(gated[n], 1)
                            dve.wait_ge(act_h_done[n], k + 1)
                            v.tensor_tensor(act_l[:, s + 2 * i, cols], t_c[:, cols], act_h[:, s + 2 * i, cols].bitcast(F32), ALU.subtract).then_inc(act_ready[n], 1)

                    gate_up(0, part == 0)
                    with dve.Fori(1, nf // 2) as i:
                        gate_up(i)
                    u0 += nf
                    j0 += 2 * nf
                    done += nf
                    more = m + 1 if part == 1 and n < 3 else None
                    if more is not None:
                        clear_sums(more)

                    def down(i, last=False):
                        for s in range(2):
                            if not (last and s == 1):
                                split_low(u0 + s + 1, i)
                            residual(s + 2 * i, j0 + s + 2 * i, s, 0.5, more, col)

                    if part == 1 and n == 3:
                        with dve.Fori(0, KD // 2 - 1) as i:
                            down(i)
                        down(KD // 2 - 1, True)
                    else:
                        with dve.Fori(0, KD // 2) as i:
                            down(i)
                    u0 += KD
                    j0 += KD

            X = ps[:, 4:6, :].rearrange("p b n -> p (b n)")
            dve.wait_ge(init_full, 1)
            v.tensor_copy(vec[:], X[:, 0:NV])
            v.tensor_copy(small[:, 1, :], X[:, P:P + G])
            v.tensor_copy(small[:, 2, :], X[:, 2 * P:2 * P + G]).then_inc(init_evac, 1)
            dve.wait_ge(init_evac, 1)
            v.tensor_scalar(vec[:, V_QN:V_QN + 1], vec[:, V_QN:V_QN + 1], float(HD) ** -0.5, None, ALU.mult)
            clear_sums(0)
            for d in range(KD):
                bank = 6 if d % 2 == 0 else 4
                dve.wait_ge(init_full, d + 2)
                v.tensor_copy(h[:, d, META:L], ps[:, bank, :])
                v.tensor_copy(h[:, d, 0:META], ps[:, bank + 1, 0:META]).then_inc(init_evac, 1)
                norm_input(0, d, ALL)
            dve.wait_ge(init_full, KD + 2)
            v.tensor_copy(c4, ps[:, 6, :])
            v.tensor_copy(c2, ps[:, 7, :]).then_inc(init_evac, 1)
            split_low(0, 0)
            ffn(0, ALL)

            def step_mix(ins, n):
                ins.then_inc(dve_mix, 1)
                dve.wait_ge(dve_mix, n)

            def states(i):
                wait(dve, xf, 4 * i)
                four = lambda x: x.rearrange("p (b g c) -> p b g c", b=2, g=4)
                src = lambda b: ps[:, b:b + 2, 0:4 * NCH].rearrange("p b (g c) -> p b g c", g=4)[:, :, :, 0:NCH - 1]
                dve.wait_ge(tab_landed, 16 * (i + 1))
                dve.wait_ge(xf, 4 * i + 3)
                v.tensor_tensor(four(sq[:])[:, :, :, 1:NCH], src(4), four(cos_t)[:, :, :, 1:NCH], ALU.mult).then_inc(xe, 1)
                dve.wait_ge(yf, 4 * i + 3)
                v.tensor_tensor(four(zs)[:, :, :, 1:NCH], src(6), four(sin_t)[:, :, :, 1:NCH], ALU.mult).then_inc(ye, 1)
                dve.wait_ge(xe, 4 * i + 3)
                dve.wait_ge(ye, 4 * i + 3)
                v.tensor_tensor(z_g[:, :, 1:NCH], sq[:].rearrange("p (g c) -> p g c", g=GT)[:, :, 1:NCH], zs_g[:, :, 1:NCH], ALU.add).then_inc(z_step, 1)
                dve.wait_ge(z_step, 2 * i + 1)
                v.tensor_tensor_scan(zs, rho_t, z, 0.0, ALU.mult, ALU.add).then_inc(z_step, 1)
                dve.wait_ge(z_step, 2 * i + 2)
                v.tensor_tensor(z, zs, cos_t, ALU.mult).then_inc(z_ready, 1)
                v.tensor_tensor(zs, zs, sin_t, ALU.mult).then_inc(z_ready, 1)

            def y_low(i):
                dve.wait_ge(yf, 4 * i + 4)
                wait(dve, yth_done, i)
                v.tensor_copy(y_t.rearrange("p (c b t) -> p b t c", b=2, t=4),
                              ps[:, 6:8, 0:4 * NCH].rearrange("p b (t c) -> p b t c", t=4)).then_inc(ye, 1)
                dve.wait_ge(yth_done, i + 1)
                v.tensor_tensor(act_l[:, 2 * KC + i, :], y_t, act_h[:, 2 * KC + i, :].bitcast(F32), ALU.subtract).then_inc(yt_ready, 1)

            def mixer(i, first):
                u, j = MIX[0] + 2 * i, MIX[1] + 4 * i
                if first:
                    dve.wait_ge(prep, count["mix_zeroed"])
                else:
                    states(i - 1)
                split_low(MIX[0] + 1, i)
                if first:
                    rms(1, ALL)
                dve.wait_ge(tile_full, j + 1)
                v.tensor_tensor(halves(u_t, ALL), tile(0, ALL), halves(r, ALL), ALU.mult).then_inc(tile_evac, 1)
                dve.wait_ge(tile_full, j + 2)
                v.tensor_tensor(halves(t_b, ALL), tile(1, ALL), halves(r, ALL), ALU.mult).then_inc(tile_evac, 1)
                if not first:
                    y_low(i - 1)
                dve.wait_ge(tile_full, j + 3)
                v.tensor_tensor(halves(t_a, ALL), tile(0, ALL), halves(r, ALL), ALU.mult).then_inc(tile_evac, 1)
                dve.wait_ge(tile_evac, j + 3)
                step_mix(v.tensor_tensor(hc[:, 2:L + 2], t_a[:], t_b[:], ALU.mult), 5 * i + 1)
                w = lambda k: (vec[:, V_CONV + k * KC + i:V_CONV + k * KC + i + 1] if isinstance(i, int)
                               else vec[:, bass.ds(i + (V_CONV + k * KC), 1)])
                step_mix(v.tensor_scalar(t_c[:], hc[:, 0:L], w(0), None, ALU.mult), 5 * i + 2)
                for k in (1, 2):
                    step_mix(v.scalar_tensor_tensor(t_c[:], hc[:, k:L + k], w(k), t_c[:], ALU.mult, ALU.add), 5 * i + 2 + k)
                dve.wait_ge(yf, 4 * i + 1)
                v.tensor_copy(u_c.rearrange("p (b n) -> p b n", b=2), ps[:, 6:8, 0:4 * NCH]).then_inc(ye, 1)
                split_low(MIX[0] + 2, i)
                dve.wait_ge(tile_full, j + 4)
                v.tensor_tensor(halves(t_a, ALL), tile(1, ALL), halves(r, ALL), ALU.mult).then_inc(tile_evac, 1)
                dve.wait_ge(tile_evac, j + 4)
                v.tensor_tensor(t_a[:], t_a[:], t_c[:], ALU.mult).then_inc(dve_mix, 1)
                dve.wait_ge(yah_done, i + 1)
                v.tensor_tensor(act_l[:, i, :], t_a[:], act_h[:, i, :].bitcast(F32), ALU.subtract).then_inc(ya_ready, 1)
                dve.wait_ge(yf, 4 * i + 2)
                yk = ps[0:H, 6:8, :].rearrange("p b n -> p (b n)").rearrange("p (g n) -> p g n", g=GT)
                v.tensor_copy(krow[0:H, :, H:P], yk[:, :, H:P]).then_inc(krow_ready, 1)
                v.tensor_tensor(krow[0:H, :, 0:H], yk[:, :, 0:H], d16[:, bass.ds(i * GT, GT), :], ALU.add).then_inc(ye, 1)

            mixer(0, True)
            with dve.Fori(1, KC) as i:
                mixer(i, False)
            states(KC - 1)
            y_low(KC - 1)
            split_low(WOUT[0], 0)
            for k in range(KC):
                wait(dve, yb_prod, k)
                v.tensor_tensor(t_c[:], act_h[:, 2 * KC + k, :].bitcast(F32), act_l[:, 2 * KC + k, :].bitcast(F32), ALU.add).then_inc(dve_mix, 1)
                dve.wait_ge(dve_mix, 5 * KC + k + 1)
                dve.wait_ge(tile_evac, GLU[1] + k + 1)
                v.tensor_tensor(t_a[:], t_b[:], t_c[:], ALU.mult).then_inc(yb_prod, 1)
                dve.wait_ge(ybh_done, k + 1)
                v.tensor_tensor(act_l[:, KC + k, :], t_a[:], act_h[:, KC + k, :].bitcast(F32), ALU.subtract).then_inc(yb_ready, 1)

            def project(u0, j0, col, m):
                clear_sums(m)
                with dve.Fori(0, KD // 4) as i:
                    for s in range(2):
                        split_low(u0 + s + 1, i)
                        for n in range(2):
                            residual(2 * s + n + 4 * i, j0 + 2 * s + n + 4 * i, n, 1.0, m, col)

            project(*WOUT, ALL, 2)
            ffn(1, ALL)
            ffn(2, ALL)

            u0, j0 = ATT

            def key_var(t):
                dve.wait_ge(hn_sum, t + 1)
                v.tensor_scalar(halves((t_b, sq)[t], ALL), banks(4 + 2 * t, ALL), 1.0 / HD, EPS, ALU.mult, ALU.add).then_inc(hn_var, 1)

            def key_norm(t):
                k_in, var, y, w = (t_a, t_c)[t], (t_b, sq)[t], s_all[:, t, 0:L], k_cur[:, t, 0:L]
                dve.wait_ge(hn_sd, t + 1)
                v.reciprocal(y, y).then_inc(hn_step, 1)
                dve.wait_ge(hn_step, 4 * t + 1)
                v.tensor_tensor(w, y, y, ALU.mult).then_inc(hn_step, 1)
                dve.wait_ge(hn_step, 4 * t + 2)
                v.scalar_tensor_tensor(w, w, -0.5, var[:], ALU.mult, ALU.mult).then_inc(hn_step, 1)
                dve.wait_ge(hn_step, 4 * t + 3)
                v.scalar_tensor_tensor(y, w, 1.5, y, ALU.add, ALU.mult).then_inc(hn_step, 1)
                dve.wait_ge(hn_step, 4 * t + 4)
                gain = vec[:, V_KN:V_KN + 1]
                by_block = lambda x, lo, nb, a, b: x[:, lo:lo + nb * P].rearrange("p (j n) -> p j n", n=P)[:, :, a:b]
                v.scalar_tensor_tensor(k_win[:, t, :, CH:BAND], by_block(k_in, META, NT, 0, P), gain, by_block(y, META, NT, 0, P), ALU.mult, ALU.mult)
                v.scalar_tensor_tensor(k_win[:, t, 1:NT, 0:CH], by_block(k_in, META + CH, NT - 1, 0, CH), gain, by_block(y, META + CH, NT - 1, 0, CH), ALU.mult, ALU.mult)
                meta = lambda x: x[:, 0:META].unsqueeze(1).to_broadcast([P, NT, META])
                v.scalar_tensor_tensor(k_win[:, t, :, BAND:KEYS], meta(k_in), gain, meta(y), ALU.mult, ALU.mult).then_inc(hn_ready, 1)

            def current_keys(g):
                rows = slice((g % 2) * HD, (g % 2 + 1) * HD)
                if g >= 2:
                    dve.wait_ge(s_full, NT * (g - 1))
                for half in range(2):
                    last = v.tensor_copy(k_cur[half * HD:(half + 1) * HD, g % 2, :], k_win[rows, g // 2, :, :].rearrange("p j n -> p (j n)"))
                last.then_inc(k_cur_ready, 1)

            qn = [0]

            def qstep(ins):
                ins.then_inc(qn_step, 1)
                qn[0] += 1
                dve.wait_ge(qn_step, qn[0])

            by_tb = lambda x: x.rearrange("p (t b h) -> p t b h", t=2, b=NT)

            def query_var(g):
                dve.wait_ge(hn_sum, 2 + 2 * g + 2)
                of_bank = lambda x: x.rearrange("p (b h) -> p b h", b=NT)
                for t in range(2):
                    qstep(v.tensor_tensor(of_bank(nq[:, 0, 2 * NT * t:2 * NT * (t + 1)]), of_bank(ps[:, 2 * t, 0:2 * NT]),
                                          rtok2[:, 0:NT].unsqueeze(2).to_broadcast([P, NT, 2]), ALU.mult))

            def query_norm(g):
                var, y, w = nq[:, 0, :], rq[:, g % 2, :], nq[:, 1, :]
                qstep(v.tensor_scalar(var, var, EPS, None, ALU.add))
                qstep(v.tensor_scalar(y.bitcast(I32), var.bitcast(I32), -0.5, 1597463007.0, ALU.mult, ALU.add))
                for _ in range(3):
                    qstep(v.tensor_tensor(w, y, y, ALU.mult))
                    qstep(v.scalar_tensor_tensor(w, w, -0.5, var, ALU.mult, ALU.mult))
                    qstep(v.scalar_tensor_tensor(y, w, 1.5, y, ALU.add, ALU.mult))
                qstep(v.tensor_tensor(by_tb(y), by_tb(y), rtok[:, 0:NT].unsqueeze(1).unsqueeze(3).to_broadcast([P, 2, NT, 2]), ALU.mult))
                assert qn[0] == QSTEPS * (g + 1)

            split_low(u0 + 1, 0)
            rms(4, ALL)
            for t in range(2):
                dve.wait_ge(tile_full, j0 + t + 1)
                v.tensor_tensor(halves((t_a, t_c)[t], ALL), tile(t, ALL), halves(r, ALL), ALU.mult).then_inc(tile_evac, 1)
            dve.wait_ge(prep, count["att_consts"])
            split_low(u0 + 2, 0)
            key_var(0)
            key_var(1)
            key_norm(0)
            dve.wait_ge(rtok_full, 1)
            v.tensor_copy(rtok[0:META, NT:NT + 1], ps[0:META, 5, NT:NT + 1]).then_inc(rtok_ready, 1)
            v.tensor_copy(rtok[:, 0:NT], ps[:, 5, 0:NT]).then_inc(rtok_ready, 1)
            dve.wait_ge(rtok_ready, 2)
            v.tensor_tensor(rtok2[:, 0:NT], rtok[:, 0:NT], rtok[:, 0:NT], ALU.mult).then_inc(rtok_ready, 1)
            dve.wait_ge(rtok_ready, 3)
            v.tensor_scalar(rtok2[:, 0:NT], rtok2[:, 0:NT], 1.0 / HD, None, ALU.mult).then_inc(rtok_ready, 1)
            dve.wait_ge(tile_full, j0 + 3)
            for t in range(2):
                for out_v, rows in value_windows(t):
                    last = v.tensor_scalar(out_v, ps[rows, t, 0:NKV * HD], rtok[rows, t:t + 1], None, ALU.mult)
            last.then_inc(tile_evac, 1)
            dve.wait_ge(vmeta_full, 1)
            for t in range(NT):
                last = v.tensor_scalar(vb[CH:KB, t, :], ps[0:META, 4, 0:NKV * HD], rtok[0:META, NT:NT + 1], None, ALU.mult)
            last.then_inc(v_ready, 1)
            key_norm(1)
            split_low(u0 + 3, 0)
            current_keys(0)
            dve.wait_ge(rtok_ready, 4)
            dve.wait_ge(sink_landed, 16)
            at = [0]

            def did(ins):
                ins.then_inc(at_step, 1)
                at[0] += 1

            def softmax(n):
                g, j = divmod(n, NT)
                st = stat[:, n % 2]
                if j == 0 and g:
                    dve.wait_ge(bias_ready, g)
                dve.wait_ge(s_full, n + 1)
                if n >= 2:
                    dve.wait_ge(pt_full, n - 1)
                for k in range(QP):
                    col = (k // 2) * 2 * NT + j * 2 + k % 2
                    last = v.scalar_tensor_tensor(s_all[:, j % 2, k * KEYS:(k + 1) * KEYS], ps[:, 4 + k % 2, (k // 2) * KEYS:(k // 2 + 1) * KEYS],
                                                  rq[:, g % 2, col:col + 1], bias[:, k * KEYS:(k + 1) * KEYS], ALU.mult, ALU.add)
                last.then_inc(s_evac, 1)
                dve.wait_ge(s_evac, n + 1)
                s4 = s_all[:, j % 2, :].rearrange("p (k n) -> p k n", k=QP)
                if j == 0:
                    did(v.memset(s4[:, :, 0:CH], -1e30))
                    dve.wait_ge(at_step, at[0])
                did(v.tensor_reduce(st[:, 0, 0:QP], s4, AX_X, ALU.max))
                dve.wait_ge(at_step, at[0])
                sinks = sink_t[:, g * QP:(g + 1) * QP]
                did(v.tensor_tensor(st[:, 1, 0:QP], st[:, 0, 0:QP], sinks, ALU.max))
                dve.wait_ge(at_step, at[0])
                v.tensor_scalar(st[:, 2, 0:QP], st[:, 1, 0:QP], -1.0, None, ALU.mult).then_inc(nm_ready, 1)
                dve.wait_ge(nm_ready, n + 1)
                did(v.tensor_tensor(st[:, 3, 0:QP], st[:, 2, 0:QP], sinks, ALU.add))
                assert at[0] == norm_steps(n)

            def normed(n):
                st = stat[:, n % 2]
                dve.wait_ge(es_ready, n + 1)
                did(v.tensor_tensor(st[:, 6, 0:QP], st[:, 4, 0:QP], st[:, 5, 0:QP], ALU.add))
                dve.wait_ge(at_step, at[0])
                did(v.reciprocal(st[:, 7, 0:QP], st[:, 6, 0:QP]))
                dve.wait_ge(at_step, at[0])
                s4 = s_all[:, n % 2, :].rearrange("p (k n) -> p k n", k=QP)
                v.tensor_tensor(s4, s4, st[:, 7, 0:QP].unsqueeze(2).to_broadcast([P, QP, KEYS]), ALU.mult).then_inc(pn_ready, 1)

            def out_low(n):
                g, j = divmod(n, NT)
                dve.wait_ge(oh_done, n + 1)
                cols = slice(META + j * P, META + (j + 1) * P)
                v.tensor_tensor(act_l[:, 2 * g:2 * g + 2, cols], ps[:, 1 + 2 * (j % 2), 0:2 * P].rearrange("p (t n) -> p t n", t=2),
                                act_h[:, 2 * g:2 * g + 2, cols].bitcast(F32), ALU.subtract).then_inc(ol_done, 1)

            query_var(0)
            query_norm(0)
            softmax(0)
            split_low(u0 + 4, 0)
            normed(0)
            softmax(1)
            for n in range(NB):
                g, j = divmod(n, NT)
                if n + 1 < NB:
                    normed(n + 1)
                if j == 0 and g + 1 < NKV:
                    query_var(g + 1)
                if n + 2 < NB:
                    softmax(n + 2)
                out_low(n)
                if g + 1 < NKV:
                    if j == 0:
                        current_keys(g + 1)
                    elif j == 1:
                        v.tensor_scalar(bias, bias, 2.0 ** (-8.0 * QP / NH), None, ALU.mult).then_inc(bias_ready, 1)
                        query_norm(g + 1)
                    elif j == 2 and g + 3 <= NKV:
                        split_low(u0 + 4 + (g + 1) % 2, (g + 1) // 2)
            project(*WO, REAL, 5)
            ffn(3, REAL)
            for d in range(0, KD, 2):
                dve.wait_ge(fin_full, d + 1)
                wait(dve, fin_evac, d)
                v.tensor_copy(arena[:, d * 512:(d + 1) * 512], ps[:, 4 + d % 4, :]).then_inc(fin_evac, 1)


_INS = ['x', 'meta_tokens', 'norm_ff1', 'ff1_w_gate', 'ff1_w_up', 'ff1_w_down', 'norm_mix', 'even_w_in', 'conv_w',
        'ssm_lambda_re', 'ssm_lambda_im', 'ssm_log_step', 'ssm_b_re', 'ssm_b_im', 'ssm_c_re', 'ssm_c_im', 'ssm_d',
        'glu_w', 'glu_b', 'even_w_out', 'attn_w_qkv', 'attn_q_norm', 'attn_k_norm', 'attn_sinks', 'attn_w_o',
        'norm_ff2', 'ff2_w_gate', 'ff2_w_up', 'ff2_w_down']


def kernel(**inputs):
    import numpy as _np
    import concourse.bacc as _bacc
    from concourse import mybir as _mybir
    from concourse.bass_utils import run_bass_kernel_spmd as _run

    nc = _bacc.Bacc("TRN2", target_bir_lowering=False, num_devices=1)
    arrays, args = {}, {}
    for name in _INS:
        arr = _np.ascontiguousarray(inputs[name])
        arrays[f"in_{name}"] = arr
        args[name] = nc.dram_tensor(f"in_{name}", arr.shape, _mybir.dt.from_np(arr.dtype), kind="ExternalInput").ap()
    out = nc.dram_tensor("out", arrays["in_x"].shape, _mybir.dt.float32, kind="ExternalOutput").ap()
    trunk_program(nc, args, out)
    res = _run(nc, [arrays], core_ids=[0])
    return res.results[0]["out"]
```
